# Optimizing a Trainium2 kernel written in Bass

```python
import jax, jax.numpy as jnp
from jax import lax
import numpy as np

D_MODEL = 1024
BATCH = 1
SEQ = 256
DEPTH = 2

HEAD_DIM = 64
N_HEADS = D_MODEL // HEAD_DIM
D_MIX = N_HEADS * HEAD_DIM
H_A = N_HEADS // 2
H_B = N_HEADS - H_A
H_C = N_HEADS // 2
H_D = N_HEADS - H_C
D_FF = 256 * ((8 * D_MODEL + 3 * 256 - 1) // (3 * 256))
FFN_RES_WEIGHT = 0.5
Q_BLOCK = 128
MOBA_BLOCK = 256
MOBA_TOPK = 3
MOBA_Q_BLOCK = 64
DILATED_BRANCHES = ((128, 1), (512, 4), (2048, 16))
ROPE_THETA = 10000.0
RMS_EPS = 1e-6
N_EVEN = (DEPTH + 1) // 2
N_ODD = DEPTH // 2


def rms_norm(x, g):
    xf = x.astype(jnp.float32)
    y = xf * lax.rsqrt(jnp.mean(xf * xf, axis=-1, keepdims=True) + RMS_EPS)
    return (y * g.astype(jnp.float32)).astype(x.dtype)

def swiglu(x, w_gate, w_up, w_down):
    return (jax.nn.silu(x @ w_gate) * (x @ w_up)) @ w_down

def rope_tables(seq):
    inv = 1.0 / (ROPE_THETA ** (jnp.arange(0, HEAD_DIM, 2, dtype=jnp.float32) / HEAD_DIM))
    ang = jnp.arange(seq, dtype=jnp.float32)[:, None] * inv[None, :]
    return jnp.cos(ang), jnp.sin(ang)

def apply_rope(x, cos, sin):
    x1, x2 = jnp.split(x, 2, axis=-1)
    c = cos.astype(x.dtype)
    s = sin.astype(x.dtype)
    return jnp.concatenate([x1 * c - x2 * s, x2 * c + x1 * s], axis=-1)

def split_heads(t, n_heads):
    b, s, _ = t.shape
    return t.reshape(b, s, n_heads, HEAD_DIM).transpose(0, 2, 1, 3)

def merge_heads(t):
    b, h, s, d = t.shape
    return t.transpose(0, 2, 1, 3).reshape(b, s, h * d)

def to_query_blocks(t, blk):
    b, h, s = t.shape[:3]
    t = t.reshape(b, h, s // blk, blk, *t.shape[3:])
    return jnp.moveaxis(t, 2, 0)

def from_query_blocks(t):
    n, b, h, blk, d = t.shape
    return jnp.moveaxis(t, 0, 2).reshape(b, h, n * blk, d)

def stick_breaking_attention(q, k, v):
    b, h, s, dh = q.shape
    scale = dh ** -0.5
    kpos = jnp.arange(s)

    def one_block(args):
        q_blk, i = args
        qpos = i * Q_BLOCK + jnp.arange(Q_BLOCK)
        strict = kpos[None, :] < qpos[:, None]
        z = jnp.einsum('bhqd,bhkd->bhqk', q_blk, k).astype(jnp.float32) * scale
        log_keep = jnp.where(strict, jax.nn.log_sigmoid(-z), 0.0)
        suffix = lax.cumsum(log_keep, axis=3, reverse=True)
        between = jnp.concatenate([suffix[..., 1:], jnp.zeros_like(suffix[..., :1])], axis=-1)
        weight = jnp.where(strict, jnp.exp(jax.nn.log_sigmoid(z) + between), 0.0)
        return jnp.einsum('bhqk,bhkd->bhqd', weight.astype(v.dtype), v)

    out = lax.map(one_block, (to_query_blocks(q, Q_BLOCK), jnp.arange(s // Q_BLOCK)))
    return from_query_blocks(out)

def moba_attention(q, k, v):
    b, h, s, dh = q.shape
    scale = dh ** -0.5
    n_kb = -(-s // MOBA_BLOCK)
    pad = n_kb * MOBA_BLOCK - s
    k_pad = jnp.pad(k, ((0, 0), (0, 0), (0, pad), (0, 0)))
    v_pad = jnp.pad(v, ((0, 0), (0, 0), (0, pad), (0, 0)))
    k_blocks = k_pad.reshape(b, h, n_kb, MOBA_BLOCK, dh)
    v_blocks = v_pad.reshape(b, h, n_kb, MOBA_BLOCK, dh)
    k_mean = jnp.mean(k_blocks.astype(jnp.float32), axis=3)
    top_k = min(MOBA_TOPK, n_kb)
    bi = jnp.arange(b)[:, None, None, None]
    hi = jnp.arange(h)[None, :, None, None]
    blk_ids = jnp.arange(n_kb)
    local = jnp.arange(MOBA_BLOCK)
    n_sel = top_k * MOBA_BLOCK

    def one_block(args):
        q_blk, i = args
        q0 = i * MOBA_Q_BLOCK
        qpos = q0 + jnp.arange(MOBA_Q_BLOCK)
        own = q0 // MOBA_BLOCK
        gate = jnp.einsum('bhqd,bhnd->bhqn', q_blk.astype(jnp.float32), k_mean)
        gate = jnp.where(blk_ids < own, gate, -jnp.inf)
        _, sel = lax.top_k(gate, top_k)
        sel_ok = jnp.arange(top_k) < own
        k_sel = k_blocks[bi, hi, sel]
        v_sel = v_blocks[bi, hi, sel]
        s_sel = jnp.einsum('bhqd,bhqnkd->bhqnk', q_blk, k_sel).astype(jnp.float32) * scale
        s_sel = jnp.where(sel_ok[:, None], s_sel, -jnp.inf).reshape(b, h, MOBA_Q_BLOCK, n_sel)
        k_own = lax.dynamic_slice_in_dim(k_pad, own * MOBA_BLOCK, MOBA_BLOCK, axis=2)
        v_own = lax.dynamic_slice_in_dim(v_pad, own * MOBA_BLOCK, MOBA_BLOCK, axis=2)
        s_own = jnp.einsum('bhqd,bhkd->bhqk', q_blk, k_own).astype(jnp.float32) * scale
        s_own = jnp.where(own * MOBA_BLOCK + local[None, :] <= qpos[:, None], s_own, -jnp.inf)
        p = jax.nn.softmax(jnp.concatenate([s_sel, s_own], axis=-1), axis=-1).astype(v.dtype)
        p_sel = p[..., :n_sel].reshape(b, h, MOBA_Q_BLOCK, top_k, MOBA_BLOCK)
        p_own = p[..., n_sel:]
        return (jnp.einsum('bhqnk,bhqnkd->bhqd', p_sel, v_sel)
                + jnp.einsum('bhqk,bhkd->bhqd', p_own, v_own))

    out = lax.map(one_block, (to_query_blocks(q, MOBA_Q_BLOCK), jnp.arange(s // MOBA_Q_BLOCK)))
    return from_query_blocks(out)

def forgetting_attention(q, k, v, log_f):
    b, h, s, dh = q.shape
    scale = dh ** -0.5
    c = jnp.cumsum(log_f, axis=-1)
    kpos = jnp.arange(s)

    def one_block(args):
        q_blk, c_blk, i = args
        qpos = i * Q_BLOCK + jnp.arange(Q_BLOCK)
        logits = (jnp.einsum('bhqd,bhkd->bhqk', q_blk, k).astype(jnp.float32) * scale
                  + c_blk[..., :, None] - c[..., None, :])
        logits = jnp.where(kpos[None, :] <= qpos[:, None], logits, -jnp.inf)
        p = jax.nn.softmax(logits, axis=-1).astype(v.dtype)
        return jnp.einsum('bhqk,bhkd->bhqd', p, v)

    out = lax.map(one_block, (to_query_blocks(q, Q_BLOCK), to_query_blocks(c, Q_BLOCK),
                              jnp.arange(s // Q_BLOCK)))
    return from_query_blocks(out)

def dilated_window_attention(q, k, v):
    b, h, s, dh = q.shape
    scale = dh ** -0.5

    def one_block(args):
        q_blk, i = args
        qpos = i * Q_BLOCK + jnp.arange(Q_BLOCK)
        maxes, denoms, outs = [], [], []
        for window, dil in DILATED_BRANCHES:
            steps = jnp.arange(window // dil + 1)
            kpos = qpos[:, None] - dil * steps[None, :]
            idx = jnp.maximum(kpos, 0)
            k_g = jnp.take(k, idx, axis=2)
            v_g = jnp.take(v, idx, axis=2)
            logits = jnp.einsum('bhqd,bhqnd->bhqn', q_blk, k_g).astype(jnp.float32) * scale
            logits = jnp.where(kpos >= 0, logits, -jnp.inf)
            m = jnp.max(logits, axis=-1, keepdims=True)
            e = jnp.exp(logits - m)
            l = jnp.sum(e, axis=-1, keepdims=True)
            outs.append(jnp.einsum('bhqn,bhqnd->bhqd', e, v_g.astype(jnp.float32)) / l)
            maxes.append(m)
            denoms.append(l)
        m_all = jnp.stack(maxes)
        s_all = jnp.stack(denoms) * jnp.exp(m_all - jnp.max(m_all, axis=0, keepdims=True))
        alpha = s_all / jnp.sum(s_all, axis=0, keepdims=True)
        return jnp.sum(alpha * jnp.stack(outs), axis=0).astype(v.dtype)

    out = lax.map(one_block, (to_query_blocks(q, Q_BLOCK), jnp.arange(s // Q_BLOCK)))
    return from_query_blocks(out)

def mix_stick_moba(xn, w_in, g_q_b, g_k_b, cos, sin):
    q, k, v = jnp.split(xn @ w_in, 3, axis=-1)
    q, k, v = split_heads(q, N_HEADS), split_heads(k, N_HEADS), split_heads(v, N_HEADS)
    out_a = stick_breaking_attention(q[:, :H_A], k[:, :H_A], v[:, :H_A])
    q_b = apply_rope(rms_norm(q[:, H_A:], g_q_b), cos, sin)
    k_b = apply_rope(rms_norm(k[:, H_A:], g_k_b), cos, sin)
    out_b = moba_attention(q_b, k_b, v[:, H_A:])
    return merge_heads(jnp.concatenate([out_a.astype(xn.dtype), out_b.astype(xn.dtype)], axis=1))

def mix_forget_dilated(xn, w_in, b_f, g_q_c, g_k_c, g_q_d, g_k_d, cos, sin):
    proj = xn @ w_in
    q, k, v = jnp.split(proj[..., :3 * D_MIX], 3, axis=-1)
    q, k, v = split_heads(q, N_HEADS), split_heads(k, N_HEADS), split_heads(v, N_HEADS)
    log_f = jax.nn.log_sigmoid((proj[..., 3 * D_MIX:] + b_f).astype(jnp.float32)).transpose(0, 2, 1)
    q_c = rms_norm(q[:, :H_C], g_q_c)
    k_c = rms_norm(k[:, :H_C], g_k_c)
    out_c = forgetting_attention(q_c, k_c, v[:, :H_C], log_f)
    q_d = apply_rope(rms_norm(q[:, H_C:], g_q_d), cos, sin)
    k_d = apply_rope(rms_norm(k[:, H_C:], g_k_d), cos, sin)
    out_d = dilated_window_attention(q_d, k_d, v[:, H_C:])
    return merge_heads(jnp.concatenate([out_c.astype(xn.dtype), out_d.astype(xn.dtype)], axis=1))

def first_inputs(seed: int = 0) -> dict:
    key = jax.random.key(seed)
    ks = jax.random.split(key, 20)

    def normal(k, shape, scale):
        return jax.random.normal(k, shape, jnp.float32) * scale

    def gain(k, shape):
        return 1.0 + 0.02 * jax.random.normal(k, shape, jnp.float32)

    return {
        'x': normal(ks[0], (BATCH, SEQ, D_MODEL), 1.0),
        'norm_ffn1': gain(ks[1], (DEPTH, D_MODEL)),
        'ffn1_w_gate': normal(ks[2], (DEPTH, D_MODEL, D_FF), D_MODEL ** -0.5),
        'ffn1_w_up': normal(ks[3], (DEPTH, D_MODEL, D_FF), D_MODEL ** -0.5),
        'ffn1_w_down': normal(ks[4], (DEPTH, D_FF, D_MODEL), D_FF ** -0.5),
        'norm_mix': gain(ks[5], (DEPTH, D_MODEL)),
        'w_in_ab': normal(ks[6], (N_EVEN, D_MODEL, 3 * D_MIX), D_MODEL ** -0.5),
        'g_q_b': gain(ks[7], (N_EVEN, HEAD_DIM)),
        'g_k_b': gain(ks[8], (N_EVEN, HEAD_DIM)),
        'w_in_cd': normal(ks[9], (N_ODD, D_MODEL, 3 * D_MIX + H_C), D_MODEL ** -0.5),
        'b_f': normal(ks[10], (N_ODD, H_C), 0.1),
        'g_q_c': gain(ks[11], (N_ODD, HEAD_DIM)),
        'g_k_c': gain(ks[12], (N_ODD, HEAD_DIM)),
        'g_q_d': gain(ks[13], (N_ODD, HEAD_DIM)),
        'g_k_d': gain(ks[14], (N_ODD, HEAD_DIM)),
        'w_out': normal(ks[15], (DEPTH, D_MIX, D_MODEL), D_MIX ** -0.5),
        'norm_ffn2': gain(ks[16], (DEPTH, D_MODEL)),
        'ffn2_w_gate': normal(ks[17], (DEPTH, D_MODEL, D_FF), D_MODEL ** -0.5),
        'ffn2_w_up': normal(ks[18], (DEPTH, D_MODEL, D_FF), D_MODEL ** -0.5),
        'ffn2_w_down': normal(ks[19], (DEPTH, D_FF, D_MODEL), D_FF ** -0.5),
    }

def first_block(x, norm_ffn1, ffn1_w_gate, ffn1_w_up, ffn1_w_down, norm_mix, w_in_ab, g_q_b, g_k_b,
              w_in_cd, b_f, g_q_c, g_k_c, g_q_d, g_k_d, w_out, norm_ffn2, ffn2_w_gate, ffn2_w_up,
              ffn2_w_down):
    cos, sin = rope_tables(x.shape[1])
    for layer in range(DEPTH):
        j = layer // 2
        x = x + FFN_RES_WEIGHT * swiglu(rms_norm(x, norm_ffn1[layer]), ffn1_w_gate[layer],
                                        ffn1_w_up[layer], ffn1_w_down[layer])
        xn = rms_norm(x, norm_mix[layer])
        if layer % 2 == 0:
            mixed = mix_stick_moba(xn, w_in_ab[j], g_q_b[j], g_k_b[j], cos, sin)
        else:
            mixed = mix_forget_dilated(xn, w_in_cd[j], b_f[j], g_q_c[j], g_k_c[j],
                                       g_q_d[j], g_k_d[j], cos, sin)
        x = x + mixed @ w_out[layer]
        x = x + FFN_RES_WEIGHT * swiglu(rms_norm(x, norm_ffn2[layer]), ffn2_w_gate[layer],
                                        ffn2_w_up[layer], ffn2_w_down[layer])
    return x


DEPTH_2 = 1

NORM_EPS = 1e-6
PLE_DIM = 256
RW_HEADS = 8
RW_HEAD_DIM = 64
RW_WIDTH = RW_HEADS * RW_HEAD_DIM
RW_DECAY_LORA = 64
RW_ICLR_LORA = 64
RW_GATE_LORA = 128
RW_GN_EPS = 64e-5
RW_COLS = 3 * RW_WIDTH + 2 * RW_DECAY_LORA + 2 * RW_ICLR_LORA + RW_GATE_LORA
MLA_HEADS = 8
MLA_NOPE_DIM = 64
MLA_ROPE_DIM = 32
MLA_V_DIM = 64
MLA_QK_DIM = MLA_NOPE_DIM + MLA_ROPE_DIM
MLA_Q_RANK = 256
MLA_KV_RANK = 128
MLA_COLS = MLA_Q_RANK + MLA_KV_RANK + MLA_ROPE_DIM
MLA_WIDTH = MLA_HEADS * MLA_V_DIM
N_BRANCHES = 2
GATE_COLS = N_BRANCHES * D_MODEL
IN_COLS = RW_COLS + MLA_COLS + GATE_COLS
PEER_HEADS = 8
PEER_N_KEYS = 128
PEER_N_EXPERTS = PEER_N_KEYS * PEER_N_KEYS
PEER_TOPK = 16
PEER_QUERY_DIM = 256
PEER_HALF = PEER_QUERY_DIM // 2
TOKEN_BLOCK = 128


def rmsnorm(x, g):
    xf = x.astype(jnp.float32)
    y = xf * lax.rsqrt(jnp.mean(xf * xf, axis=-1, keepdims=True) + NORM_EPS)
    return (y * g).astype(x.dtype)

def centred_shift(u):
    prev = jnp.pad(u[:, :-1], ((0, 0), (1, 0), (0, 0)))
    nxt = jnp.pad(u[:, 1:], ((0, 0), (0, 1), (0, 0)))
    return 0.5 * (prev + nxt) - u

def _heads(t, n_heads, head_dim):
    return t.reshape(t.shape[:-1] + (n_heads, head_dim))

def rope_tables_2(positions):
    inv = ROPE_THETA ** (-jnp.arange(0, MLA_ROPE_DIM, 2, dtype=jnp.float32) / MLA_ROPE_DIM)
    ang = positions.astype(jnp.float32)[..., None] * inv
    return jnp.cos(ang), jnp.sin(ang)

def apply_rope_2(x, cos, sin):
    xf = x.astype(jnp.float32)
    half = xf.shape[-1] // 2
    x1, x2 = xf[..., :half], xf[..., half:]
    return jnp.concatenate([x1 * cos - x2 * sin, x2 * cos + x1 * sin], axis=-1).astype(x.dtype)

def rwkv7_scan(r, a_vec, b_vec, v, k, decay):
    def step(state, inp):
        r_t, a_t, b_t, v_t, k_t, w_t = inp
        sa = jnp.einsum('bdhvk,bdhk->bdhv', state, a_t)
        state = (state * w_t[..., None, :] + sa[..., :, None] * b_t[..., None, :]
                 + v_t[..., :, None] * k_t[..., None, :])
        return state, jnp.einsum('bdhvk,bdhk->bdhv', state, r_t)
    B = r.shape[1]
    init = jnp.zeros((B, 2, RW_HEADS, RW_HEAD_DIM, RW_HEAD_DIM), jnp.float32)
    _, out = lax.scan(step, init, (r, a_vec, b_vec, v, k, decay))
    return out

def rwkv7_time_mix(u, mu, w0, w2, a0, a2, g2, k_k, k_a, r_k, gn_w, gn_b):
    f32 = jnp.float32
    B, T, _ = u.shape
    H, N, W = RW_HEADS, RW_HEAD_DIM, RW_WIDTH
    u = u + mu * centred_shift(u)
    o0 = 3 * W
    o1 = o0 + 2 * RW_DECAY_LORA
    o2 = o1 + 2 * RW_ICLR_LORA
    r, k, v = u[..., :W], u[..., W:2 * W], u[..., 2 * W:o0]
    lw = u[..., o0:o1].reshape(B, T, 2, RW_DECAY_LORA)
    la = u[..., o1:o2].reshape(B, T, 2, RW_ICLR_LORA)
    lg = u[..., o2:]
    w_log = -jax.nn.softplus(-(w0 + jnp.einsum('btdl,dlc->btdc', jnp.tanh(lw), w2)).astype(f32)) - 0.5
    decay = jnp.exp(-jnp.exp(w_log))
    a = jax.nn.sigmoid((a0 + jnp.einsum('btdl,dlc->btdc', la, a2)).astype(f32))
    g = jax.nn.sigmoid(lg) @ g2
    kk = _heads((k * k_k).astype(f32), H, N)
    kk = kk / jnp.maximum(jnp.sqrt(jnp.sum(kk * kk, axis=-1, keepdims=True)), 1e-12)
    k_dir = k.astype(f32)[:, :, None, :] * (1.0 + (a - 1.0) * k_a.astype(f32))
    r_h = _heads(r.astype(f32), H, N)
    v_h = _heads(v.astype(f32), H, N)
    k_h = _heads(k_dir, H, N)
    a_h = _heads(a, H, N)
    both = lambda t: jnp.stack([t, t], axis=2)

    def time_major(t):
        t = jnp.concatenate([t[:, :, :1], jnp.flip(t[:, :, 1:], axis=1)], axis=2)
        return jnp.moveaxis(t, 1, 0)

    out = rwkv7_scan(time_major(both(r_h)), time_major(both(-kk)),
                     time_major(kk[:, :, None] * a_h), time_major(both(v_h)),
                     time_major(k_h), time_major(_heads(decay, H, N)))
    out = jnp.moveaxis(out, 0, 1)
    o = out[:, :, 0] + jnp.flip(out[:, :, 1], axis=1)
    m = jnp.mean(o, axis=-1, keepdims=True)
    var = jnp.mean(jnp.square(o - m), axis=-1, keepdims=True)
    o = ((o - m) * lax.rsqrt(var + RW_GN_EPS)).reshape(B, T, W) * gn_w + gn_b
    bonus = jnp.sum(jnp.sum(r_h[:, :, None] * k_h * _heads(r_k, H, N), axis=-1, keepdims=True), axis=2) * v_h
    o = o + bonus.reshape(B, T, W)
    return (o * g).astype(u.dtype)

def bidir_attention(q, k, v):
    B, T, H, Dq = q.shape
    scale = Dq ** -0.5
    qb = jnp.moveaxis(q.reshape(B, T // Q_BLOCK, Q_BLOCK, H, Dq), 1, 0)

    def block(qi):
        s = jnp.einsum('bqhd,bkhd->bhqk', qi, k).astype(jnp.float32) * scale
        p = jax.nn.softmax(s, axis=-1)
        return jnp.einsum('bhqk,bkhd->bqhd', p.astype(v.dtype), v)

    o = lax.map(block, qb)
    return jnp.moveaxis(o, 0, 1).reshape(B, T, H, v.shape[-1])

def mla_mix(u, positions, g_qa, w_qup, g_kva, w_kvup):
    B, T, _ = u.shape
    H = MLA_HEADS
    cq = u[..., :MLA_Q_RANK]
    ckv = u[..., MLA_Q_RANK:MLA_Q_RANK + MLA_KV_RANK]
    kr = u[..., MLA_Q_RANK + MLA_KV_RANK:]
    q = (rmsnorm(cq, g_qa) @ w_qup).reshape(B, T, H, MLA_QK_DIM)
    kv = (rmsnorm(ckv, g_kva) @ w_kvup).reshape(B, T, H, MLA_NOPE_DIM + MLA_V_DIM)
    cos, sin = rope_tables_2(positions)
    q_rope = apply_rope_2(q[..., MLA_NOPE_DIM:], cos[:, :, None], sin[:, :, None])
    k_rope = apply_rope_2(kr, cos, sin)
    qh = jnp.concatenate([q[..., :MLA_NOPE_DIM], q_rope], axis=-1)
    kh = jnp.concatenate([kv[..., :MLA_NOPE_DIM],
                          jnp.broadcast_to(k_rope[:, :, None, :], (B, T, H, MLA_ROPE_DIM))], axis=-1)
    o = bidir_attention(qh, kh, kv[..., MLA_NOPE_DIM:])
    return o.reshape(B, T, MLA_WIDTH)

def peer_ffn(h, w_q, sub_keys, expert_u, expert_v):
    B, T, D = h.shape
    hb_all = h.reshape(-1, TOKEN_BLOCK, D)

    def block(hb):
        n = hb.shape[0]
        q = (hb @ w_q).reshape(n, PEER_HEADS, 2, PEER_HALF)
        s = jnp.einsum('nhcd,hckd->nhck', q, sub_keys).astype(jnp.float32)
        sc, ix = lax.top_k(s, PEER_TOPK)
        cand = sc[:, :, 0, :, None] + sc[:, :, 1, None, :]
        cidx = ix[:, :, 0, :, None] * PEER_N_KEYS + ix[:, :, 1, None, :]
        top, pos = lax.top_k(cand.reshape(n, PEER_HEADS, PEER_TOPK * PEER_TOPK), PEER_TOPK)
        eidx = jnp.take_along_axis(cidx.reshape(n, PEER_HEADS, -1), pos, axis=-1)
        gate = jax.nn.softmax(top, axis=-1)
        act = jax.nn.gelu(jnp.einsum('nhed,nd->nhe', expert_u[eidx], hb), approximate=False)
        return jnp.einsum('nhe,nhed->nd', (gate * act).astype(hb.dtype), expert_v[eidx])

    return lax.map(block, hb_all).reshape(B, T, D)

def second_inputs(seed: int = 0) -> dict:
    key = jax.random.key(seed)
    ks = jax.random.split(key, 32)
    nrm = lambda k, shape, s: jax.random.normal(k, shape, jnp.float32) * s
    gain = lambda k, shape: 1.0 + 0.05 * jax.random.normal(k, shape, jnp.float32)
    L, D, W = DEPTH_2, D_MODEL, RW_WIDTH
    return {
        'x': nrm(ks[0], (BATCH, SEQ, D), 1.0),
        'p': nrm(ks[1], (DEPTH_2, BATCH, SEQ, PLE_DIM), 1.0),
        'positions': jnp.broadcast_to(jnp.arange(SEQ, dtype=jnp.int32)[None, :], (BATCH, SEQ)),
        'g_mix': gain(ks[2], (L, D)),
        'w_in': nrm(ks[3], (L, D, IN_COLS), D ** -0.5),
        'rw_mu': jax.random.uniform(ks[4], (L, RW_COLS), jnp.float32),
        'rw_w0': jax.random.uniform(ks[5], (L, 2, W), jnp.float32, -6.0, -1.0),
        'rw_w2': nrm(ks[6], (L, 2, RW_DECAY_LORA, W), 0.1 * RW_DECAY_LORA ** -0.5),
        'rw_a0': nrm(ks[7], (L, 2, W), 0.1),
        'rw_a2': nrm(ks[8], (L, 2, RW_ICLR_LORA, W), 0.5 * RW_ICLR_LORA ** -0.5),
        'rw_g2': nrm(ks[9], (L, RW_GATE_LORA, W), RW_GATE_LORA ** -0.5),
        'rw_k_k': 0.85 + nrm(ks[10], (L, W), 0.05),
        'rw_k_a': gain(ks[11], (L, W)),
        'rw_r_k': nrm(ks[12], (L, W), 0.1),
        'rw_gn_w': gain(ks[13], (L, W)),
        'rw_gn_b': nrm(ks[14], (L, W), 0.01),
        'mla_g_qa': gain(ks[15], (L, MLA_Q_RANK)),
        'mla_w_qup': nrm(ks[16], (L, MLA_Q_RANK, MLA_HEADS * MLA_QK_DIM), MLA_Q_RANK ** -0.5),
        'mla_g_kva': gain(ks[17], (L, MLA_KV_RANK)),
        'mla_w_kvup': nrm(ks[18], (L, MLA_KV_RANK, MLA_HEADS * (MLA_NOPE_DIM + MLA_V_DIM)), MLA_KV_RANK ** -0.5),
        'w_br_rwkv': nrm(ks[19], (L, W, D), W ** -0.5),
        'w_br_mla': nrm(ks[20], (L, MLA_WIDTH, D), MLA_WIDTH ** -0.5),
        'w_out': nrm(ks[21], (L, D, D), D ** -0.5),
        'g_ffn': gain(ks[22], (L, D)),
        'peer_w_q': nrm(ks[23], (L, D, PEER_HEADS * PEER_QUERY_DIM), D ** -0.5),
        'peer_sub_keys': nrm(ks[24], (L, PEER_HEADS, 2, PEER_N_KEYS, PEER_HALF), PEER_HALF ** -0.5),
        'peer_u': nrm(ks[25], (L, PEER_N_EXPERTS, D), D ** -0.5),
        'peer_v': nrm(ks[26], (L, PEER_N_EXPERTS, D), PEER_HEADS ** -0.5),
        'g_ple': gain(ks[27], (L, D)),
        'w_ple_gate': nrm(ks[28], (L, D, D), D ** -0.5),
        'w_ple_proj': nrm(ks[29], (L, PLE_DIM, D), PLE_DIM ** -0.5),
        'g_final': gain(ks[30], (D,)),
    }

def second_block(x, p, positions, g_mix, w_in, rw_mu, rw_w0, rw_w2, rw_a0, rw_a2, rw_g2,
              rw_k_k, rw_k_a, rw_r_k, rw_gn_w, rw_gn_b, mla_g_qa, mla_w_qup, mla_g_kva,
              mla_w_kvup, w_br_rwkv, w_br_mla, w_out, g_ffn, peer_w_q, peer_sub_keys,
              peer_u, peer_v, g_ple, w_ple_gate, w_ple_proj, g_final):
    B, T, D = x.shape
    for i in range(DEPTH_2):
        h = rmsnorm(x, g_mix[i])
        u = h @ w_in[i]
        u_rw = u[..., :RW_COLS]
        u_mla = u[..., RW_COLS:RW_COLS + MLA_COLS]
        gates = jax.nn.sigmoid(u[..., RW_COLS + MLA_COLS:]).reshape(B, T, N_BRANCHES, D)
        y_rw = rwkv7_time_mix(u_rw, rw_mu[i], rw_w0[i], rw_w2[i], rw_a0[i], rw_a2[i], rw_g2[i],
                              rw_k_k[i], rw_k_a[i], rw_r_k[i], rw_gn_w[i], rw_gn_b[i])
        y_mla = mla_mix(u_mla, positions, mla_g_qa[i], mla_w_qup[i], mla_g_kva[i], mla_w_kvup[i])
        merged = gates[:, :, 0] * (y_rw @ w_br_rwkv[i]) + gates[:, :, 1] * (y_mla @ w_br_mla[i])
        x = x + merged @ w_out[i]
        x = x + peer_ffn(rmsnorm(x, g_ffn[i]), peer_w_q[i], peer_sub_keys[i], peer_u[i], peer_v[i])
        x = x + (p[i] @ w_ple_proj[i]) * jax.nn.sigmoid(rmsnorm(x, g_ple[i]) @ w_ple_gate[i])
    return rmsnorm(x, g_final)


def setup_inputs(seed=0):
    out = dict(first_inputs(seed))
    for name, value in second_inputs(seed + 1).items():
        if name != "x":
            out[name + "_2"] = value
    return out


def reference(
    x, norm_ffn1, ffn1_w_gate, ffn1_w_up, ffn1_w_down, norm_mix, w_in_ab, g_q_b, g_k_b, w_in_cd,
    b_f, g_q_c, g_k_c, g_q_d, g_k_d, w_out, norm_ffn2, ffn2_w_gate, ffn2_w_up, ffn2_w_down, p_2,
    positions_2, g_mix_2, w_in_2, rw_mu_2, rw_w0_2, rw_w2_2, rw_a0_2, rw_a2_2, rw_g2_2,
    rw_k_k_2, rw_k_a_2, rw_r_k_2, rw_gn_w_2, rw_gn_b_2, mla_g_qa_2, mla_w_qup_2, mla_g_kva_2,
    mla_w_kvup_2, w_br_rwkv_2, w_br_mla_2, w_out_2, g_ffn_2, peer_w_q_2, peer_sub_keys_2,
    peer_u_2, peer_v_2, g_ple_2, w_ple_gate_2, w_ple_proj_2, g_final_2,
):
    x = first_block(
        x, norm_ffn1, ffn1_w_gate, ffn1_w_up, ffn1_w_down, norm_mix, w_in_ab, g_q_b, g_k_b,
        w_in_cd, b_f, g_q_c, g_k_c, g_q_d, g_k_d, w_out, norm_ffn2, ffn2_w_gate, ffn2_w_up,
        ffn2_w_down,
    )
    return second_block(
        x, p_2, positions_2, g_mix_2, w_in_2, rw_mu_2, rw_w0_2, rw_w2_2, rw_a0_2, rw_a2_2,
        rw_g2_2, rw_k_k_2, rw_k_a_2, rw_r_k_2, rw_gn_w_2, rw_gn_b_2, mla_g_qa_2, mla_w_qup_2,
        mla_g_kva_2, mla_w_kvup_2, w_br_rwkv_2, w_br_mla_2, w_out_2, g_ffn_2, peer_w_q_2,
        peer_sub_keys_2, peer_u_2, peer_v_2, g_ple_2, w_ple_gate_2, w_ple_proj_2, g_final_2,
    )


_drawn_inputs = setup_inputs


def setup_inputs(seed=0):
    import zlib

    import numpy as np

    out = dict(_drawn_inputs(seed))
    spreads = {}
    factors = {'norm_ffn1': 2.891,
     'g_q_b': 7.936,
     'g_k_b': 8.0,
     'b_f': 3.716,
     'g_q_c': 6.557,
     'g_k_c': 6.888,
     'g_q_d': 8.0,
     'g_k_d': 8.0,
     'norm_ffn2': 3.442,
     'rw_w2_2': 64.0,
     'rw_a0_2': 3.967,
     'rw_k_k_2': 28.072,
     'rw_k_a_2': 8.646,
     'rw_gn_w_2': 26.584,
     'rw_gn_b_2': 64.0,
     'mla_g_qa_2': 8.0,
     'mla_g_kva_2': 5.497,
     'g_ple_2': 63.96,
     'rw_r_k_2': 5.367,
     'g_ffn_2': 8.0,
     'peer_u_2': 2.873}
    for name, (base, spread) in spreads.items():
        noise = np.random.default_rng([zlib.crc32(name.encode()), seed]).standard_normal(out[name].shape)
        drawn = base * np.exp(spread * noise) if base else spread * noise
        out[name] = __import__('jax').numpy.asarray(drawn.astype(out[name].dtype))
    for name, factor in factors.items():
        out[name] = (out[name] * factor).astype(out[name].dtype)
    return out
```

```python
from contextlib import ExitStack

import concourse.bass as bass
import numpy as np
from concourse import mybir

F32 = mybir.dt.float32
U32 = mybir.dt.uint32
I32 = mybir.dt.int32
ACT = mybir.ActivationFunctionType
ALU = mybir.AluOpType
AX = mybir.AxisListType

P = 128
T = 256
D = 1024
KC = D // P
HD = 64
DFF = 2816
GROUPS = DFF // 256
CHUNKS = DFF // P
EPS = 1e-6
RW_COLS, MLA_COLS = 1920, 416
N_KEYS, TOPK, PH = 128, 16, 8
NEG = -1.0e30
DECAY = float(np.exp(-0.5))
GN_EPS = 64e-5

VEC = {}
_n = 0
for _name, _w in (
    ("norm_ffn1", 16), ("norm_mix", 16), ("norm_ffn2", 16), ("g_mix_2", 8), ("g_ffn_2", 8), ("g_ple_2", 8),
    ("g_final_2", 8), ("rw_mu_2", 15), ("rw_w0_2", 8), ("rw_a0_2", 8), ("rw_k_k_2", 4), ("rw_k_a_2", 4),
    ("rw_r_k_2", 4), ("rw_gn_w_2", 4), ("rw_gn_b_2", 4), ("mla_g_qa_2", 2), ("mla_g_kva_2", 1),
    ("g_q_b", 1), ("g_k_b", 1), ("g_q_c", 1), ("g_k_c", 1), ("g_q_d", 1), ("g_k_d", 1),
):
    VEC[_name] = _n
    _n += _w
NVEC = _n

CON = {}
_n = 0
for _name, _w in (
    ("ident", 128), ("ones", 128), ("heads", 128), ("suffix", 128), ("after", 128), ("causal", 384),
    ("dilated", 384), ("cos", 256), ("sin", 256), ("turn", 128), ("turn_mla", 32), ("seen", 512),
    ("level", 2 * 7 * 128), ("inv", 1), ("eps", 4), ("count", 16), ("one", 1),
):
    CON[_name] = _n
    _n += _w
NCON = _n


def constants():
    c = np.zeros((P, NCON), np.float32)

    def put(name, value):
        value = np.asarray(value, np.float32)
        c[: value.shape[0], CON[name] : CON[name] + value.shape[1]] = value

    i = np.arange(P)
    row, col = i[:, None], i[None, :]
    put("ident", row == col)
    put("ones", np.ones((P, P)))
    put("heads", (row // HD) == (col // HD))
    put("suffix", -8.0 * (row >= col))
    put("after", -8.0 * np.ones((P, P)))
    tri = np.where(col <= row, 0.0, NEG)
    put("causal", np.concatenate([tri, np.zeros((P, P)), tri], 1))

    def branches(dist):
        n = ((dist >= 0) & (dist <= 128)).astype(int) + ((dist >= 0) & (dist % 4 == 0)) + ((dist >= 0) & (dist % 16 == 0))
        return np.where(n > 0, 8.0 * np.log(np.maximum(n, 1)), NEG)

    put("dilated", np.concatenate([branches(row - col), branches(128 + row - col), branches(row - col)], 1))
    inv = (1.0 / (np.float32(10000.0) ** (np.arange(0, HD, 2, dtype=np.float32) / np.float32(HD)))).astype(np.float32)
    ang = (np.arange(T, dtype=np.float32)[:, None] * inv[None, :]).astype(np.float32).astype(np.float64)
    put("cos", np.tile(np.cos(ang).T, (4, 1)))
    put("sin", np.tile(np.sin(ang).T, (4, 1)))
    turn = np.zeros((P, P))
    for h in (0, HD):
        for j in range(32):
            turn[h + 32 + j, h + j] = -1.0
            turn[h + j, h + 32 + j] = 1.0
    put("turn", turn)
    turn = np.zeros((P, 32))
    for j in range(16):
        turn[64 + 16 + j, j] = -1.0
        turn[64 + j, 16 + j] = 1.0
    put("turn_mla", turn)
    put("seen", np.concatenate([row < col, row <= col, row > col, row >= col], 1))
    level = np.zeros((P, 2, 7, P))
    for l in range(7):
        n = 1 << l
        same = (row // (2 * n)) == (col // (2 * n))
        level[:, 0, l] = same & (row // n < col // n)
        level[:, 1, l] = same & (row // n > col // n)
    put("level", level.reshape(P, -1))
    inv2 = (np.float32(10000.0) ** (-np.arange(0, 32, 2, dtype=np.float32) / np.float32(32))).astype(np.float32)
    v = np.zeros((P, 1))
    v[64:96, 0] = np.tile(inv2, 2)
    put("inv", v)
    put("eps", np.tile(np.array([[EPS, GN_EPS, 1e-24, 0.0]]), (P, 1)))
    put("count", np.tile(np.arange(16)[None, :], (P, 1)))
    put("one", np.ones((P, 1)))
    return c


def pack_vectors(inputs):
    v = np.zeros((P, NVEC), np.float32)
    for name, at in VEC.items():
        a = np.asarray(inputs[name])
        if name.startswith("g_") and a.size == HD:
            v[:HD, at : at + 1] = a.reshape(HD, 1)
            v[HD:, at : at + 1] = a.reshape(HD, 1)
        else:
            w = a.size // P
            v[:, at : at + w] = a.reshape(w, P).T
    return v


def build(nc, A, out):
    ctx = ExitStack()
    with ctx:
        sb = lambda name, shape, dt=F32: ctx.enter_context(nc.sbuf_tensor(name + "_sb", shape, dt))
        sem = lambda name: ctx.enter_context(nc.semaphore(name))

        xT = sb("xT", [P, KC, T])
        xn = sb("xn", [P, KC, T])
        sq = sb("sq", [P, KC, T])
        RING = 6
        ring = sb("ring", [P, RING, 2048])
        con = sb("con", [P, NCON])
        vec = sb("vec", [P, NVEC])
        rstd = sb("rstd", [P, T])
        std = sb("std", [P, T])
        sgate = sb("sgate", [P, 2, T])
        hT = sb("hT", [P, 2, T])
        small = sb("small", [P, 256])
        ARENA = 28400
        arena = sb("arena", [P, ARENA])
        bank = [ctx.enter_context(nc.psum_tensor(f"bank{b}", [P, 512], F32)) for b in range(8)]

        def view(at, *shape, dt=None):
            n = int(np.prod(shape))
            assert at + n <= ARENA
            v = arena[:, at : at + n]
            if dt is not None:
                v = v.bitcast(dt)
            names = "abcde"[: len(shape)]
            if len(shape) == 1:
                return v
            return v.rearrange(f"p ({' '.join(names)}) -> p {' '.join(names)}", **{n_: s for n_, s in zip(names[1:], shape[1:])})

        C = lambda name, w, off=0: con[:, CON[name] + off : CON[name] + off + w]
        V = lambda name, c=0: vec[:, VEC[name] + c : VEC[name] + c + 1]
        ident = C("ident", P)
        eps = lambda j: C("eps", 1, j)

        loaded_x, loaded_c, loaded_v = sem("loaded_x"), sem("loaded_c"), sem("loaded_v")
        slot_loaded = [sem(f"slot{i}_loaded") for i in range(RING)]
        slot_free = sem("slot_free")
        sq_ready, ssq_ready, std_ready, xn_ready = sem("sq_ready"), sem("ssq_ready"), sem("std_ready"), sem("xn_ready")
        x_ready, y_ready = sem("x_ready"), sem("y_ready")
        gu_ready, silu_ready, h_ready = sem("gu_ready"), sem("silu_ready"), sem("h_ready")
        full = [sem(f"bank{b}_full") for b in range(8)]
        free = [sem(f"bank{b}_free") for b in range(8)]
        dve_done, act_done, pool_done = sem("dve_done"), sem("act_done"), sem("pool_done")
        named = {}

        def S(name):
            if name not in named:
                named[name] = sem(name)
            return named[name]

        SCALE = {0: 0.125, 1: 0.125, 2: 96.0 ** -0.5}

        fill_of, fills = {}, [0] * 8

        def plan(label, b):
            fills[b] += 1
            assert label not in fill_of, label
            fill_of[label] = (b, fills[b])

        def fill_begin(pe, label):
            b, n = fill_of[label]
            if n > 1:
                pe.wait_ge(free[b], n - 1)
            return bank[b]

        def fill_end(ins, label):
            ins.then_inc(full[fill_of[label][0]], 1)

        def take(eng, label):
            b, n = fill_of[label]
            eng.wait_ge(full[b], n)
            return bank[b]

        def give(ins, label):
            ins.then_inc(free[fill_of[label][0]], 1)

        def emptied(eng, label):
            b, n = fill_of[label]
            eng.wait_ge(free[b], n)

        class Chain:

            def __init__(self, s):
                self.s, self.n = s, 0

            def link(self, eng, ins):
                ins.then_inc(self.s, 1)
                self.n += 1
                eng.wait_ge(self.s, self.n)

        at = {}
        k = 0
        for l in range(2):
            at["ffn", 2 * l] = k; k += 3 * GROUPS
            at["qkv", l] = k; k += 12
            at["wo", l] = k; k += 4
            at["ffn", 2 * l + 1] = k; k += 3 * GROUPS
        at["in2"] = k; k += 18
        at["mla"] = k; k += 2
        at["br"] = k; k += 4
        at["wo", 2] = k; k += 4
        at["wq"] = k; k += 8
        at["keys"] = k; k += 1
        at["pg"] = k; k += 4
        at["pp"] = k; k += 1
        slot = lambda k, *shape: ring[:, k % RING, 0 : int(np.prod(shape))].rearrange("p (k n) -> p k n", k=shape[0])

        ffn_w = [
            (A["ffn1_w_gate"][0], A["ffn1_w_up"][0], A["ffn1_w_down"][0]),
            (A["ffn2_w_gate"][0], A["ffn2_w_up"][0], A["ffn2_w_down"][0]),
            (A["ffn1_w_gate"][1], A["ffn1_w_up"][1], A["ffn1_w_down"][1]),
            (A["ffn2_w_gate"][1], A["ffn2_w_up"][1], A["ffn2_w_down"][1]),
        ]
        norm_g = [("norm_ffn1", 0), ("norm_mix", 0), ("norm_ffn2", 0), ("norm_ffn1", 8), ("norm_mix", 8),
                  ("norm_ffn2", 8), ("g_mix_2", 0), ("g_ffn_2", 0), ("g_ple_2", 0), ("g_final_2", 0)]
        rows = lambda w: w.rearrange("(k p) n -> p k n", p=P)

        QK = view(0, 16, T)
        VT = view(4096, 2, D)
        MIX = view(6144, KC, T)
        SM = [view(8192 + 512 * j, 512) for j in range(2)]
        PR = [view(9216 + 512 * j, 512) for j in range(2)]
        PT = [view(10240 + 512 * j, 512) for j in range(2)]
        ZR = [view(11264 + 512 * j, 512) for j in range(2)]
        ZL = [view(12288 + 512 * j, 512) for j in range(2)]
        HSQ = [view(13312 + 512 * j, 512) for j in range(2)]
        HSTD = [view(14336 + 512 * j, 512) for j in range(2)]
        ROT = view(15360, 512)
        WF = view(16384, KC, 8)
        FG = view(16448, 4, T)
        FL = view(17472, 8, T)
        FR = view(19520, 8, T)
        MX = small[:, 0:4]
        NM = small[:, 4:8]
        RS = small[:, 8:12]
        RI = small[:, 12:16]

        unit_base = {0: 0, 1: 8, 2: 24}
        N_SOFT = {0: 8, 1: 16, 2: 8}

        qk_pairs = {
            0: [(4, "g_q_b", 1), (6, "g_q_b", 1), (12, "g_k_b", 1), (14, "g_k_b", 1)],
            1: [(0, "g_q_c", 0), (2, "g_q_c", 0), (8, "g_k_c", 0), (10, "g_k_c", 0),
                (4, "g_q_d", 1), (6, "g_q_d", 1), (12, "g_k_d", 1), (14, "g_k_d", 1)],
        }

        def plan_norm(n):
            plan(("ssq", n), 7)

        def plan_layer(l):
            for m in range(16):
                plan(("qk", l, m), 4 + m % 3)
            for j in range(8):
                plan(("v", l, j), 4 + (16 + j) % 3)
            if l == 1:
                plan(("forget", l), 7)
            for i, (m, g, rope) in enumerate(qk_pairs[l]):
                plan(("hssq", l, i), 4 + i % 2)
            for i, (m, g, rope) in enumerate(qk_pairs[l]):
                if rope:
                    plan(("rot", l, i), 6 + i % 2)
            if l == 0:
                for t in range(8 + 2):
                    if t < 8:
                        plan(("z", l, t), 4 + t % 2)
                    if t >= 2 and t % 2 == 0:
                        plan(("o", l, (t - 2) // 2), (t - 2) // 2 % 4)
                plan_soft(l, 8, 4)
            else:
                plan_soft(l, 16, 0)
            for m in range(4):
                plan(("y", l, m), m)

        def plan_soft(l, n, pair0):
            for t in range(n + 2):
                if t < n:
                    plan(("s", l, t), 4 + t % 2)
                if 1 <= t <= n:
                    plan(("pt", l, t - 1), 6 + (t - 1) % 2)
                if t >= 2 and t % 2 == 0:
                    plan(("o", l, pair0 + (t - 2) // 2), (pair0 + (t - 2) // 2) % 4)

        US = view(0, 15, T)
        GATES = view(3840, 16, T)
        YM = view(7936, 4, T)
        YR = view(8960, 4, T)
        U0 = view(9984, 15, T + 2)
        CQ = view(13856, 2, T)
        CKV = view(14368, T)
        KR = view(14624, T)
        CQN = view(14880, 2, T)
        CKVN = view(15392, T)
        QM = view(15648, 8, T)
        KM = view(17696, 8, T)
        VM = view(19744, 2, 512)
        COSM = view(20768, T)
        SINM = view(21024, T)
        SM2 = [view(21280 + 512 * j, 512) for j in range(2)]
        PR2 = [view(22304 + 512 * j, 512) for j in range(2)]
        PT2 = [view(23328 + 512 * j, 512) for j in range(2)]
        TMPM = view(24352, 8, T)
        ANG = view(26400, T)
        ANG2 = view(26656, T)
        POS = view(26912, T, dt=I32)
        POSF = view(27168, T)
        AR = view(9984, 8, 2, 2, P)
        BT = view(14080, 8, 2, P)
        KT = view(16128, 8, 2, P)
        CF = view(18176, 8, 2, P)
        CE = view(20224, 8, 2, P)
        RATE = view(22272, 8, T)
        KD = view(24320, 8, T)
        KK = view(26368, 4, T)
        G2 = xn[:, 0:4, :]
        VTM = xn[:, 4:8, :].rearrange("p a b -> p (a b)").rearrange("p (c n) -> p c n", c=2)
        BTM = sq[:, 0:4, :].rearrange("p a b -> p (a b)").rearrange("p (d n) -> p d n", d=2)
        KTM = sq[:, 4:8, :].rearrange("p a b -> p (a b)").rearrange("p (d n) -> p d n", d=2)
        UNIT = 18176
        M4 = [view(UNIT + 2048 * u, 2, 4, P) for u in range(4)]
        LV = [view(UNIT + 2048 * u + 1024, 2, P) for u in range(4)]
        WW = [view(UNIT + 2048 * u + 1280, 2, P) for u in range(4)]
        TNTT = [view(UNIT + 2048 * u + 1536, 2, 2, P) for u in range(4)]
        SSC = small[:, 16:24]
        REF = small[:, 24:40].rearrange("p (a c) -> p a c", c=2)
        XX = [view(26368 + 128 * u, P) for u in range(4)]
        UU = [view(26880 + 128 * u, P) for u in range(4)]
        ST = view(1024, 8, P)
        LORA = [view(8960, 512), view(9472, 512), view(27648, 512)]
        MG = view(9984, 8, T)
        MT = [view(12032 + 256 * j, T) for j in range(2)]
        WAVES = [(0, 0), (1, 1), (0, 1), (1, 0)]

        HTOK = view(0, 2, D)
        ACC = view(2048, 2, D)
        QP = view(4096, 16, T)
        SC = view(8192, 2, 16, P)
        GB = 8
        GR = view(4096, GB, D)
        SCR = view(12288, 16, P)
        TV = view(14336, 16, 16)
        TI = view(14592, 16, 16, dt=U32)
        TIF = view(14848, 16, 16)
        CAND = view(15104, 8, 256)
        CSCR = view(17152, 8, 256)
        BV = view(19200, 8, 16)
        BP = view(19328, 8, 16, dt=U32)
        BI = view(19456, P, dt=U32)
        BF = view(19584, P)
        EQ = view(19712, P, 16)
        E0 = view(21760, P)
        E1 = view(21888, P)
        EIDX = view(22016, 2, P, dt=U32)
        GATE = view(22272, 2, P)
        DOTS = view(22528, 2, P)
        WT = view(22784, 2, P)
        PEX = view(23040, 8, 16)
        STAGE = sb("stage", [P, 16], U32)
        DSTAGE = small[:, 80:88]
        WSTAGE = small[:, 96:104]
        SUM8 = small[:, 112:128]
        JUNK = [view(23168 + D * j, D) for j in range(2)]
        PIN = view(25216, 2, T)

        plan_norm(0)
        plan_norm(1)
        plan_layer(0)
        plan_norm(2)
        plan_norm(3)
        plan_norm(4)
        plan_layer(1)
        plan_norm(5)
        plan_norm(6)
        for m in range(35):
            plan(("u", m), m % 4)
        plan(("mssq", 0), 4)
        plan(("mssq", 1), 5)
        for h in range(8):
            plan(("mq", h), h % 4)
        for h in range(8):
            plan(("mk", h), h % 4)
        for j in range(2):
            plan(("mv", j), 4 + j)
        for j in range(5):
            plan(("mrot", j), 6 + j % 2)
        plan_soft(2, 8, 0)
        for d in range(2):
            for hp in range(4):
                plan(("lw", d, hp), 0 + hp % 4)
                plan(("la", d, hp), 4 + hp % 2)
        for hp in range(4):
            plan(("lg", hp), 6 + hp % 2)
        for j in range(2):
            plan(("kkss", j), 4 + j)
        for j in range(4):
            plan(("vtm", j), 0 + j)
        for j in range(8):
            plan(("bkt", j), 4 + j % 4)
        for j in range(2):
            plan(("bonus", j), j)
        for w in range(4):
            for u in range(4):
                for e in range(2):
                    plan(("gram", w, u, e), 4 * e + u)
            for l in range(7):
                for u in range(4):
                    plan(("W", w, l, u), u)
                if l:
                    for u in range(4):
                        plan(("TT", w, l, u), 4 + u)
            for u in range(4):
                plan(("X", w, u), u)
            for u in range(4):
                plan(("U", w, u), 4 + u)
            for u in range(4):
                plan(("O", w, u), u)
            if w < 2:
                for u in range(4):
                    plan(("ST", w, u), 4 + u)
        for j in range(2):
            plan(("gmean", j), j)
        for j in range(2):
            plan(("gvar", j), 2 + j)
        for m in range(8):
            plan(("br", 0, m), m % 4)
            plan(("br", 1, m), 4 + m % 4)
        for m in range(4):
            plan(("y", 2, m), m)
        plan_norm(7)
        for m in range(16):
            plan(("pq", m), m % 4)
        for j in range(4):
            plan(("htok", j), 4 + j)
        for j in range(8):
            plan(("sc", j), j % 4)
        for j in range(4):
            plan(("back", j), 4 + j)
        plan_norm(8)
        for m in range(8):
            plan(("pg", m), m % 4)
            plan(("pp", m), 4 + m % 3)
        plan_norm(9)

        def residual_done(eng, n):
            if n in (1, 3, 4, 6, 9):
                eng.wait_ge(x_ready, {1: 1, 3: 2, 4: 3, 6: 4, 9: 5}[n])
            for m in range(4 if n in (2, 5, 7, 8) else 0):
                emptied(eng, {2: ("y", 0, m), 5: ("y", 1, m), 7: ("y", 2, m), 8: ("back", m)}[n])

        block = ctx.enter_context(nc.Block())

        @block.sync
        def _(sp):
            def fetch(k, dst, src, i=0, wait=True):
                if wait and k >= RING:
                    sp.wait_ge(slot_free, k - RING + 1 + (RING * i))
                sp.dma_start(dst, src).then_inc(slot_loaded[k % RING], 16)

            def ffn_group(k, w, g, i=0):
                gate, up, down = w
                n0 = g * 256 + i * 512 if isinstance(i, int) else i * 512 + g * 256
                fetch(k, slot(k, KC, 256), rows(gate)[:, :, bass.ds(n0, 256)], i)
                fetch(k + 1, slot(k + 1, KC, 256), rows(up)[:, :, bass.ds(n0, 256)], i)
                fetch(k + 2, slot(k + 2, 2, D), down[bass.ds(n0, 256), :].rearrange("(k p) n -> p k n", p=P), i)

            def ffn(f):
                k0, w = at["ffn", f], ffn_w[f]
                for g in range(2):
                    ffn_group(k0 + 3 * g, w, g)
                with sp.Fori(0, (GROUPS - 3) // 2) as i:
                    for g in (2, 3):
                        ffn_group(k0 + 3 * g, w, g, i)
                ffn_group(k0 + 3 * (GROUPS - 1), w, GROUPS - 1)

            def square(k0, w, n):
                for s in range(n):
                    fetch(k0 + s, slot(k0 + s, KC, 256), rows(w)[:, :, s * 256 : (s + 1) * 256])

            for l, w_in in ((0, A["w_in_ab"][0]), (1, A["w_in_cd"][0])):
                ffn(2 * l)
                square(at["qkv", l], w_in, 12)
                square(at["wo", l], A["w_out"][l], 4)
                ffn(2 * l + 1)
            w2 = A["w_in_2"][0]
            cols = [(256 * s, 256 * s + 256) for s in range(9)] + [(2304, 2336)] + [
                (2336 + 256 * s, 2592 + 256 * s) for s in range(8)]
            for s, (a, b) in enumerate(cols):
                k = at["in2"] + s
                fetch(k, slot(k, KC, b - a), rows(w2)[:, :, a:b])
            k = at["mla"]
            fetch(k, slot(k, 2, 768), rows(A["mla_w_qup_2"][0]))
            fetch(k + 1, slot(k + 1, 1, 1024), rows(A["mla_w_kvup_2"][0]))
            k = at["br"]
            for j, w in enumerate((A["w_br_rwkv_2"][0], A["w_br_mla_2"][0])):
                for s in range(2):
                    fetch(k + 2 * s + j, slot(k + 2 * s + j, 4, 512), rows(w)[:, :, s * 512 : (s + 1) * 512])
            square(at["wo", 2], A["w_out_2"][0], 4)
            square(at["wq"], A["peer_w_q_2"][0], 8)
            k = at["keys"]
            fetch(k, slot(k, 16, 128), A["sub_keys_t"].rearrange("h d k -> d h k"))
            square(at["pg"], A["w_ple_gate_2"][0], 4)
            k = at["pp"]
            fetch(k, slot(k, 2, 1024), rows(A["w_ple_proj_2"][0]))

        @block.tensor
        def _(pe):
            owed = [0]

            def mm(dst, lhsT, rhs, start, stop_, loose=False):
                return pe.matmul(dst, lhsT, rhs, start=start, stop=stop_, skip_group_check=loose)

            def release(ins):
                if owed[0]:
                    ins.then_inc(slot_free, owed[0])
                    owed[0] = 0

            def have(k, i=0):
                pe.wait_ge(slot_loaded[k % RING], 16 * (k // RING + 1) + 16 * i)

            def norm(n):
                dst = fill_begin(pe, ("ssq", n))
                for k in range(KC):
                    if k % 4 == 0:
                        pe.wait_ge(sq_ready, 2 * n + k // 4 + 1)
                    ins = mm(dst[:, 0:T], C("ones", P), sq[:, k, :], k == 0, k == KC - 1)
                    if k == 0:
                        release(ins)
                fill_end(ins, ("ssq", n))

            def ffn(f, n):
                k0, base = at["ffn", f], CHUNKS * f

                def gate_up(k, c, i, first):
                    b, s = bank[4 + c % 2], c % 2
                    if not first:
                        pe.wait_ge(h_ready, base + c - 1 + 4 * i)
                    for j in range(2):
                        if s == 0:
                            have(k + j, i)
                        w = slot(k + j, KC, 256)
                        for kk in range(KC):
                            if c == 0 and first and j == 0:
                                pe.wait_ge(xn_ready, KC * n + kk + 1)
                            ins = mm(b[:, j * T : (j + 1) * T], w[:, kk, s * P : (s + 1) * P], xn[:, kk, :],
                                     kk == 0, kk == KC - 1)
                        if s == 1 and j == 0:
                            ins.then_inc(slot_free, 1)
                    ins.then_inc(gu_ready, 1)
                    if s == 1:
                        owed[0] += 1

                def down(k, c, i):
                    if c % 2 == 0:
                        have(k + 2, i)
                    pe.wait_ge(h_ready, base + c + 1 + 4 * i)
                    w = slot(k + 2, 2, D)
                    for m in range(KC):
                        ins = mm(bank[m // 2][:, (m % 2) * T : (m % 2 + 1) * T], w[:, c % 2, m * P : (m + 1) * P],
                                 hT[:, c % 2, :], c == 0 and m % 2 == 0, c == CHUNKS - 1, loose=True)
                        if m == 0:
                            release(ins)
                    if c == CHUNKS - 1:
                        ins.then_inc(y_ready, 1)
                        owed[0] += 1
                    elif c % 2 == 1:
                        ins.then_inc(slot_free, 1)

                def group(g, i=0):
                    for s in range(2):
                        c = 2 * g + s
                        gate_up(k0 + 3 * g, c, i, g == 0)
                        if c > 0:
                            down(k0 + 3 * ((c - 1) // 2), c - 1, i)

                group(0)
                group(1)
                with pe.Fori(0, (GROUPS - 3) // 2) as i:
                    group(2, i)
                    group(3, i)
                group(GROUPS - 1)
                down(k0 + 3 * (GROUPS - 1), CHUNKS - 1, 0)

            def out_product(l, n_wait, src):
                for m in range(KC):
                    k = at["wo", l] + m // 2
                    b = fill_begin(pe, ("y", l, m // 2)) if m % 2 == 0 else bank[fill_of["y", l, m // 2][0]]
                    if m % 2 == 0:
                        have(k)
                    for kk in range(KC):
                        if m == 0:
                            n_wait(kk)
                        ins = mm(b[:, (m % 2) * T : (m % 2 + 1) * T], slot(k, KC, 256)[:, kk, (m % 2) * P : (m % 2 + 1) * P],
                                 src[:, kk, :], kk == 0, kk == KC - 1)
                        if kk == 0:
                            release(ins)
                    if m % 2:
                        fill_end(ins, ("y", l, m // 2))
                        owed[0] += 1

            def soft(l, n, pair0, q_of, k_of, v_of, both, extra=None):
                base = unit_base[l]
                for t in range(n + 2):
                    if t < n:
                        b = fill_begin(pe, ("s", l, t))
                        if both:
                            for qb in range(2):
                                ins = mm(b[:, qb * T : (qb + 1) * T], q_of(t)[:, qb * P : (qb + 1) * P], k_of(t), True, True)
                        else:
                            for a, w, qb in ((0, P, 0), (P, T, 1)):
                                ext = extra is not None and extra(t)
                                ins = mm(b[:, a : a + w], q_of(t)[:, qb * P : (qb + 1) * P], k_of(t)[:, 0:w], True, not ext)
                                if ext:
                                    ins = mm(b[:, a : a + w], FL[0:2, t, qb * P : (qb + 1) * P], FR[0:2, t, 0:w], False, True)
                        fill_end(ins, ("s", l, t))
                    if 1 <= t <= n:
                        u = t - 1
                        b = fill_begin(pe, ("pt", l, u))
                        pe.wait_ge(S("weights_ready"), base + u + 1)
                        pr = (PR2 if both else PR)[u % 2]
                        moves = ((0, 0), (P, 2 * P), (2 * P, P), (3 * P, 3 * P)) if both else ((0, 0), (P, P), (2 * P, 2 * P))
                        for src, dst in moves:
                            ins = pe.transpose(b[:, dst : dst + P], pr[:, src : src + P], ident)
                        fill_end(ins, ("pt", l, u))
                    if t >= 2:
                        u = t - 2
                        pair = ("o", l, pair0 + u // 2)
                        b = fill_begin(pe, pair) if u % 2 == 0 else bank[fill_of[pair][0]]
                        emptied(pe, ("pt", l, u))
                        ptb = (PT2 if both else PT)[u % 2]
                        o = b[(u % 2) * HD : (u % 2 + 1) * HD, 0:T]
                        mm(o, v_of(u, 0), ptb[:, 0:T], True, False)
                        if both:
                            ins = mm(o, v_of(u, 1), ptb[:, T : 2 * T], False, True)
                        else:
                            ins = mm(o[:, P:T], v_of(u, 1), ptb[:, T : T + P], False, True)
                        if u % 2:
                            fill_end(ins, pair)


            head = lambda buf, c0, h: buf[(h % 2) * HD : (h % 2 + 1) * HD, c0 + h // 2, :]

            def stick():
                for t in range(8 + 2):
                    if t < 8:
                        b = fill_begin(pe, ("z", 0, t))
                        q, k = head(QK, 0, t), head(QK, 8, t)
                        ins = mm(b[:, 0:T], k[:, 0:P], q, True, False, loose=True)
                        release(ins)
                        mm(b[:, T : T + P], k[:, P:T], q[:, P:T], False, False, loose=True).then_inc(S("z_ready"), 1)
                    if 1 <= t <= 8:
                        u = t - 1
                        b, lg = bank[4 + u % 2], ZL[u % 2]
                        pe.wait_ge(S("keep_ready"), 2 * u + 2)
                        mm(b[:, 0:T], C("suffix", P), lg[:, 0:T], False, False, loose=True)
                        mm(b[:, P:T], C("after", P), lg[:, T : T + P], False, True, loose=True)
                        fill_end(mm(b[:, T : T + P], C("suffix", P), lg[:, T : T + P], False, True, loose=True), ("z", 0, u))
                    if t >= 2:
                        u = t - 2
                        pair = ("o", 0, u // 2)
                        b = fill_begin(pe, pair) if u % 2 == 0 else bank[fill_of[pair][0]]
                        pe.wait_ge(S("stick_ready"), 2 * u + 2)
                        o = b[(u % 2) * HD : (u % 2 + 1) * HD, 0:T]
                        mm(o, VT[:, 0, u * HD : (u + 1) * HD], PT[u % 2][:, 0:T], True, False)
                        ins = mm(o[:, P:T], VT[:, 1, u * HD : (u + 1) * HD], PT[u % 2][:, T : T + P], False, True)
                        if u % 2:
                            fill_end(ins, pair)

            def layer(l):
                for s in range(12):
                    k = at["qkv", l] + s
                    have(k)
                    w = slot(k, KC, 256)
                    for half in range(2):
                        label = ("qk", l, 2 * s + half) if s < 8 else ("v", l, 2 * (s - 8) + half)
                        b = fill_begin(pe, label)
                        for kk in range(KC):
                            if s == 0 and half == 0:
                                pe.wait_ge(xn_ready, KC * (1 + 3 * l) + kk + 1)
                            if s < 8:
                                ins = mm(b[:, 0:T], w[:, kk, half * P : (half + 1) * P], xn[:, kk, :], kk == 0, kk == KC - 1)
                            else:
                                ins = mm(b[:, 0:T], xn[:, kk, half * P : (half + 1) * P], w[:, kk, :], kk == 0, kk == KC - 1)
                            if kk == 0:
                                release(ins)
                        fill_end(ins, label)
                    owed[0] += 1
                if l == 1:
                    b = fill_begin(pe, ("forget", 1))
                    pe.wait_ge(S("wf_loaded"), 16)
                    for kk in range(KC):
                        ins = mm(b[0:8, 0:T], WF[:, kk, :], xn[:, kk, :], kk == 0, kk == KC - 1)
                        if kk == 0:
                            release(ins)
                    fill_end(ins, ("forget", 1))
                first = 4 * l
                for i, (m, g, rope) in enumerate(qk_pairs[l]):
                    b = fill_begin(pe, ("hssq", l, i))
                    pe.wait_ge(S("hsq_ready"), first + i + 1)
                    fill_end(mm(b[:, 0:512], C("heads", P), HSQ[i % 2], True, True), ("hssq", l, i))
                for i, (m, g, rope) in enumerate(qk_pairs[l]):
                    if rope:
                        b = fill_begin(pe, ("rot", l, i))
                        pe.wait_ge(S("hn_ready"), first + i + 1)
                        fill_end(mm(b[:, 0:512], C("turn", P), QK[:, m : m + 2, :].rearrange("p a b -> p (a b)"), True, True),
                                 ("rot", l, i))
                for m in (13, 14, 15):
                    emptied(pe, ("qk", l, m))
                for j in (5, 6, 7):
                    emptied(pe, ("v", l, j))
                if l == 0:
                    stick()
                else:
                    pe.wait_ge(S("hn_ready"), 12)
                    pe.wait_ge(S("forget_ready"), 32)
                pe.wait_ge(S("rope_ready"), 4 * (l + 1))
                h0 = 8 if l == 0 else 0
                soft(l, 8 if l == 0 else 16, 4 if l == 0 else 0,
                     lambda t: head(QK, 0, h0 + t), lambda t: head(QK, 8, h0 + t),
                     lambda t, kb: VT[:, kb, (h0 + t) * HD : (h0 + t + 1) * HD], False,
                     (lambda t: t < 8) if l == 1 else None)
                out_product(l, lambda kk: emptied(pe, ("o", l, kk)), MIX)

            def second_in():
                for s in range(18):
                    k = at["in2"] + s
                    have(k)
                    width = 32 if s == 9 else 256
                    w = slot(k, KC, width)
                    for half in range(1 if s == 9 else 2):
                        m = 2 * s + half if s < 10 else 2 * s - 1 + half
                        b = fill_begin(pe, ("u", m))
                        for kk in range(KC):
                            if m == 0:
                                pe.wait_ge(xn_ready, KC * 6 + kk + 1)
                            if s == 9:
                                ins = mm(b[64:96, 0:T], w[:, kk, :], xn[:, kk, :], kk == 0, kk == KC - 1)
                            else:
                                ins = mm(b[:, 0:T], w[:, kk, half * P : (half + 1) * P], xn[:, kk, :], kk == 0, kk == KC - 1)
                            if kk == 0:
                                release(ins)
                        fill_end(ins, ("u", m))
                    owed[0] += 1

            def latent():
                pe.wait_ge(S("csq_ready"), 2)
                b = fill_begin(pe, ("mssq", 0))
                release(mm(b[:, 0:T], C("ones", P), TMPM[:, 0, :], True, False))
                fill_end(mm(b[:, 0:T], C("ones", P), TMPM[:, 1, :], False, True), ("mssq", 0))
                b = fill_begin(pe, ("mssq", 1))
                fill_end(mm(b[:, 0:T], C("ones", P), TMPM[:, 2, :], True, True), ("mssq", 1))
                kq = at["mla"]
                wq, wkv = slot(kq, 2, 768), slot(kq + 1, 1, 1024)
                have(kq)
                pe.wait_ge(S("cn_ready"), 3)
                for h in range(8):
                    b = fill_begin(pe, ("mq", h))
                    for kk in range(2):
                        ins = mm(b[0:96, 0:T], wq[:, kk, h * 96 : h * 96 + 96], CQN[:, kk, :], kk == 0, kk == 1)
                    fill_end(ins, ("mq", h))
                owed[0] += 1
                have(kq + 1)
                for h in range(8):
                    b = fill_begin(pe, ("mk", h))
                    fill_end(mm(b[0:64, 0:T], wkv[:, 0, h * P : h * P + 64], CKVN, True, True), ("mk", h))
                for j in range(2):
                    b = fill_begin(pe, ("mv", j))
                    fill_end(mm(b[:, 0:512].rearrange("p (a b) -> p a b", a=8), CKVN[:, j * P : (j + 1) * P],
                                wkv[:, 0, :].rearrange("p (a b) -> p a b", a=8)[:, :, 64:128], True, True), ("mv", j))
                owed[0] += 1
                for j in range(5):
                    b = fill_begin(pe, ("mrot", j))
                    if j < 4:
                        emptied(pe, ("mq", 2 * j))
                        emptied(pe, ("mq", 2 * j + 1))
                        src = QM[64:96, 2 * j : 2 * j + 2, :].rearrange("p a b -> p (a b)")
                    else:
                        emptied(pe, ("u", 18))
                        src = KR[64:96, :]
                    n = 512 if j < 4 else T
                    fill_end(mm(b[64:96, 0:n], C("turn_mla", 32)[64:96, :], src, True, True), ("mrot", j))
                pe.wait_ge(S("mrope_ready"), 2)
                for h in (5, 6, 7):
                    emptied(pe, ("mk", h))
                for j in range(2):
                    emptied(pe, ("mv", j))
                soft(2, 8, 0, lambda t: QM[0:96, t, :], lambda t: KM[0:96, t, :],
                     lambda t, kb: VM[:, kb, t * HD : (t + 1) * HD], True)

            def recurrence():
                pe.wait_ge(S("lora_loaded"), 48)
                pe.wait_ge(S("lora_in_ready"), 2)
                pe.wait_ge(S("shifted"), 15)
                for d in range(2):
                    for hp in range(4):
                        for j, name in enumerate(("lw", "la")):
                            b = fill_begin(pe, (name, d, hp))
                            ins = mm(b[:, 0:T], LORA[j][64 * d : 64 * d + 64, hp * P : (hp + 1) * P],
                                     US[64 * d : 64 * d + 64, 12 + j, :], True, True)
                            fill_end(ins, (name, d, hp))
                for hp in range(4):
                    b = fill_begin(pe, ("lg", hp))
                    fill_end(mm(b[:, 0:T], LORA[2][:, hp * P : (hp + 1) * P], US[:, 14, :], True, True), ("lg", hp))
                for j in range(2):
                    b = fill_begin(pe, ("kkss", j))
                    pe.wait_ge(S("kksq_ready"), 1)
                    fill_end(mm(b[:, 0:512], C("heads", P), sq[:, 2 * j : 2 * j + 2, :].rearrange("p a b -> p (a b)"), True, True),
                             ("kkss", j))
                for j in range(4):
                    c, half = j // 2, j % 2
                    b = fill_begin(pe, ("vtm", j))
                    for i in range(2):
                        ins = pe.transpose(b[:, i * P : (i + 1) * P], US[:, 8 + 2 * half + i, c * P : (c + 1) * P], ident)
                    fill_end(ins, ("vtm", j))
                pe.wait_ge(S("bkt_ready"), 2)
                for j in range(8):
                    d = j // 4
                    b = fill_begin(pe, ("bkt", j))
                    pe.transpose(b[:, 0:P], BT[:, j, d, :], ident)
                    fill_end(pe.transpose(b[:, P : 2 * P], KT[:, j, d, :], ident), ("bkt", j))
                pe.wait_ge(S("bonus_in_ready"), 4)
                for j in range(2):
                    b = fill_begin(pe, ("bonus", j))
                    fill_end(mm(b[:, 0:512], C("heads", P), US[:, 4 + 2 * j : 6 + 2 * j, :].rearrange("p a b -> p (a b)"), True, True),
                             ("bonus", j))
                for j in range(4):
                    emptied(pe, ("vtm", j))
                for j in range(4, 8):
                    emptied(pe, ("bkt", j))
                pe.wait_ge(S("ar_ready"), 2)
                for w, (d, c) in enumerate(WAVES):
                    for u in range(4):
                        j = 4 * d + u
                        for e in range(2):
                            ps = slice(64 * e, 64 * e + 64)
                            b = fill_begin(pe, ("gram", w, u, e))
                            ar = AR[ps, j, c, :, :].rearrange("p a b -> p (a b)")
                            mm(b[:, 0:T], BT[ps, j, c, :], ar, True, True)
                            fill_end(mm(b[:, T : 2 * T], KT[ps, j, c, :], ar, True, True), ("gram", w, u, e))
                    for l in range(7):
                        for u in range(4):
                            b = fill_begin(pe, ("W", w, l, u))
                            pe.wait_ge(S("level_ready"), 28 * w + 4 * l + u + 1)
                            if l:
                                emptied(pe, ("TT", w, l - 1, u) if l > 1 else ("W", w, 0, u))
                            for e in range(2):
                                if l:
                                    ins = mm(b[:, e * P : (e + 1) * P], LV[u][:, e, :], TNTT[u][:, 0, e, :], True, True)
                                else:
                                    ins = pe.transpose(b[:, e * P : (e + 1) * P], LV[u][:, e, :], ident)
                            fill_end(ins, ("W", w, l, u))
                        if l:
                            for u in range(4):
                                b = fill_begin(pe, ("TT", w, l, u))
                                emptied(pe, ("W", w, l, u))
                                for e in range(2):
                                    if l < 6:
                                        mm(b[:, e * P : (e + 1) * P], TNTT[u][:, 1, e, :], WW[u][:, e, :], True, True)
                                    ins = mm(b[:, (2 + e) * P : (3 + e) * P], WW[u][:, e, :], TNTT[u][:, 1, e, :], True, True)
                                fill_end(ins, ("TT", w, l, u))
                    for u in range(4):
                        j = 4 * d + u
                        b = fill_begin(pe, ("X", w, u))
                        if w >= 2:
                            emptied(pe, ("ST", w - 2, u))
                        if w >= 2:
                            mm(b[:, 0:P], AR[:, j, c, 0, :], ST[:, j, :], True, False, loose=True)
                        for e in range(2):
                            ins = mm(b[:, e * HD : (e + 1) * HD], M4[u][:, e, 2, :],
                                     VTM[:, c, u * P + e * HD : u * P + (e + 1) * HD], w < 2, True, loose=w >= 2)
                        fill_end(ins, ("X", w, u))
                    for u in range(4):
                        b = fill_begin(pe, ("U", w, u))
                        emptied(pe, ("X", w, u))
                        emptied(pe, ("TT", w, 6, u))
                        for e in range(2):
                            ins = mm(b[:, e * HD : (e + 1) * HD], TNTT[u][:, 1, e, :], XX[u][:, e * HD : (e + 1) * HD], True, True)
                        fill_end(ins, ("U", w, u))
                    for u in range(4):
                        j = 4 * d + u
                        b = fill_begin(pe, ("O", w, u))
                        emptied(pe, ("U", w, u))
                        if w >= 2:
                            mm(b[:, 0:P], ST[:, j, :], AR[:, j, c, 1, :], True, False, loose=True)
                        for e in range(2):
                            o = b[64 * e : 64 * e + 64, 0:P]
                            mm(o, VTM[:, c, u * P + e * HD : u * P + (e + 1) * HD], M4[u][:, e, 3, :], w < 2, False, loose=w >= 2)
                            ins = mm(o, UU[u][:, e * HD : (e + 1) * HD], M4[u][:, e, 1, :], False, True, loose=w >= 2)
                        fill_end(ins, ("O", w, u))
                    if w < 2:
                        for u in range(4):
                            b = fill_begin(pe, ("ST", w, u))
                            for e in range(2):
                                ps = slice(64 * e, 64 * e + 64)
                                cols = slice(u * P + e * HD, u * P + (e + 1) * HD)
                                mm(b[ps, 0:HD], BTM[:, d, cols], UU[u][:, e * HD : (e + 1) * HD], True, False)
                                ins = mm(b[ps, 0:HD], KTM[:, d, cols], VTM[:, c, cols], False, True)
                            fill_end(ins, ("ST", w, u))
                for name in ("gmean", "gvar"):
                    for j in range(2):
                        b = fill_begin(pe, (name, j))
                        if name == "gmean":
                            for u in range(4):
                                emptied(pe, ("O", 3, u))
                        else:
                            pe.wait_ge(S("ysq_ready"), 1)
                        src = YR if name == "gmean" else sq
                        fill_end(mm(b[:, 0:512], C("heads", P), src[:, 2 * j : 2 * j + 2, :].rearrange("p a b -> p (a b)"), True, True),
                                 (name, j))

            def branches_out():
                pe.wait_ge(S("y_rw_ready"), 1)
                for pair in range(4):
                    emptied(pe, ("o", 2, pair))
                for m in range(8):
                    for j, src in enumerate((YR, YM)):
                        k = at["br"] + 2 * (m // 4) + j
                        b = fill_begin(pe, ("br", j, m))
                        if m % 4 == 0:
                            have(k)
                        for kk in range(4):
                            ins = mm(b[:, 0:T], slot(k, 4, 512)[:, kk, (m % 4) * P : (m % 4 + 1) * P], src[:, kk, :], kk == 0, kk == 3)
                            if kk == 0:
                                release(ins)
                        fill_end(ins, ("br", j, m))
                        if m % 4 == 3:
                            owed[0] += 1
                out_product(2, lambda kk: pe.wait_ge(S("merged"), kk + 1), MG)

            def experts():
                for m in range(16):
                    k = at["wq"] + m // 2
                    if m % 2 == 0:
                        have(k)
                    b = fill_begin(pe, ("pq", m))
                    for kk in range(KC):
                        if m == 0:
                            pe.wait_ge(xn_ready, KC * 7 + kk + 1)
                        ins = mm(b[:, 0:T], slot(k, KC, 256)[:, kk, (m % 2) * P : (m % 2 + 1) * P], xn[:, kk, :], kk == 0, kk == KC - 1)
                        if kk == 0:
                            release(ins)
                    fill_end(ins, ("pq", m))
                    owed[0] += m % 2
                for j in range(4):
                    b = fill_begin(pe, ("htok", j))
                    for i in range(4):
                        ins = pe.transpose(b[:, i * P : (i + 1) * P], xn[:, 4 * (j % 2) + i, (j // 2) * P : (j // 2 + 1) * P], ident)
                        if i == 0:
                            release(ins)
                    fill_end(ins, ("htok", j))
                k = at["keys"]
                have(k)
                for m in (12, 13, 14, 15):
                    emptied(pe, ("pq", m))
                for j in range(8):
                    b = fill_begin(pe, ("sc", j))
                    for i in range(4):
                        hc = 4 * (j % 4) + i
                        ins = mm(b[:, i * P : (i + 1) * P], QP[:, hc, (j // 4) * P : (j // 4 + 1) * P], slot(k, 16, P)[:, hc, :], True, True)
                    fill_end(ins, ("sc", j))
                owed[0] += 1
                for j in range(4):
                    b = fill_begin(pe, ("back", j))
                    for i in range(4):
                        tb = i % 2
                        if j == 0:
                            pe.wait_ge(S("rows_used"), 8 * (16 * (3 + tb) + 1))
                        m = 2 * j + i // 2
                        ins = pe.transpose(b[:, i * P : (i + 1) * P], ACC[:, tb, m * P : (m + 1) * P], ident)
                        if i == 0:
                            release(ins)
                    fill_end(ins, ("back", j))

            def ple():
                pe.wait_ge(S("p_loaded"), 16)
                kp = at["pp"]
                for m in range(8):
                    k = at["pg"] + m // 2
                    if m % 2 == 0:
                        have(k)
                    b = fill_begin(pe, ("pg", m))
                    for kk in range(KC):
                        if m == 0:
                            pe.wait_ge(xn_ready, KC * 8 + kk + 1)
                        ins = mm(b[:, 0:T], slot(k, KC, 256)[:, kk, (m % 2) * P : (m % 2 + 1) * P], xn[:, kk, :], kk == 0, kk == KC - 1)
                    fill_end(ins, ("pg", m))
                    if m == 0:
                        have(kp)
                    b = fill_begin(pe, ("pp", m))
                    for kk in range(2):
                        ins = mm(b[:, 0:T], slot(kp, 2, 1024)[:, kk, m * P : (m + 1) * P], PIN[:, kk, :], kk == 0, kk == 1)
                    fill_end(ins, ("pp", m))

            pe.wait_ge(loaded_c, 16)
            for l in range(2):
                norm(3 * l)
                ffn(2 * l, 3 * l)
                norm(3 * l + 1)
                layer(l)
                norm(3 * l + 2)
                ffn(2 * l + 1, 3 * l + 2)
            norm(6)
            second_in()
            latent()
            recurrence()
            branches_out()
            norm(7)
            experts()
            norm(8)
            ple()
            norm(9)

        @block.scalar
        def _(act):
            chain = Chain(act_done)
            act.dma_start(xT[:, :, :], rows(A["xT"])).then_inc(loaded_x, 16)
            act.dma_start(con[:, :], A["con"]).then_inc(loaded_c, 16)
            act.dma_start(vec[:, :], A["vec"]).then_inc(loaded_v, 16)
            act.dma_start(WF, rows(A["w_in_cd"][0])[:, :, 3 * D : 3 * D + 8]).then_inc(S("wf_loaded"), 16)
            act.dma_start(small[0:8, 40:41], A["b_f"].rearrange("a n -> n a")).then_inc(S("bf_loaded"), 16)
            act.wait_ge(loaded_x, 16)
            act.wait_ge(loaded_c, 16)
            act.wait_ge(loaded_v, 16)

            def norm(n):
                residual_done(act, n)
                for half in range(2):
                    act.activation(sq[:, 4 * half : 4 * half + 4, :], xT[:, 4 * half : 4 * half + 4, :],
                                   ACT.Square).then_inc(sq_ready, 1)
                src = take(act, ("ssq", n))
                give(act.activation(std[:, :], src[:, 0:T], ACT.Sqrt, bias=eps(0), scale=1.0 / D), ("ssq", n))

            def ffn(f):
                base = CHUNKS * f
                act.preload_act_table(ACT.Silu)

                def chunk(c, i=0):
                    act.wait_ge(gu_ready, base + c + 1 + 4 * i)
                    act.activation(sgate[:, c % 2, :], bank[4 + c % 2][:, 0:T], ACT.Silu).then_inc(silu_ready, 1)

                for c in range(4):
                    chunk(c)
                with act.Fori(0, (GROUPS - 3) // 2) as i:
                    for c in range(4, 8):
                        chunk(c, i)
                for c in (CHUNKS - 2, CHUNKS - 1):
                    chunk(c)

            def soft(l, n, both):
                base = unit_base[l]
                sm, pr, ptb = (SM2, PR2, PT2) if both else (SM, PR, PT)
                for t in range(n + 1):
                    if t < n:
                        act.wait_ge(S("max_ready"), base + t + 1)
                        src = take(act, ("s", l, t)) if both else sm[t % 2]
                        for qb, (a, w) in enumerate(((0, T), (T, T)) if both else ((0, P), (P, T))):
                            c = 2 * (t % 2) + qb
                            ins = act.activation(pr[t % 2][:, a : a + w], src[:, a : a + w], ACT.Exp,
                                                 bias=NM[:, c : c + 1], scale=SCALE[l], accum_out=RS[:, c : c + 1])
                            if not both:
                                ins.then_inc(S("exp_ready"), 1)
                        if both:
                            give(ins, ("s", l, t))
                    if t >= 1:
                        u = t - 1
                        b = take(act, ("pt", l, u))
                        w = 512 if both else 384
                        give(act.activation(ptb[u % 2][:, 0:w], b[:, 0:w], ACT.Copy), ("pt", l, u))

            def layer(l):
                for m in range(16):
                    b = take(act, ("qk", l, m))
                    give(act.activation(QK[:, m, :], b[:, 0:T], ACT.Copy), ("qk", l, m))
                for m in (13, 14, 15):
                    emptied(act, ("qk", l, m))
                first = 4 * l
                for i, (m, g, rope) in enumerate(qk_pairs[l]):
                    act.activation(HSQ[i % 2], QK[:, m : m + 2, :].rearrange("p a b -> p (a b)"),
                                   ACT.Square).then_inc(S("hsq_ready"), 1)
                    b = take(act, ("hssq", l, i))
                    if i >= 2:
                        act.wait_ge(S("hn_ready"), first + i - 1)
                    give(act.activation(HSTD[i % 2], b[:, 0:512], ACT.Sqrt, bias=eps(0), scale=1.0 / HD), ("hssq", l, i))
                act.preload_act_table_set("natural_log_exp_and_others")
                if l == 1:
                    b = take(act, ("forget", 1))
                    act.wait_ge(S("bf_loaded"), 16)
                    chain.link(act, act.activation(FG[0:8, 0, :], b[0:8, 0:T], ACT.Abs, bias=small[0:8, 40:41]))
                    chain.link(act, act.activation(FG[0:8, 0, :], FG[0:8, 0, :], ACT.Exp, scale=-1.0))
                    act.activation(FG[0:8, 0, :], FG[0:8, 0, :], ACT.Ln, bias=C("one", 1)[0:8, :]).then_inc(S("fln_ready"), 1)
                else:
                    for t in range(8 + 1):
                        if t < 8:
                            act.wait_ge(S("z_ready"), t + 1)
                            zl, z = ZL[t % 2][:, 0:384], bank[4 + t % 2][:, 0:384]
                            act.activation(zl, z, ACT.Abs).then_inc(S("abs_ready"), 1)
                            act.wait_ge(S("abs_ready"), t + 1)
                            chain.link(act, act.activation(zl, zl, ACT.Exp, scale=-0.125))
                            act.activation(zl, zl, ACT.Ln, bias=C("one", 1)).then_inc(S("ln_ready"), 1)
                        if t >= 1:
                            u = t - 1
                            b = take(act, ("z", 0, u))
                            give(act.activation(PT[u % 2][:, 0:384], b[:, 0:384], ACT.Exp, scale=0.125), ("z", 0, u))
                soft(l, 8 if l == 0 else 16, False)

            def second_in():
                act.preload_act_table(ACT.Sigmoid)
                residual_done(act, 6)
                act.dma_start(LORA[0], A["rw_w2_2"][0].rearrange("d l n -> (d l) n")).then_inc(S("lora_loaded"), 16)
                act.dma_start(LORA[1], A["rw_a2_2"][0].rearrange("d l n -> (d l) n")).then_inc(S("lora_loaded"), 16)
                act.dma_start(LORA[2], A["rw_g2_2"][0]).then_inc(S("lora_loaded"), 16)
                for m in range(35):
                    b = take(act, ("u", m))[:, 0:T]
                    if m < 15:
                        dst = U0[:, m, 1 : T + 1]
                    elif m < 17:
                        dst = CQ[:, m - 15, :]
                    elif m == 17:
                        dst = CKV
                    elif m == 18:
                        dst, b = KR[64:96, :], b[64:96, :]
                    else:
                        dst = GATES[:, m - 19, :]
                    give(act.activation(dst, b, ACT.Copy if m < 19 else ACT.Sigmoid), ("u", m))

            def latent():
                for m in (15, 16, 17):
                    emptied(act, ("u", m))
                act.activation(TMPM[:, 0:2, :], CQ, ACT.Square).then_inc(S("csq_ready"), 1)
                act.activation(TMPM[:, 2, :], CKV, ACT.Square).then_inc(S("csq_ready"), 1)
                for j, width in ((0, 256), (1, 128)):
                    b = take(act, ("mssq", j))
                    give(act.activation(TMPM[:, 3 + j, :], b[:, 0:T], ACT.Sqrt, bias=eps(0), scale=1.0 / width), ("mssq", j))
                act.wait_ge(S("angle_ready"), 2)
                act.activation(SINM[64:96, :], ANG[64:96, :], ACT.Sin).then_inc(S("trig_ready"), 1)
                act.activation(COSM[64:96, :], ANG2[64:96, :], ACT.Sin).then_inc(S("trig_ready"), 1)
                for h in range(8):
                    b = take(act, ("mq", h))
                    give(act.activation(QM[0:96, h, :], b[0:96, 0:T], ACT.Copy), ("mq", h))
                for h in range(8):
                    b = take(act, ("mk", h))
                    give(act.activation(KM[0:64, h, :], b[0:64, 0:T], ACT.Copy), ("mk", h))
                act.preload_act_table(ACT.Exp)
                soft(2, 8, True)

            def recurrence():
                act.preload_act_table(ACT.Sigmoid)
                act.wait_ge(S("shifted"), 15)
                act.activation(US[:, 12, :], US[:, 12, :], ACT.Tanh).then_inc(S("lora_in_ready"), 1)
                act.activation(US[:, 14, :], US[:, 14, :], ACT.Sigmoid).then_inc(S("lora_in_ready"), 1)
                for d in range(2):
                    for hp in range(4):
                        j = 4 * d + hp
                        b = take(act, ("lw", d, hp))
                        give(act.activation(CF[:, j, :, :].rearrange("p a b -> p (a b)"), b[:, 0:T], ACT.Sigmoid,
                                            bias=V("rw_w0_2", j)), ("lw", d, hp))
                        b = take(act, ("la", d, hp))
                        give(act.activation(RATE[:, j, :], b[:, 0:T], ACT.Sigmoid, bias=V("rw_a0_2", j)), ("la", d, hp))
                for u in (32, 33, 34):
                    emptied(act, ("u", u))
                for hp in range(4):
                    b = take(act, ("lg", hp))
                    give(act.activation(G2[:, hp, :], b[:, 0:T], ACT.Copy), ("lg", hp))
                act.wait_ge(S("kk_ready"), 4)
                act.activation(sq[:, 0:4, :], KK, ACT.Square).then_inc(S("kksq_ready"), 1)
                for j in range(2):
                    emptied(act, ("kkss", j))
                act.activation(sq[:, 4:8, :], sq[:, 4:8, :], ACT.Sqrt).then_inc(S("kkstd_ready"), 1)
                act.preload_act_table(ACT.Exp)
                act.wait_ge(S("decay_ready"), 1)
                for d, (q, q_in, s) in enumerate(((CF, CE, 1.0), (CE, CF, -1.0))):
                    js = slice(4 * d, 4 * d + 4)
                    act.activation(BT[:, js, :, :], q[:, js, :, :], ACT.Exp, scale=-s).then_inc(S("expd_ready"), 1)
                    act.activation(AR[:, js, :, 0, :], q_in[:, js, :, :], ACT.Exp, scale=s).then_inc(S("expd_ready"), 1)
                    act.activation(AR[:, js, :, 1, :], q[:, js, :, :], ACT.Exp, scale=s).then_inc(S("expd_ready"), 1)
                act.activation(SSC, SSC, ACT.Exp).then_inc(S("carry_ready"), 1)
                for w in range(4):
                    for l in range(1, 7):
                        for u in range(4):
                            b = take(act, ("W", w, l, u))
                            give(act.activation(WW[u].rearrange("p a b -> p (a b)"), b[:, 0:T], ACT.Copy), ("W", w, l, u))
                    for u in range(4):
                        b = take(act, ("X", w, u))
                        give(act.activation(XX[u], b[:, 0:P], ACT.Copy), ("X", w, u))
                    for u in range(4):
                        b = take(act, ("U", w, u))
                        give(act.activation(UU[u], b[:, 0:P], ACT.Copy), ("U", w, u))
                for j in range(2):
                    emptied(act, ("gmean", j))
                act.activation(sq[:, 0:4, :], YR, ACT.Square).then_inc(S("ysq_ready"), 1)
                for j in range(2):
                    b = take(act, ("gvar", j))
                    give(act.activation(sq[:, 4 + 2 * j : 6 + 2 * j, :].rearrange("p a b -> p (a b)"), b[:, 0:512], ACT.Sqrt,
                                        bias=eps(1), scale=1.0 / HD), ("gvar", j))

            def experts():
                for m in range(16):
                    b = take(act, ("pq", m))
                    give(act.activation(QP[:, m, :], b[:, 0:T], ACT.Copy), ("pq", m))
                for j in range(4):
                    b = take(act, ("htok", j))
                    give(act.activation(HTOK[:, j // 2, (j % 2) * 512 : (j % 2 + 1) * 512], b[:, 0:512], ACT.Copy), ("htok", j))
                for j in range(8):
                    b = take(act, ("sc", j))
                    give(act.activation(SC[:, j // 4, 4 * (j % 4) : 4 * (j % 4) + 4, :].rearrange("p a b -> p (a b)"),
                                        b[:, 0:512], ACT.Copy), ("sc", j))
                act.preload_act_table(ACT.Exp)
                for tb in range(2):
                    act.wait_ge(S("gate_in_ready"), tb + 1)
                    act.activation(PEX, PEX, ACT.Exp).then_inc(S("gate_exp_ready"), 1)
                act.preload_act_table(ACT.Gelu)
                for tb in range(2):
                    act.wait_ge(S("dots_ready"), 16 * (tb + 1))
                    act.activation(WT[:, tb, :], DOTS[:, tb, :], ACT.Gelu).then_inc(S("gelu_ready"), 1)

            def ple():
                act.preload_act_table(ACT.Sigmoid)
                for m in range(8):
                    b = take(act, ("pg", m))
                    give(act.activation(view(4096 + T * m, T), b[:, 0:T], ACT.Sigmoid), ("pg", m))

            for l in range(2):
                norm(3 * l)
                ffn(2 * l)
                norm(3 * l + 1)
                layer(l)
                norm(3 * l + 2)
                ffn(2 * l + 1)
            norm(6)
            second_in()
            latent()
            recurrence()
            norm(7)
            experts()
            norm(8)
            act.dma_start(PIN, rows(A["pT"])).then_inc(S("p_loaded"), 16)
            ple()
            norm(9)

        @block.vector
        def _(dve):
            chain = Chain(dve_done)
            link = lambda ins: chain.link(dve, ins)
            dve.wait_ge(loaded_x, 16)
            dve.wait_ge(loaded_c, 16)
            dve.wait_ge(loaded_v, 16)

            def norm(n):
                name, c0 = norm_g[n]
                emptied(dve, ("ssq", n))
                link(dve.reciprocal(rstd[:, :], std[:, :]))
                for k in range(KC):
                    dve.scalar_tensor_tensor(out=xn[:, k, :], in0=xT[:, k, :], scalar=V(name, c0 + k), in1=rstd[:, :],
                                             op0=ALU.mult, op1=ALU.mult).then_inc(xn_ready, 1)

            def ffn(f):
                base = CHUNKS * f

                def chunk(c, i=0):
                    dve.wait_ge(silu_ready, base + c + 1 + 4 * i)
                    dve.tensor_tensor(hT[:, c % 2, :], sgate[:, c % 2, :], bank[4 + c % 2][:, T : 2 * T],
                                      ALU.mult).then_inc(h_ready, 1)

                for c in range(4):
                    chunk(c)
                with dve.Fori(0, (GROUPS - 3) // 2) as i:
                    for c in range(4, 8):
                        chunk(c, i)
                for c in (CHUNKS - 2, CHUNKS - 1):
                    chunk(c)
                dve.wait_ge(y_ready, f + 1)
                for m in range(4):
                    xs = xT[:, 2 * m : 2 * m + 2, :].rearrange("p a b -> p (a b)")
                    ins = dve.scalar_tensor_tensor(out=xs, in0=bank[m][:, :], scalar=0.5, in1=xs, op0=ALU.mult, op1=ALU.add)
                ins.then_inc(x_ready, 1)

            def residual(label, done=True):
                for m in range(4):
                    b = take(dve, (*label, m))
                    xs = xT[:, 2 * m : 2 * m + 2, :].rearrange("p a b -> p (a b)")
                    give(dve.tensor_tensor(xs, xs, b[:, :], ALU.add), (*label, m))

            def mix_out(l, pair, dst):
                b = take(dve, ("o", l, pair))
                give(dve.tensor_copy(dst[:, pair, :], b[:, 0:T]), ("o", l, pair))

            def soft(l, n, pair0, both, mask_of, dst):
                base = unit_base[l]
                sm, pr = (SM2, PR2) if both else (SM, PR)
                for t in range(n + 4):
                    if t < n:
                        b = take(dve, ("s", l, t))
                        mx = MX[:, 2 * (t % 2) : 2 * (t % 2) + 2]
                        if both:
                            link(dve.tensor_reduce(mx, b[:, 0:512].rearrange("p (a b) -> p a b", a=2), AX.X, ALU.max))
                        else:
                            mask = mask_of(t)
                            dve.tensor_tensor_reduce(sm[t % 2][:, 0:P], b[:, 0:P], mask[:, 0:P], 1.0, -3.0e38,
                                                     ALU.add, ALU.max, mx[:, 0:1])
                            give(dve.tensor_tensor_reduce(sm[t % 2][:, P : 3 * P], b[:, P : 3 * P], mask[:, P : 3 * P], 1.0,
                                                          -3.0e38, ALU.add, ALU.max, mx[:, 1:2]), ("s", l, t))
                            emptied(dve, ("s", l, t))
                        dve.tensor_scalar(NM[:, 2 * (t % 2) : 2 * (t % 2) + 2], mx, -SCALE[l], None, ALU.mult)\
                           .then_inc(S("max_ready"), 1)
                    if 1 <= t <= n:
                        u = t - 1
                        if both:
                            emptied(dve, ("s", l, u))
                        else:
                            dve.wait_ge(S("exp_ready"), 2 * (base + u + 1))
                        c = 2 * (u % 2)
                        link(dve.reciprocal(RI[:, c : c + 2], RS[:, c : c + 2]))
                        for qb, (a, w) in enumerate(((0, T), (T, T)) if both else ((0, P), (P, T))):
                            v = pr[u % 2][:, a : a + w]
                            ins = dve.tensor_scalar(v, v, RI[:, c + qb : c + qb + 1], None, ALU.mult)
                        ins.then_inc(S("weights_ready"), 1)
                    if t >= 3 and (t - 3) % 2:
                        mix_out(l, pair0 + (t - 3) // 2, dst)

            def layer(l):
                for j in range(8):
                    b = take(dve, ("v", l, j))
                    give(dve.tensor_copy(VT[:, j % 2, (j // 2) * 256 : (j // 2 + 1) * 256], b[:, 0:T]), ("v", l, j))
                for i, (m, g, rope) in enumerate(qk_pairs[l]):
                    emptied(dve, ("hssq", l, i))
                    link(dve.reciprocal(HSTD[i % 2], HSTD[i % 2]))
                    qk = QK[:, m : m + 2, :].rearrange("p a b -> p (a b)")
                    dve.scalar_tensor_tensor(out=qk, in0=qk, scalar=V(g), in1=HSTD[i % 2], op0=ALU.mult,
                                             op1=ALU.mult).then_inc(S("hn_ready"), 1)
                if l == 1:
                    b = take(dve, ("forget", 1))
                    dve.wait_ge(S("bf_loaded"), 16)
                    dve.wait_ge(S("fln_ready"), 1)
                    give(dve.tensor_scalar(FG[0:8, 1, :], b[0:8, 0:T], small[0:8, 40:41], 0.0, ALU.add, ALU.min), ("forget", 1))
                    emptied(dve, ("forget", 1))
                    link(dve.tensor_tensor(FG[0:8, 2, :], FG[0:8, 1, :], FG[0:8, 0, :], ALU.subtract))
                    link(dve.memset(FG[0:8, 1, :], 1.0))
                    link(dve.tensor_tensor_scan(FG[0:8, 3, :], FG[0:8, 1, :], FG[0:8, 2, :], 0.0, ALU.mult, ALU.add))
                    dve.tensor_scalar(FG[0:8, 0, :], FG[0:8, 3, :], 8.0, None, ALU.mult).then_inc(S("sums_ready"), 1)
                    dve.tensor_scalar(FG[0:8, 1, :], FG[0:8, 3, :], -8.0, None, ALU.mult).then_inc(S("sums_ready"), 1)
                roped = 4 * l
                for i, (m, g, rope) in enumerate(qk_pairs[l]):
                    if rope:
                        b = take(dve, ("rot", l, i))
                        qk = QK[:, m : m + 2, :]
                        table = lambda name: C(name, T).unsqueeze(1).broadcast_to([P, 2, T])
                        rot = ROT.rearrange("p (a b) -> p a b", a=2)
                        if roped:
                            dve.wait_ge(S("rope_ready"), roped)
                        roped += 1
                        give(dve.tensor_tensor(rot, b[:, 0:512].rearrange("p (a b) -> p a b", a=2), table("sin"), ALU.mult),
                             ("rot", l, i))
                        link(dve.tensor_tensor(qk, qk, table("cos"), ALU.mult))
                        emptied(dve, ("rot", l, i))
                        dve.tensor_tensor(qk, qk, rot, ALU.add).then_inc(S("rope_ready"), 1)
                if l == 0:
                    for t in range(8 + 4):
                        if t < 8:
                            dve.wait_ge(S("abs_ready"), t + 1)
                            z, r, zl = bank[4 + t % 2][:, 0:384], ZR[t % 2][:, 0:384], ZL[t % 2][:, 0:384]
                            link(dve.tensor_scalar(r, z, 0.0, 0.125, ALU.max, ALU.mult))
                            dve.wait_ge(S("ln_ready"), t + 1)
                            dve.tensor_tensor(zl, zl, r, ALU.add).then_inc(S("softplus_ready"), 1)
                        if t >= 3 and (t - 3) % 2:
                            mix_out(0, (t - 3) // 2, MIX)
                causal = lambda t: C("causal", 384)
                soft(l, 8 if l == 0 else 16, 4 if l == 0 else 0, False,
                     causal if l == 0 else lambda t: C("causal" if t < 8 else "dilated", 384), MIX)
                residual(("y", l))

            def second_in():
                residual_done(dve, 6)
                link(dve.memset(U0[:, :, 0:1], 0.0))
                link(dve.memset(U0[:, :, T + 1 : T + 2], 0.0))
                for g in range(3):
                    ms = slice(5 * g, 5 * g + 5)
                    for m in range(5 * g + 1, 5 * g + 5):
                        emptied(dve, ("u", m))
                    link(dve.tensor_tensor(US[:, ms, :], U0[:, ms, 0:T], U0[:, ms, 2 : T + 2], ALU.add))
                    link(dve.scalar_tensor_tensor(out=US[:, ms, :], in0=US[:, ms, :], scalar=0.5, in1=U0[:, ms, 1 : T + 1],
                                                  op0=ALU.mult, op1=ALU.subtract))
                    for m in range(5 * g, 5 * g + 5):
                        dve.scalar_tensor_tensor(out=US[:, m, :], in0=US[:, m, :], scalar=V("rw_mu_2", m),
                                                 in1=U0[:, m, 1 : T + 1], op0=ALU.mult, op1=ALU.add).then_inc(S("shifted"), 1)

            def latent():
                r = slice(64, 96)
                dve.wait_ge(S("pos_loaded"), 16)
                link(dve.tensor_copy(POSF[r, :], POS[r, :]))
                link(dve.tensor_scalar(POSF[r, :], POSF[r, :], C("inv", 1)[r, :], None, ALU.mult))
                whole, hi, lo = 12582912.0, 6.28125, 0.0019353071795864769
                for dst, quarter in ((ANG, 0.0), (ANG2, 0.25)):
                    link(dve.tensor_scalar(dst[r, :], POSF[r, :], 1.0 / (2 * np.pi), quarter, ALU.mult, ALU.add))
                    link(dve.tensor_scalar(dst[r, :], dst[r, :], whole, None, ALU.add))
                    link(dve.tensor_scalar(dst[r, :], dst[r, :], -whole, None, ALU.add))
                    link(dve.scalar_tensor_tensor(out=COSM[r, :], in0=dst[r, :], scalar=-hi, in1=POSF[r, :],
                                                  op0=ALU.mult, op1=ALU.add))
                    link(dve.scalar_tensor_tensor(out=dst[r, :], in0=dst[r, :], scalar=-lo, in1=COSM[r, :],
                                                  op0=ALU.mult, op1=ALU.add))
                    link(dve.tensor_scalar(dst[r, :], dst[r, :], quarter * 2 * np.pi, 3.1415925, ALU.add, ALU.min))
                    dve.tensor_scalar(dst[r, :], dst[r, :], -3.1415925, None, ALU.max).then_inc(S("angle_ready"), 1)
                for j in range(2):
                    emptied(dve, ("mssq", j))
                link(dve.reciprocal(TMPM[:, 3:5, :], TMPM[:, 3:5, :]))
                for dst, src, g, j in ((CQN[:, 0, :], CQ[:, 0, :], V("mla_g_qa_2", 0), 3), (CQN[:, 1, :], CQ[:, 1, :], V("mla_g_qa_2", 1), 3),
                                       (CKVN, CKV, V("mla_g_kva_2"), 4)):
                    dve.scalar_tensor_tensor(out=dst, in0=src, scalar=g, in1=TMPM[:, j, :], op0=ALU.mult,
                                             op1=ALU.mult).then_inc(S("cn_ready"), 1)
                for j in range(2):
                    b = take(dve, ("mv", j))
                    give(dve.tensor_copy(VM[:, j, :], b[:, 0:512]), ("mv", j))
                dve.wait_ge(S("trig_ready"), 2)
                dve.wait_ge(S("cn_ready"), 3)
                sin2 = SINM[r, :].unsqueeze(1).broadcast_to([32, 2, T])
                for j in range(4):
                    b = take(dve, ("mrot", j))
                    give(dve.tensor_tensor(TMPM[r, 2 * j : 2 * j + 2, :], b[r, 0:512].rearrange("p (a b) -> p a b", a=2), sin2, ALU.mult),
                         ("mrot", j))
                link(dve.tensor_tensor(QM[r, :, :], QM[r, :, :], COSM[r, :].unsqueeze(1).broadcast_to([32, 8, T]), ALU.mult))
                for j in range(2, 4):
                    emptied(dve, ("mrot", j))
                dve.tensor_tensor(QM[r, :, :], QM[r, :, :], TMPM[r, :, :], ALU.add).then_inc(S("mrope_ready"), 1)
                b = take(dve, ("mrot", 4))
                give(dve.tensor_tensor(POSF[r, :], b[r, 0:T], SINM[r, :], ALU.mult), ("mrot", 4))
                emptied(dve, ("u", 18))
                link(dve.tensor_tensor(KR[r, :], KR[r, :], COSM[r, :], ALU.mult))
                emptied(dve, ("mrot", 4))
                dve.tensor_tensor(KM[r, :, :], KR[r, :].unsqueeze(1).broadcast_to([32, 8, T]),
                                  POSF[r, :].unsqueeze(1).broadcast_to([32, 8, T]), ALU.add).then_inc(S("mrope_ready"), 1)
                soft(2, 8, 0, True, None, YM)

            def recurrence():
                flat = lambda v: v.rearrange("p a b -> p (a b)")
                for hp in range(4):
                    emptied(dve, ("lw", 1, hp))
                    emptied(dve, ("lw", 0, hp))
                link(dve.tensor_scalar(CE, CF, -DECAY, None, ALU.mult))
                for j in range(8):
                    for c in range(2):
                        ins = dve.tensor_tensor_scan(CF[:, j, c, :], C("ones", P), CE[:, j, c, :], 0.0, ALU.mult, ALU.add)
                link(ins)
                link(dve.tensor_tensor(CE, CF, CE, ALU.subtract))
                dve.tensor_copy(REF[:, 0:4, :], CF[:, 0:4, :, 63])
                link(dve.tensor_copy(REF[:, 4:8, :], CE[:, 4:8, :, 64]))
                for buf in (CF, CE):
                    ins = dve.tensor_tensor(buf, buf, REF.unsqueeze(3).broadcast_to([P, 8, 2, P]), ALU.subtract)
                link(ins)
                dve.tensor_tensor(SSC, CF[:, :, 0, P - 1], REF[:, :, 1], ALU.add).then_inc(S("decay_ready"), 1)
                for hp in range(4):
                    dve.tensor_scalar(KK[:, hp, :], US[:, 4 + hp, :], V("rw_k_k_2", hp), None, ALU.mult).then_inc(S("kk_ready"), 1)
                for j in range(2):
                    b = take(dve, ("kkss", j))
                    give(dve.tensor_scalar(flat(sq[:, 4 + 2 * j : 6 + 2 * j, :]), b[:, 0:512], 1e-24, None, ALU.max), ("kkss", j))
                dve.wait_ge(S("kkstd_ready"), 1)
                link(dve.reciprocal(sq[:, 4:8, :], sq[:, 4:8, :]))
                link(dve.tensor_tensor(KK, KK, sq[:, 4:8, :], ALU.mult))
                for hp in range(4):
                    emptied(dve, ("la", 0, hp))
                    emptied(dve, ("la", 1, hp))
                for j in range(8):
                    link(dve.tensor_scalar(KD[:, j, :], RATE[:, j, :], 1.0, V("rw_k_a_2", j % 4), ALU.subtract, ALU.mult))
                    ins = dve.scalar_tensor_tensor(out=KD[:, j, :], in0=KD[:, j, :], scalar=1.0, in1=US[:, 4 + j % 4, :],
                                                   op0=ALU.add, op1=ALU.mult)
                link(ins)
                dve.wait_ge(S("expd_ready"), 6)
                link(dve.tensor_tensor(KT.rearrange("p j c t -> p j (c t)"), BT.rearrange("p j c t -> p j (c t)"), KD, ALU.mult))
                for d in range(2):
                    js = slice(4 * d, 4 * d + 4)
                    kk4 = KK.rearrange("p h (c t) -> p h c t", c=2)
                    r4 = US[:, 0:4, :].rearrange("p h (c t) -> p h c t", c=2)
                    ins = dve.tensor_tensor(RATE[:, js, :], RATE[:, js, :], KK, ALU.mult)
                    dve.tensor_tensor(AR[:, js, :, 0, :], AR[:, js, :, 0, :], kk4, ALU.mult)
                    dve.tensor_tensor(AR[:, js, :, 1, :], AR[:, js, :, 1, :], r4, ALU.mult).then_inc(S("ar_ready"), 1)
                dve.wait_ge(S("ar_ready"), 2)
                bt = BT.rearrange("p j c t -> p (j c t)")
                dve.scalar_tensor_tensor(out=bt, in0=bt, scalar=-1.0, in1=RATE.rearrange("p j t -> p (j t)"),
                                         op0=ALU.mult, op1=ALU.mult).then_inc(S("bkt_ready"), 2)
                link(dve.tensor_tensor(US[:, 4:8, :], KD[:, 0:4, :], KD[:, 4:8, :], ALU.add))
                for hp in range(4):
                    dve.scalar_tensor_tensor(out=US[:, 4 + hp, :], in0=US[:, hp, :], scalar=V("rw_r_k_2", hp),
                                             in1=US[:, 4 + hp, :], op0=ALU.mult, op1=ALU.mult).then_inc(S("bonus_in_ready"), 1)
                for j in range(4):
                    b = take(dve, ("vtm", j))
                    give(dve.tensor_copy(VTM[:, j // 2, (j % 2) * T : (j % 2 + 1) * T], b[:, 0:T]), ("vtm", j))
                for j in range(8):
                    d, hp = j // 4, j % 4
                    b = take(dve, ("bkt", j))
                    dve.tensor_copy(BTM[:, d, hp * P : (hp + 1) * P], b[:, 0:P])
                    give(dve.tensor_copy(KTM[:, d, hp * P : (hp + 1) * P], b[:, P : 2 * P]), ("bkt", j))
                for j in range(2):
                    b = take(dve, ("bonus", j))
                    give(dve.tensor_tensor(flat(US[:, 2 * j : 2 * j + 2, :]), b[:, 0:512], flat(US[:, 8 + 2 * j : 10 + 2 * j, :]),
                                           ALU.mult), ("bonus", j))
                for j in range(2):
                    emptied(dve, ("bonus", j))
                link(dve.memset(ST, 0.0))
                dve.wait_ge(S("carry_ready"), 1)
                eye = ident.unsqueeze(1).broadcast_to([P, 2, P])
                for w, (d, c) in enumerate(WAVES):
                    seen = C("seen", 2 * P, 2 * P * d).rearrange("p (a b) -> p a b", a=2).unsqueeze(1).broadcast_to([P, 2, 2, P])
                    for u in range(4):
                        for e in range(2):
                            b = take(dve, ("gram", w, u, e))
                            give(dve.tensor_tensor(M4[u][:, e, :, :].rearrange("p (k a) t -> p k a t", k=2),
                                                   b[:, 0:512].rearrange("p (k a t) -> p k a t", k=2, a=2), seen, ALU.mult),
                                 ("gram", w, u, e))
                    for l in range(7):
                        for u in range(4):
                            if l == 0:
                                dve.wait_ge(S("level_ready"), 28 * w + u + 1)
                                dve.tensor_tensor(TNTT[u][:, 1, :, :], LV[u], eye, ALU.add)
                                b = take(dve, ("W", w, 0, u))
                                give(dve.tensor_tensor(TNTT[u][:, 0, :, :], b[:, 0:T].rearrange("p (a b) -> p a b", a=2), eye, ALU.add),
                                     ("W", w, 0, u))
                            else:
                                b = take(dve, ("TT", w, l, u))
                                half = TNTT[u].rearrange("p a e t -> p (a e t)")
                                lo = 0 if l < 6 else 2 * P
                                emptied(dve, ("TT", w, l - 1, u) if l > 1 else ("W", w, 0, u))
                                give(dve.tensor_tensor(half[:, lo:512], half[:, lo:512], b[:, lo:512], ALU.add), ("TT", w, l, u))
                    for u in range(4):
                        b = take(dve, ("O", w, u))
                        y = YR[:, u, c * P : (c + 1) * P]
                        if w < 2:
                            ins = dve.tensor_copy(y, b[:, 0:P])
                        else:
                            ins = dve.tensor_tensor(y, y, b[:, 0:P], ALU.add)
                        give(ins, ("O", w, u))
                    if w < 2:
                        for u in range(4):
                            j = 4 * d + u
                            b = take(dve, ("ST", w, u))
                            for e in range(2):
                                ps = slice(64 * e, 64 * e + 64)
                                ins = dve.tensor_scalar(ST[ps, j, ps], b[ps, 0:HD], SSC[ps, j : j + 1], None, ALU.mult)
                            give(ins, ("ST", w, u))
                for j in range(2):
                    b = take(dve, ("gmean", j))
                    ys = flat(YR[:, 2 * j : 2 * j + 2, :])
                    for u in range(4):
                        emptied(dve, ("O", 3, u))
                    give(dve.scalar_tensor_tensor(out=ys, in0=b[:, 0:512], scalar=-1.0 / HD, in1=ys, op0=ALU.mult, op1=ALU.add),
                         ("gmean", j))
                for j in range(2):
                    emptied(dve, ("gvar", j))
                link(dve.reciprocal(sq[:, 4:8, :], sq[:, 4:8, :]))
                link(dve.tensor_tensor(YR, YR, sq[:, 4:8, :], ALU.mult))
                for hp in range(4):
                    ins = dve.tensor_scalar(YR[:, hp, :], YR[:, hp, :], V("rw_gn_w_2", hp), V("rw_gn_b_2", hp), ALU.mult, ALU.add)
                link(ins)
                link(dve.tensor_tensor(YR, YR, US[:, 0:4, :], ALU.add))
                for hp in range(4):
                    emptied(dve, ("lg", hp))
                dve.tensor_tensor(YR, YR, G2, ALU.mult).then_inc(S("y_rw_ready"), 1)

            def branches_out():
                for m in range(8):
                    b = take(dve, ("br", 0, m))
                    give(dve.tensor_tensor(MG[:, m, :], GATES[:, m, :], b[:, 0:T], ALU.mult), ("br", 0, m))
                    b = take(dve, ("br", 1, m))
                    give(dve.tensor_tensor(MT[m % 2], GATES[:, 8 + m, :], b[:, 0:T], ALU.mult), ("br", 1, m))
                    emptied(dve, ("br", 1, m))
                    dve.tensor_tensor(MG[:, m, :], MG[:, m, :], MT[m % 2], ALU.add).then_inc(S("merged"), 1)
                residual(("y", 2))

            def best(tb):
                def top16(n, scores, scratch, vals, idx):
                    for r in range(2):
                        src = scores if r == 0 else scratch
                        lo = slice(8 * r, 8 * r + 8)
                        for j in range(n):
                            ins = dve.max(vals[:, j, lo], src[:, j, :])
                        link(ins)
                        for j in range(n):
                            ins = dve.max_index(idx[:, j, lo], vals[:, j, lo], src[:, j, :])
                            if r == 0:
                                ins = dve.match_replace(scratch[:, j, :], vals[:, j, lo], src[:, j, :], -3.0e38)
                        link(ins)

                top16(16, SC[:, tb, :, :], SCR, TV, TI)
                link(dve.tensor_copy(TIF, TI))
                tv = TV.rearrange("p (h c) k -> p h c k", c=2)
                ti = TIF.rearrange("p (h c) k -> p h c k", c=2)
                link(dve.tensor_tensor(CAND.rearrange("p h (a b) -> p h a b", a=16),
                                       tv[:, :, 0, :].unsqueeze(3).broadcast_to([P, 8, 16, 16]),
                                       tv[:, :, 1, :].unsqueeze(2).broadcast_to([P, 8, 16, 16]), ALU.add))
                top16(8, CAND, CSCR, BV, BP)
                bp = BP.rearrange("p h e -> p (h e)")
                count = C("count", 16).unsqueeze(1).broadcast_to([P, P, 16])
                for half, (op, n, dst) in enumerate(((ALU.logical_shift_right, 4, E0), (ALU.bitwise_and, 15, E1))):
                    link(dve.tensor_scalar(BI, bp, n, None, op))
                    link(dve.tensor_copy(BF, BI))
                    link(dve.tensor_tensor(EQ, BF.unsqueeze(2).broadcast_to([P, P, 16]), count, ALU.is_equal))
                    eq4 = EQ.rearrange("p (h e) i -> p h e i", h=8)
                    link(dve.tensor_tensor(eq4, eq4, ti[:, :, half, :].unsqueeze(2).broadcast_to([P, 8, 16, 16]), ALU.mult))
                    link(dve.tensor_reduce(dst, EQ, AX.X, ALU.add))
                link(dve.scalar_tensor_tensor(out=E0, in0=E0, scalar=float(N_KEYS), in1=E1, op0=ALU.mult, op1=ALU.add))
                dve.tensor_scalar(EIDX[:, tb, :], E0, float(N_KEYS * N_KEYS - 1), None, ALU.min).then_inc(S("rows_known"), 1)
                dve.tensor_tensor(PEX, BV, BV[:, :, 0:1].broadcast_to([P, 8, 16]), ALU.subtract).then_inc(S("gate_in_ready"), 1)
                dve.wait_ge(S("gate_exp_ready"), tb + 1)
                link(dve.tensor_reduce(SUM8[:, 0:8], PEX, AX.X, ALU.add))
                link(dve.reciprocal(SUM8[:, 8:16], SUM8[:, 0:8]))
                link(dve.tensor_tensor(GATE[:, tb, :].rearrange("p (h e) -> p h e", h=8), PEX,
                                       SUM8[:, 8:16].unsqueeze(2).broadcast_to([P, 8, 16]), ALU.mult))

            def experts():
                for j in range(4, 8):
                    emptied(dve, ("sc", j))
                best(0)
                best(1)
                dve.sem_inc(S("rows_used"), 8)
                for j in range(4):
                    emptied(dve, ("htok", j))
                used = S("rows_used")
                for tb in range(2):
                    q = tb
                    with dve.Fori(0, 16) as i:
                        for j in range(8):
                            dve.wait_ge(S(f"row{j}_loaded"), 16 * (16 * q + 1) + 16 * i)
                            if j >= 2:
                                dve.wait_ge(used, 8 * (16 * q + 1) + j - 1 + 8 * i)
                            dve.tensor_tensor_reduce(JUNK[j % 2], GR[:, j, :], HTOK[:, tb, :], 1.0, 0.0, ALU.mult, ALU.add,
                                                     DSTAGE[:, j : j + 1]).then_inc(used, 1)
                        dve.wait_ge(used, 8 * (16 * q + 2) + 8 * i)
                        dve.tensor_copy(DOTS[:, tb, bass.ds(i * 8, 8)], DSTAGE).then_inc(S("dots_ready"), 1)
                        dve.wait_ge(S("dots_ready"), 16 * tb + 1 + i)
                link(dve.memset(ACC, 0.0))
                for tb in range(2):
                    q = 2 + tb
                    dve.wait_ge(S("gelu_ready"), tb + 1)
                    link(dve.tensor_tensor(WT[:, tb, :], WT[:, tb, :], GATE[:, tb, :], ALU.mult))
                    with dve.Fori(0, 16) as i:
                        dve.wait_ge(used, 8 * (16 * q + 1) + 8 * i)
                        dve.tensor_copy(WSTAGE, WT[:, tb, bass.ds(i * 8, 8)]).then_inc(S("wstage"), 1)
                        dve.wait_ge(S("wstage"), 16 * tb + 1 + i)
                        for j in range(8):
                            dve.wait_ge(S(f"row{j}_loaded"), 16 * (16 * q + 1) + 16 * i)
                            if j:
                                dve.wait_ge(used, 8 * (16 * q + 1) + j + 8 * i)
                            dve.scalar_tensor_tensor(out=ACC[:, tb, :], in0=GR[:, j, :], scalar=WSTAGE[:, j : j + 1],
                                                     in1=ACC[:, tb, :], op0=ALU.mult, op1=ALU.add).then_inc(used, 1)
                residual(("back",))

            def ple():
                for m in range(8):
                    b = take(dve, ("pp", m))
                    emptied(dve, ("pg", m))
                    s = view(4096 + T * m, T)
                    give(dve.tensor_tensor(s, s, b[:, 0:T], ALU.mult), ("pp", m))
                    emptied(dve, ("pp", m))
                    ins = dve.tensor_tensor(xT[:, m, :], xT[:, m, :], s, ALU.add)
                ins.then_inc(x_ready, 1)

            for l in range(2):
                norm(3 * l)
                ffn(2 * l)
                norm(3 * l + 1)
                layer(l)
                norm(3 * l + 2)
                ffn(2 * l + 1)
            norm(6)
            second_in()
            latent()
            recurrence()
            branches_out()
            norm(7)
            experts()
            norm(8)
            ple()
            norm(9)

        @block.gpsimd
        def _(pool):
            chain = Chain(pool_done)
            link = lambda ins: chain.link(pool, ins)

            def keep_before(buf, sem_):
                for a in (0, T):
                    v = buf[:, a : a + P]
                    pool.affine_select(out=v, in_=v, pattern=[[1, P]], compare_op=ALU.is_gt, fill=0.0, base=0,
                                       channel_multiplier=-1).then_inc(sem_, 1)

            for t in range(8 + 1):
                if t < 8:
                    pool.wait_ge(S("softplus_ready"), t + 1)
                    keep_before(ZL[t % 2], S("keep_ready"))
                if t >= 1:
                    emptied(pool, ("z", 0, t - 1))
                    keep_before(PT[(t - 1) % 2], S("stick_ready"))
            link(pool.memset(FL[0:2, :, :], 1.0))
            link(pool.memset(FR[0:2, :, :], 1.0))
            pool.wait_ge(S("sums_ready"), 2)
            pool.dma_start(FL[0:1, :, :], FG[0:8, 0, :]).then_inc(S("forget_ready"), 16)
            pool.dma_start(FR[1:2, :, :], FG[0:8, 1, :]).then_inc(S("forget_ready"), 16)
            residual_done(pool, 6)
            pool.dma_start(POS[64:96, :], A["positions"].partition_broadcast(32)).then_inc(S("pos_loaded"), 16)
            for w, (d, c) in enumerate(WAVES):
                for l in range(7):
                    for u in range(4):
                        if l == 0:
                            emptied(pool, ("gram", w, u, 0))
                            emptied(pool, ("gram", w, u, 1))
                        else:
                            b, n = fill_of["W", w, l - 1, u]
                            pool.wait_ge(full[b], n)
                            if l == 1:
                                emptied(pool, ("W", w, 0, u))
                        mask = C("level", P, (7 * d + l) * P).unsqueeze(1).broadcast_to([P, 2, P])
                        pool.tensor_tensor(LV[u], M4[u][:, :, 0, :], mask, ALU.mult).then_inc(S("level_ready"), 1)
            used = S("rows_used")
            pool.wait_ge(used, 8)
            free_rows = pool.alloc_register("free_rows")
            pool.reg_mov(free_rows, 1)
            for q, table in enumerate(("peer_u_2", "peer_u_2", "peer_v_2", "peer_v_2")):
                tb = q % 2
                with pool.Fori(0, 8) as i:
                    for half in range(2):
                        stage = STAGE[:, 8 * half : 8 * half + 8]
                        row_free = pool.snap(free_rows)
                        pool.tensor_copy(stage, EIDX[:, tb, bass.ds(i * 16 + 8 * half, 8)]).then_inc(S("staged"), 1)
                        pool.wait_ge(S("staged"), 16 * q + half + 1 + 2 * i)
                        for j in range(8):
                            if j:
                                row_free = pool.snap(free_rows)
                            pool.wait_ge(used, row_free)
                            pool.reg_add(free_rows, free_rows, 1)
                            pool.indirect_dma_start(out=GR[:, j, :], out_offset=None, in_=A[table][0],
                                                    in_offset=bass.IndirectOffsetOnAxis(ap=stage[:, j : j + 1], axis=0))\
                                .then_inc(S(f"row{j}_loaded"), 16)
            pool.wait_ge(xn_ready, 10 * KC)
            pool.dma_start(rows(out), xn[:, :, :]).then_inc(S("stored"), 16)
            pool.wait_ge(S("stored"), 16)


def kernel(**inputs):
    import concourse.bacc as bacc
    from concourse.bass_utils import run_bass_kernel_spmd

    arrays = {}
    take = lambda name: np.ascontiguousarray(np.asarray(inputs[name]))
    arrays["xT"] = np.ascontiguousarray(take("x")[0].T)
    arrays["pT"] = np.ascontiguousarray(take("p_2")[0, 0].T)
    arrays["positions"] = take("positions_2")[0]
    keys = take("peer_sub_keys_2")[0].reshape(16, N_KEYS, P)
    arrays["sub_keys_t"] = np.ascontiguousarray(keys.transpose(0, 2, 1))
    arrays["con"] = constants()
    arrays["vec"] = pack_vectors(inputs)
    for name in ("ffn1_w_gate", "ffn1_w_up", "ffn1_w_down", "ffn2_w_gate", "ffn2_w_up", "ffn2_w_down", "w_in_ab",
                 "w_in_cd", "b_f", "w_out", "w_in_2", "rw_w2_2", "rw_a2_2", "rw_g2_2", "mla_w_qup_2", "mla_w_kvup_2",
                 "w_br_rwkv_2", "w_br_mla_2", "w_out_2", "peer_w_q_2", "peer_u_2", "peer_v_2", "w_ple_gate_2",
                 "w_ple_proj_2"):
        arrays[name] = take(name)

    nc = bacc.Bacc("TRN2", target_bir_lowering=False, num_devices=1)
    aps = {
        name: nc.dram_tensor(name, a.shape, mybir.dt.from_np(a.dtype), kind="ExternalInput").ap()
        for name, a in arrays.items()
    }
    out = nc.dram_tensor("out", (D, T), F32, kind="ExternalOutput").ap()
    build(nc, aps, out)
    r = run_bass_kernel_spmd(nc, [arrays], core_ids=[0])
    return np.ascontiguousarray(r.results[0]["out"].T)[None]
```

```python
from contextlib import ExitStack

import concourse.bass as bass
import numpy as np
from concourse import mybir

F32 = mybir.dt.float32
U32 = mybir.dt.uint32
F32R = mybir.dt.float32r
I32 = mybir.dt.int32
ACT = mybir.ActivationFunctionType
ALU = mybir.AluOpType
AX = mybir.AxisListType

P = 128
T = 256
D = 1024
KC = D // P
HD = 64
DFF = 2816
GROUPS = DFF // 256
CHUNKS = DFF // P
EPS = 1e-6
RW_COLS, MLA_COLS = 1920, 416
N_KEYS, TOPK, PH = 128, 16, 8
NEG = -1.0e30
DECAY = float(np.exp(-0.5))
GN_EPS = 64e-5

VEC = {}
_n = 0
for _name, _w in (
    ("norm_ffn1", 16), ("norm_mix", 16), ("norm_ffn2", 16), ("g_mix_2", 8), ("g_ffn_2", 8), ("g_ple_2", 8),
    ("g_final_2", 8), ("rw_mu_2", 15), ("rw_w0_2", 8), ("rw_a0_2", 8), ("rw_k_k_2", 4), ("rw_k_a_2", 4),
    ("rw_r_k_2", 4), ("rw_gn_w_2", 4), ("rw_gn_b_2", 4), ("mla_g_qa_2", 2), ("mla_g_kva_2", 1),
    ("g_q_b", 1), ("g_k_b", 1), ("g_q_c", 1), ("g_k_c", 1), ("g_q_d", 1), ("g_k_d", 1),
):
    VEC[_name] = _n
    _n += _w
NVEC = _n

CON = {}
_n = 0
for _name, _w in (
    ("ones", 128), ("eps", 4), ("ident", 128), ("heads", 128), ("suffix", 128), ("after", 128), ("causal", 384),
    ("dilated", 384), ("cos", 256), ("sin", 256), ("turn", 128), ("turn_mla", 32), ("seen", 512),
    ("level", 2 * 7 * 128), ("inv", 1), ("count", 16), ("one", 1),
):
    CON[_name] = _n
    _n += _w
NCON = _n
NFIRST = CON["ident"]


def constants():
    c = np.zeros((P, NCON), np.float32)

    def put(name, value):
        value = np.asarray(value, np.float32)
        c[: value.shape[0], CON[name] : CON[name] + value.shape[1]] = value

    i = np.arange(P)
    row, col = i[:, None], i[None, :]
    put("ident", row == col)
    put("ones", np.ones((P, P)))
    put("heads", (row // HD) == (col // HD))
    put("suffix", -8.0 * (row >= col))
    put("after", -8.0 * np.ones((P, P)))
    tri = np.where(col <= row, 0.0, NEG)
    put("causal", np.concatenate([tri, np.zeros((P, P)), tri], 1))

    def branches(dist):
        n = ((dist >= 0) & (dist <= 128)).astype(int) + ((dist >= 0) & (dist % 4 == 0)) + ((dist >= 0) & (dist % 16 == 0))
        return np.where(n > 0, 8.0 * np.log(np.maximum(n, 1)), NEG)

    put("dilated", np.concatenate([branches(row - col), branches(128 + row - col), branches(row - col)], 1))
    inv = (1.0 / (np.float32(10000.0) ** (np.arange(0, HD, 2, dtype=np.float32) / np.float32(HD)))).astype(np.float32)
    ang = (np.arange(T, dtype=np.float32)[:, None] * inv[None, :]).astype(np.float32).astype(np.float64)
    put("cos", np.tile(np.cos(ang).T, (4, 1)))
    put("sin", np.tile(np.sin(ang).T, (4, 1)))
    turn = np.zeros((P, P))
    for h in (0, HD):
        for j in range(32):
            turn[h + 32 + j, h + j] = -1.0
            turn[h + j, h + 32 + j] = 1.0
    put("turn", turn)
    turn = np.zeros((P, 32))
    for j in range(16):
        turn[64 + 16 + j, j] = -1.0
        turn[64 + j, 16 + j] = 1.0
    put("turn_mla", turn)
    put("seen", np.concatenate([row < col, row <= col, row > col, row >= col], 1))
    level = np.zeros((P, 2, 7, P))
    for l in range(7):
        n = 1 << l
        same = (row // (2 * n)) == (col // (2 * n))
        level[:, 0, l] = same & (row // n < col // n)
        level[:, 1, l] = same & (row // n > col // n)
    put("level", level.reshape(P, -1))
    inv2 = (np.float32(10000.0) ** (-np.arange(0, 32, 2, dtype=np.float32) / np.float32(32))).astype(np.float32)
    v = np.zeros((P, 1))
    v[64:96, 0] = np.tile(inv2, 2)
    put("inv", v)
    put("eps", np.tile(np.array([[EPS, GN_EPS, 1e-24, 0.0]]), (P, 1)))
    put("count", np.tile(np.arange(16)[None, :], (P, 1)))
    put("one", np.ones((P, 1)))
    return c


def pack_vectors(inputs):
    v = np.zeros((P, NVEC), np.float32)
    for name, at in VEC.items():
        a = np.asarray(inputs[name])
        if name.startswith("g_") and a.size == HD:
            v[:HD, at : at + 1] = a.reshape(HD, 1)
            v[HD:, at : at + 1] = a.reshape(HD, 1)
        else:
            w = a.size // P
            v[:, at : at + w] = a.reshape(w, P).T
    return v


def build(nc, A, out):
    ctx = ExitStack()
    with ctx:
        sb = lambda name, shape, dt=F32: ctx.enter_context(nc.sbuf_tensor(name + "_sb", shape, dt))
        sem = lambda name: ctx.enter_context(nc.semaphore(name))

        xT = sb("xT", [P, KC, T])
        xn_at = nc.sbuf_base
        xn = sb("xn", [P, KC, T])
        sq_at = nc.sbuf_base
        sq = sb("sq", [P, KC, T])
        RING = 6
        ring = sb("ring", [P, RING, 2048])
        con = sb("con", [P, NCON])
        vec = sb("vec", [P, NVEC])
        rstd = sb("rstd", [P, T])
        std = sb("std", [P, T])
        sgate = sb("sgate", [P, 2, T])
        hT = sb("hT", [P, 2, T])
        small = sb("small", [P, 256])
        ARENA = 28416
        arena_at = nc.sbuf_base
        arena = sb("arena", [P, ARENA])
        bank = [ctx.enter_context(nc.psum_tensor(f"bank{b}", [P, 512], F32)) for b in range(8)]

        def view(at, *shape, dt=None):
            n = int(np.prod(shape))
            assert at + n <= ARENA
            v = arena[:, at : at + n]
            if dt is not None:
                v = v.bitcast(dt)
            names = "abcde"[: len(shape)]
            if len(shape) == 1:
                return v
            return v.rearrange(f"p ({' '.join(names)}) -> p {' '.join(names)}", **{n_: s for n_, s in zip(names[1:], shape[1:])})

        C = lambda name, w, off=0: con[:, CON[name] + off : CON[name] + off + w]
        V = lambda name, c=0: vec[:, VEC[name] + c : VEC[name] + c + 1]
        ident = C("ident", P)
        eps = lambda j: C("eps", 1, j)

        loaded_x, loaded_c, loaded_v = sem("loaded_x"), sem("loaded_c"), sem("loaded_v")
        slot_loaded = [sem(f"slot{i}_loaded") for i in range(RING)]
        slot_free = sem("slot_free")
        sq_ready, ssq_ready, std_ready, xn_ready = sem("sq_ready"), sem("ssq_ready"), sem("std_ready"), sem("xn_ready")
        x_ready, y_ready = sem("x_ready"), sem("y_ready")
        gu_ready, silu_ready, h_ready = sem("gu_ready"), sem("silu_ready"), sem("h_ready")
        full = [sem(f"bank{b}_full") for b in range(8)]
        free = [sem(f"bank{b}_free") for b in range(8)]
        dve_done, act_done, pool_done = sem("dve_done"), sem("act_done"), sem("pool_done")
        named = {}

        def S(name):
            if name not in named:
                named[name] = sem(name)
            return named[name]

        SCALE = {0: 0.125, 1: 0.125, 2: 96.0 ** -0.5}

        fast = lambda name, shape, at_: nc.alloc_sbuf_tensor_at(name + "_sb", shape, F32R, offset=at_)
        hi_ready, split_ready, pair_used = sem("hi_ready"), sem("split_ready"), sem("pair_used")
        xh_ready, hraw_ready, hh_ready = sem("xh_ready"), sem("hraw_ready"), sem("hh_ready")
        xh = fast("xh", [P, KC, T], xn_at)
        xl = fast("xl", [P, KC, T], sq_at)
        PAIR = {("gate", 0): 8192, ("up", 0): 12288, ("gate", 1): 0, ("up", 1): 4096, ("down", 0): 16384, ("down", 1): 16384}
        parts = fast("parts", [P, 5 * 4096], arena_at)
        whi = lambda kind, g: parts[:, PAIR[kind, g % 2] : PAIR[kind, g % 2] + 2048]
        wlo = lambda kind, g: parts[:, PAIR[kind, g % 2] + 2048 : PAIR[kind, g % 2] + 4096]
        HH = fast("h_high", [P, 2, T], arena_at + 4 * 20480)
        HL = fast("h_low", [P, 2, T], arena_at + 4 * 20992)
        FFN_SLOTS = 3 * GROUPS

        def splits_after(c):
            g = c // 2
            return [("down", g)] if c % 2 == 0 else [("gate", g + 2), ("up", g + 2)] if g + 2 < GROUPS else []

        def place(kind, g):
            if kind == "down":
                return 3 * g + 4 if g < GROUPS - 1 else FFN_SLOTS - 1
            return (max(3 * g - 1, 0)) + (kind == "up")

        fill_of, fills = {}, [0] * 8

        def plan(label, b):
            fills[b] += 1
            assert label not in fill_of, label
            fill_of[label] = (b, fills[b])

        def fill_begin(pe, label):
            b, n = fill_of[label]
            if n > 1:
                pe.wait_ge(free[b], n - 1)
            return bank[b]

        def fill_end(ins, label):
            ins.then_inc(full[fill_of[label][0]], 1)

        def take(eng, label):
            b, n = fill_of[label]
            eng.wait_ge(full[b], n)
            return bank[b]

        def give(ins, label):
            ins.then_inc(free[fill_of[label][0]], 1)

        def emptied(eng, label):
            b, n = fill_of[label]
            eng.wait_ge(free[b], n)

        class Chain:

            def __init__(self, s):
                self.s, self.n = s, 0

            def link(self, eng, ins):
                ins.then_inc(self.s, 1)
                self.n += 1
                eng.wait_ge(self.s, self.n)

        at = {}
        k = 0
        for l in range(2):
            at["ffn", 2 * l] = k; k += 3 * GROUPS
            at["qkv", l] = k; k += 12
            at["wo", l] = k; k += 4
            at["ffn", 2 * l + 1] = k; k += 3 * GROUPS
        at["in2"] = k; k += 10
        at["mla"] = k; k += 2
        at["gates"] = k; k += 8
        at["br"] = k; k += 4
        at["wo", 2] = k; k += 4
        at["wq"] = k; k += 8
        at["pg"] = k; k += 4
        at["pp"] = k; k += 1
        ffn_at = [at["ffn", f] for f in range(4)]

        def freed(k):
            before = sum(min(max(k - a, 0), FFN_SLOTS) for a in ffn_at)
            if any(a <= k < a + FFN_SLOTS for a in ffn_at):
                return split_ready, before + 1
            return slot_free, k - before + 1

        slot = lambda k, *shape: ring[:, k % RING, 0 : int(np.prod(shape))].rearrange("p (k n) -> p k n", k=shape[0])

        ffn_w = [
            (A["ffn1_w_gate"][0], A["ffn1_w_up"][0], A["ffn1_w_down"][0]),
            (A["ffn2_w_gate"][0], A["ffn2_w_up"][0], A["ffn2_w_down"][0]),
            (A["ffn1_w_gate"][1], A["ffn1_w_up"][1], A["ffn1_w_down"][1]),
            (A["ffn2_w_gate"][1], A["ffn2_w_up"][1], A["ffn2_w_down"][1]),
        ]
        norm_g = [("norm_ffn1", 0), ("norm_mix", 0), ("norm_ffn2", 0), ("norm_ffn1", 8), ("norm_mix", 8),
                  ("norm_ffn2", 8), ("g_mix_2", 0), ("g_ffn_2", 0), ("g_ple_2", 0), ("g_final_2", 0)]
        rows = lambda w: w.rearrange("(k p) n -> p k n", p=P)

        QK = view(0, 16, T)
        VT = view(4096, 2, D)
        MIX = view(6144, KC, T)
        SM = [view(8192 + 512 * j, 512) for j in range(2)]
        PR = [view(a, 512) for a in (9216, 9728, 15872)]
        PT = [view(10240 + 512 * j, 512) for j in range(2)]
        ZR = [view(11264 + 512 * j, 512) for j in range(2)]
        ZL = [view(12288 + 512 * j, 512) for j in range(2)]
        HSQ = [view(13312 + 512 * j, 512) for j in range(2)]
        HSTD = [view(14336 + 512 * j, 512) for j in range(2)]
        ROT = view(15360, 512)
        WF = view(ARENA - KC * 8, KC, 8)
        FG = view(16448, 4, T)
        FL = view(17472, 8, T)
        FR = view(19520, 8, T)
        MX, NM, RS, RI = (small[:, 128 + 6 * j : 134 + 6 * j] for j in range(4))

        unit_base = {0: 0, 1: 8, 2: 24}
        N_SOFT = {0: 8, 1: 16, 2: 8}

        qk_pairs = {
            0: [(4, "g_q_b", 1), (6, "g_q_b", 1), (12, "g_k_b", 1), (14, "g_k_b", 1)],
            1: [(0, "g_q_c", 0), (2, "g_q_c", 0), (8, "g_k_c", 0), (10, "g_k_c", 0),
                (4, "g_q_d", 1), (6, "g_q_d", 1), (12, "g_k_d", 1), (14, "g_k_d", 1)],
        }

        def with_values(l, j):
            n = len(qk_pairs[l]) // 4
            return range(n * (j // 2), n * (j // 2 + 1)) if j % 2 else ()

        def plan_norm(n):
            plan(("ssq", n), 7)

        def plan_layer(l):
            for m in range(16):
                plan(("qk", l, m), 4 + m % 3)
            for j in range(8):
                plan(("v", l, j), 4 + (16 + j) % 3)
                for i in with_values(l, j):
                    plan(("hssq", l, i), i % 2)
            if l == 1:
                plan(("forget", l), 7)
            for i, (m, g, rope) in enumerate(qk_pairs[l]):
                if rope:
                    plan(("rot", l, i), 6 + i % 2)
            if l == 0:
                for t in range(8 + 2):
                    if t < 8:
                        plan(("z", l, t), 4 + t % 2)
                    if t >= 2 and t % 2 == 0:
                        plan(("o", l, (t - 2) // 2), (t - 2) // 2 % 4)
                plan_soft(l, 8, 4)
            else:
                plan_soft(l, 16, 0)
            for m in range(4):
                plan(("y", l, m), m)

        def plan_soft(l, n, pair0):
            for t in range(n + 3):
                if t < n:
                    plan(("s", l, t), 4 + t % 2)
                if 2 <= t < n + 2:
                    plan(("pt", l, t - 2), 6 + t % 2)
                if t >= 3 and t % 2:
                    plan(("o", l, pair0 + (t - 3) // 2), (pair0 + (t - 3) // 2) % 4)

        US = view(0, 15, T)
        GATES = view(3840, 16, T)
        YM = view(7936, 4, T)
        YR = view(8960, 4, T)
        U0 = view(9984, 15, T + 2)
        CQ = view(13856, 2, T)
        CKV = view(14368, T)
        KR = view(14624, T)
        CQN = view(14880, 2, T)
        CKVN = view(15392, T)
        QM = view(15648, 8, T)
        KM = view(17696, 8, T)
        VM = view(19744, 2, 512)
        COSM = view(20768, T)
        SINM = view(21024, T)
        PR2 = [view(21280 + 512 * j, 512) for j in range(3)]
        PT2 = [view(23328 + 512 * j, 512) for j in range(2)]
        TMPM = view(24352, 8, T)
        ANG = view(26400, T)
        ANG2 = view(26656, T)
        POS = view(26912, T, dt=I32)
        POSF = view(27168, T)
        AR = view(9984, 8, 2, 2, P)
        BT = view(14080, 8, 2, P)
        KT = view(16128, 8, 2, P)
        CF = view(18176, 8, 2, P)
        CE = view(20224, 8, 2, P)
        RATE = view(22272, 8, T)
        KD = view(24320, 8, T)
        KK = view(26368, 4, T)
        G2 = [sgate, hT]
        VTM = view(27392, 2, 512)
        BTM = sq[:, 0:4, :].rearrange("p a b -> p (a b)").rearrange("p (d n) -> p d n", d=2)
        KTM = sq[:, 4:8, :].rearrange("p a b -> p (a b)").rearrange("p (d n) -> p d n", d=2)
        UNIT = 18176
        M4 = [view(UNIT + 2048 * u, 2, 4, P) for u in range(4)]
        LV = [view(UNIT + 2048 * u + 1024, 2, P) for u in range(4)]
        WW = [view(UNIT + 2048 * u + 1280, 2, P) for u in range(4)]
        TNTT = [view(UNIT + 2048 * u + 1536, 2, 2, P) for u in range(4)]
        SSC = small[:, 16:24]
        REF = small[:, 24:40].rearrange("p (a c) -> p a c", c=2)
        XX = [view(26368 + 128 * u, P) for u in range(4)]
        UU = [view(26880 + 128 * u, P) for u in range(4)]
        ST = view(1024, 8, P)
        LORA = [view(8960, 512), view(9472, 512), view(27648, 512)]
        MG = view(9984, 8, T)
        MT = [view(12032 + 256 * j, T) for j in range(2)]
        WAVES = [(0, 0), (1, 1), (0, 1), (1, 0)]

        HTOK = view(0, 2, D)
        ACC = view(2048, 2, D)
        QP = view(4096, 16, T)
        SC = view(8192, 2, 16, P)
        GB = 8
        GR = view(4096, GB, D)
        SCR = view(12288, 2, 2, P)
        TV = view(12800, 2, 16, 16)
        TI = view(13312, 2, 16, 16, dt=U32)
        TIF = view(13824, 2, 16, 16)
        CAND = view(15104, 8, 256)
        CSCR = view(17152, 8, 256)
        BV = view(19200, 8, 16)
        BP = view(19328, 8, 16, dt=U32)
        BI = view(19456, P, dt=U32)
        BF = view(19584, P)
        EQ = view(19712, P, 16)
        E0 = view(21760, P)
        E1 = view(21888, P)
        EIDX = view(22016, 2, P, dt=U32)
        GATE = view(22272, 2, P)
        DOTS = view(22528, 2, P)
        WT = view(22784, 2, P)
        PEX = view(23040, 8, 16)
        STAGE = sb("stage", [P, 16], U32)
        DSTAGE = small[:, 80:88]
        WSTAGE = small[:, 96:104]
        SUM8 = small[:, 112:128]
        JUNK = [view(23168 + D * j, D) for j in range(2)]
        PIN = view(25216, 2, T)
        KEYS = view(25728, 16, P)

        plan_norm(0)
        plan_norm(1)
        plan_layer(0)
        plan_norm(2)
        plan_norm(3)
        plan_norm(4)
        plan_layer(1)
        plan_norm(5)
        plan_norm(6)
        for m in range(19):
            plan(("u", m), m % 4)
        plan(("mssq", 0), 4)
        plan(("mssq", 1), 5)
        for h in range(8):
            plan(("mq", h), h % 4)
        for h in range(8):
            plan(("mk", h), h % 4)
        for j in range(2):
            plan(("mv", j), 4 + j)
        for m in range(0, 2):
            plan(("gate", m), m % 4)
        for j in range(5):
            plan(("mrot", j), 6 + j % 2)
        for m in range(2, 6):
            plan(("gate", m), m % 4)
        plan_soft(2, 8, 0)
        for d in range(2):
            for hp in range(4):
                plan(("lw", d, hp), 0 + hp % 4)
                plan(("la", d, hp), 4 + hp % 2)
        for hp in range(4):
            plan(("lg", hp), 6 + hp % 2)
        for m in range(6, 8):
            plan(("gate", m), 6 + m % 2)
        for j in range(2):
            plan(("kkss", j), 4 + j)
        for j in range(4):
            plan(("vtm", j), 0 + j)
        for m in range(8, 16):
            plan(("gate", m), 6 + m % 2)
        for j in range(8):
            plan(("bkt", j), 4 + j % 4)
        for j in range(2):
            plan(("bonus", j), j)
        for w in range(4):
            for u in range(4):
                for e in range(2):
                    plan(("gram", w, u, e), 4 * e + u)
            for l in range(7):
                for u in range(4):
                    plan(("W", w, l, u), u)
                if l:
                    for u in range(4):
                        plan(("TT", w, l, u), 4 + u)
            for u in range(4):
                plan(("X", w, u), u)
            for u in range(4):
                plan(("U", w, u), 4 + u)
            for u in range(4):
                plan(("O", w, u), u)
            if w < 2:
                for u in range(4):
                    plan(("ST", w, u), 4 + u)
        for j in range(2):
            plan(("gmean", j), j)
        for j in range(2):
            plan(("gvar", j), 2 + j)
        for m in range(8):
            plan(("br", 0, m), m % 4)
            plan(("br", 1, m), 4 + m % 4)
        for m in range(4):
            plan(("y", 2, m), m)
        plan_norm(7)
        for h in range(8 + 1):
            if h < 8:
                plan(("pq", 2 * h), 2 * h % 4)
                plan(("pq", 2 * h + 1), (2 * h + 1) % 4)
            if h:
                plan(("sc", h - 1), 4 + (h - 1) % 2)
        for j in range(4):
            plan(("htok", j), 6 + j % 2)
        for j in range(4):
            plan(("back", j), 4 + j)
        plan_norm(8)
        for m in range(8):
            plan(("pg", m), m % 4)
            plan(("pp", m), 4 + m % 3)
        plan_norm(9)

        def residual_done(eng, n, pairs=range(4)):
            for m in pairs:
                if n in (1, 3, 4, 6, 9):
                    eng.wait_ge(x_ready, 4 * {1: 0, 3: 1, 4: 2, 6: 3, 9: 4}[n] + m + 1)
                elif n:
                    emptied(eng, {2: ("y", 0, m), 5: ("y", 1, m), 7: ("y", 2, m), 8: ("back", m)}[n])

        block = ctx.enter_context(nc.Block())

        @block.sync
        def _(sp):
            def fetch(k, dst, src, i=0, wait=True):
                if wait and k >= RING:
                    who, n = freed(k - RING)
                    sp.wait_ge(who, n + RING * i)
                sp.dma_start(dst, src).then_inc(slot_loaded[k % RING], 16)

            def ffn(f):
                gate, up, down = ffn_w[f]

                def part(kind, g, i=0):
                    k = at["ffn", f] + place(kind, g)
                    n0 = i * 512 + g * 256
                    if kind == "down":
                        fetch(k, slot(k, 2, D), down[bass.ds(n0, 256), :].rearrange("(k p) n -> p k n", p=P), i)
                    else:
                        fetch(k, slot(k, KC, 256), rows(gate if kind == "gate" else up)[:, :, bass.ds(n0, 256)], i)

                def triple(g, i=0):
                    part("gate", g, i)
                    part("up", g, i)
                    part("down", g - 1, i)

                for g in range(2):
                    part("gate", g)
                    part("up", g)
                part("down", 0)
                triple(2)
                with sp.Fori(0, (GROUPS - 3) // 2) as i:
                    triple(3, i)
                    triple(4, i)
                part("down", GROUPS - 1)

            def square(k0, w, n):
                for s in range(n):
                    fetch(k0 + s, slot(k0 + s, KC, 256), rows(w)[:, :, s * 256 : (s + 1) * 256])

            sp.wait_ge(loaded_x, 16)
            for l, w_in in ((0, A["w_in_ab"][0]), (1, A["w_in_cd"][0])):
                ffn(2 * l)
                square(at["qkv", l], w_in, 12)
                square(at["wo", l], A["w_out"][l], 4)
                ffn(2 * l + 1)
            w2 = A["w_in_2"][0]
            cols = [(256 * s, 256 * s + 256) for s in range(9)] + [(2304, 2336)]
            for s, (a, b) in enumerate(cols):
                k = at["in2"] + s
                fetch(k, slot(k, KC, b - a), rows(w2)[:, :, a:b])
            k = at["mla"]
            fetch(k, slot(k, 2, 768), rows(A["mla_w_qup_2"][0]))
            fetch(k + 1, slot(k + 1, 1, 1024), rows(A["mla_w_kvup_2"][0]))
            for s in range(8):
                k = at["gates"] + s
                fetch(k, slot(k, KC, 256), rows(w2)[:, :, 2336 + 256 * s : 2592 + 256 * s])
            k = at["br"]
            for j, w in enumerate((A["w_br_rwkv_2"][0], A["w_br_mla_2"][0])):
                for s in range(2):
                    fetch(k + 2 * s + j, slot(k + 2 * s + j, 4, 512), rows(w)[:, :, s * 512 : (s + 1) * 512])
            square(at["wo", 2], A["w_out_2"][0], 4)
            square(at["wq"], A["peer_w_q_2"][0], 8)
            square(at["pg"], A["w_ple_gate_2"][0], 4)
            k = at["pp"]
            fetch(k, slot(k, 2, 1024), rows(A["w_ple_proj_2"][0]))

        @block.tensor
        def _(pe):
            owed = [0]
            owed_pairs = [0]

            def mm(dst, lhsT, rhs, start, stop_, loose=False):
                return pe.matmul(dst, lhsT, rhs, start=start, stop=stop_, skip_group_check=loose)

            def mm3(dst, w_hi, w_lo, x_hi, x_lo, start, stop_, loose=False):
                first = mm(dst, w_hi, x_hi, start, False, loose)
                mm(dst, w_lo, x_hi, False, False, loose)
                return first, mm(dst, w_hi, x_lo, False, stop_, loose)

            def release(ins):
                assert not (owed[0] and owed_pairs[0])
                for n, who in ((owed, slot_free), (owed_pairs, pair_used)):
                    if n[0]:
                        ins.then_inc(who, n[0])
                        n[0] = 0

            def have(k, i=0):
                pe.wait_ge(slot_loaded[k % RING], 16 * (k // RING + 1) + 16 * i)

            def norm(n):
                dst = fill_begin(pe, ("ssq", n))
                for k in range(KC):
                    if k % 2 == 0:
                        pe.wait_ge(sq_ready, 4 * n + k // 2 + 1)
                    ins = mm(dst[:, 0:T], C("ones", P), sq[:, k, :], k == 0, k == KC - 1)
                    if k == 0:
                        release(ins)
                fill_end(ins, ("ssq", n))

            def ffn(f, n):
                base, base_s = CHUNKS * f, FFN_SLOTS * f

                def gate_up(c, i):
                    b, s, g = bank[4 + c % 2], c % 2, c // 2
                    if c >= 2:
                        pe.wait_ge(hraw_ready, base + c - 1 + 4 * i)
                    for j, kind in enumerate(("gate", "up")):
                        if s == 0:
                            pe.wait_ge(split_ready, base_s + place(kind, g) + 1 + 6 * i)
                        hi = whi(kind, g).rearrange("p (k n) -> p k n", k=KC)
                        lo = wlo(kind, g).rearrange("p (k n) -> p k n", k=KC)
                        cols = slice(s * P, (s + 1) * P)
                        for kk in range(KC):
                            if c == 0 and j == 0:
                                pe.wait_ge(xn_ready, KC * n + kk + 1)
                            _, ins = mm3(b[:, j * T : (j + 1) * T], hi[:, kk, cols], lo[:, kk, cols],
                                         xh[:, kk, :], xl[:, kk, :], kk == 0, kk == KC - 1)
                        if s == 1 and j == 0:
                            ins.then_inc(pair_used, 1)
                    ins.then_inc(gu_ready, 1)
                    if s == 1:
                        owed_pairs[0] += 1

                def down(c, i):
                    g = c // 2
                    if c % 2 == 0:
                        pe.wait_ge(split_ready, base_s + place("down", g) + 1 + 6 * i)
                    pe.wait_ge(h_ready, base + c + 1 + 4 * i)
                    hi = whi("down", g).rearrange("p (k n) -> p k n", k=2)[:, c % 2, :]
                    lo = wlo("down", g).rearrange("p (k n) -> p k n", k=2)[:, c % 2, :]
                    for m in range(KC):
                        cols = slice(m * P, (m + 1) * P)
                        first, ins = mm3(bank[m // 2][:, (m % 2) * T : (m % 2 + 1) * T], hi[:, cols], lo[:, cols],
                                         HH[:, c % 2, :], HL[:, c % 2, :], c == 0 and m % 2 == 0, c == CHUNKS - 1, loose=True)
                        if m == 0:
                            release(first)
                        if c == CHUNKS - 1 and m % 2:
                            ins.then_inc(y_ready, 1)
                    if c == CHUNKS - 1:
                        owed_pairs[0] += 1
                    elif c % 2 == 1:
                        ins.then_inc(pair_used, 1)

                def group(g, i=0):
                    for s in range(2):
                        c = 2 * g + s
                        gate_up(c, i)
                        if c > 0:
                            down(c - 1, i)

                group(0)
                group(1)
                with pe.Fori(0, (GROUPS - 3) // 2) as i:
                    group(2, i)
                    group(3, i)
                group(GROUPS - 1)
                down(CHUNKS - 1, 0)

            def out_product(l, n_wait, src):
                for m in range(KC):
                    k = at["wo", l] + m // 2
                    b = fill_begin(pe, ("y", l, m // 2)) if m % 2 == 0 else bank[fill_of["y", l, m // 2][0]]
                    if m % 2 == 0:
                        have(k)
                    for kk in range(KC):
                        if m == 0:
                            n_wait(kk)
                        ins = mm(b[:, (m % 2) * T : (m % 2 + 1) * T], slot(k, KC, 256)[:, kk, (m % 2) * P : (m % 2 + 1) * P],
                                 src[:, kk, :], kk == 0, kk == KC - 1)
                        if kk == 0:
                            release(ins)
                    if m % 2:
                        fill_end(ins, ("y", l, m // 2))
                        owed[0] += 1

            def soft(l, n, pair0, q_of, k_of, v_of, both, extra=None):
                base = unit_base[l]
                for t in range(n + 3):
                    if t < n:
                        b = fill_begin(pe, ("s", l, t))
                        if both:
                            for qb in range(2):
                                ins = mm(b[:, qb * T : (qb + 1) * T], q_of(t)[:, qb * P : (qb + 1) * P], k_of(t), True, True)
                        else:
                            for a, w, qb in ((0, P, 0), (P, T, 1)):
                                ext = extra is not None and extra(t)
                                ins = mm(b[:, a : a + w], q_of(t)[:, qb * P : (qb + 1) * P], k_of(t)[:, 0:w], True, not ext)
                                if ext:
                                    ins = mm(b[:, a : a + w], FL[0:2, t, qb * P : (qb + 1) * P], FR[0:2, t, 0:w], False, True)
                        fill_end(ins, ("s", l, t))
                    if 2 <= t < n + 2:
                        u = t - 2
                        b = fill_begin(pe, ("pt", l, u))
                        pe.wait_ge(S("weights_ready"), base + u + 1)
                        pr = (PR2 if both else PR)[u % 3]
                        moves = ((0, 0), (P, 2 * P), (2 * P, P), (3 * P, 3 * P)) if both else ((0, 0), (P, P), (2 * P, 2 * P))
                        for src, dst in moves:
                            ins = pe.transpose(b[:, dst : dst + P], pr[:, src : src + P], ident)
                        fill_end(ins, ("pt", l, u))
                    if t >= 3:
                        u = t - 3
                        pair = ("o", l, pair0 + u // 2)
                        b = fill_begin(pe, pair) if u % 2 == 0 else bank[fill_of[pair][0]]
                        emptied(pe, ("pt", l, u))
                        ptb = (PT2 if both else PT)[u % 2]
                        o = b[(u % 2) * HD : (u % 2 + 1) * HD, 0:T]
                        mm(o, v_of(u, 0), ptb[:, 0:T], True, False)
                        if both:
                            ins = mm(o, v_of(u, 1), ptb[:, T : 2 * T], False, True)
                        else:
                            ins = mm(o[:, P:T], v_of(u, 1), ptb[:, T : T + P], False, True)
                        if u % 2:
                            fill_end(ins, pair)


            head = lambda buf, c0, h: buf[(h % 2) * HD : (h % 2 + 1) * HD, c0 + h // 2, :]

            def stick():
                for t in range(8 + 2):
                    if t < 8:
                        b = fill_begin(pe, ("z", 0, t))
                        q, k = head(QK, 0, t), head(QK, 8, t)
                        ins = mm(b[:, 0:T], k[:, 0:P], q, True, False, loose=True)
                        release(ins)
                        mm(b[:, T : T + P], k[:, P:T], q[:, P:T], False, False, loose=True).then_inc(S("z_ready"), 1)
                    if 1 <= t <= 8:
                        u = t - 1
                        b, lg = bank[4 + u % 2], ZL[u % 2]
                        pe.wait_ge(S("keep_ready"), 2 * u + 2)
                        mm(b[:, 0:T], C("suffix", P), lg[:, 0:T], False, False, loose=True)
                        mm(b[:, P:T], C("after", P), lg[:, T : T + P], False, True, loose=True)
                        fill_end(mm(b[:, T : T + P], C("suffix", P), lg[:, T : T + P], False, True, loose=True), ("z", 0, u))
                    if t >= 2:
                        u = t - 2
                        pair = ("o", 0, u // 2)
                        b = fill_begin(pe, pair) if u % 2 == 0 else bank[fill_of[pair][0]]
                        pe.wait_ge(S("stick_ready"), 2 * u + 2)
                        o = b[(u % 2) * HD : (u % 2 + 1) * HD, 0:T]
                        mm(o, VT[:, 0, u * HD : (u + 1) * HD], PT[u % 2][:, 0:T], True, False)
                        ins = mm(o[:, P:T], VT[:, 1, u * HD : (u + 1) * HD], PT[u % 2][:, T : T + P], False, True)
                        if u % 2:
                            fill_end(ins, pair)

            def layer(l):
                if l == 0:
                    pe.wait_ge(S("masks_loaded"), 16)
                first = 4 * l
                for s in range(12):
                    k = at["qkv", l] + s
                    have(k)
                    w = slot(k, KC, 256)
                    for half in range(2):
                        label = ("qk", l, 2 * s + half) if s < 8 else ("v", l, 2 * (s - 8) + half)
                        b = fill_begin(pe, label)
                        for kk in range(KC):
                            if s == 0 and half == 0:
                                pe.wait_ge(xn_ready, KC * (1 + 3 * l) + kk + 1)
                            if s < 8:
                                ins = mm(b[:, 0:T], w[:, kk, half * P : (half + 1) * P], xn[:, kk, :], kk == 0, kk == KC - 1)
                            else:
                                ins = mm(b[:, 0:T], xn[:, kk, half * P : (half + 1) * P], w[:, kk, :], kk == 0, kk == KC - 1)
                            if kk == 0:
                                release(ins)
                        fill_end(ins, label)
                        for i in with_values(l, 2 * (s - 8) + half) if s >= 8 else ():
                            b = fill_begin(pe, ("hssq", l, i))
                            pe.wait_ge(S("hsq_ready"), first + i + 1)
                            fill_end(mm(b[:, 0:512], C("heads", P), HSQ[i % 2], True, True), ("hssq", l, i))
                    owed[0] += 1
                if l == 1:
                    b = fill_begin(pe, ("forget", 1))
                    pe.wait_ge(S("wf_loaded"), 16)
                    for kk in range(KC):
                        ins = mm(b[0:8, 0:T], WF[:, kk, :], xn[:, kk, :], kk == 0, kk == KC - 1)
                        if kk == 0:
                            release(ins)
                    fill_end(ins, ("forget", 1))
                for i, (m, g, rope) in enumerate(qk_pairs[l]):
                    if rope:
                        b = fill_begin(pe, ("rot", l, i))
                        pe.wait_ge(S("hn_ready"), first + i + 1)
                        fill_end(mm(b[:, 0:512], C("turn", P), QK[:, m : m + 2, :].rearrange("p a b -> p (a b)"), True, True),
                                 ("rot", l, i))
                for m in (13, 14, 15):
                    emptied(pe, ("qk", l, m))
                for j in (5, 6, 7):
                    emptied(pe, ("v", l, j))
                if l == 0:
                    stick()
                else:
                    pe.wait_ge(S("hn_ready"), 12)
                    pe.wait_ge(S("forget_ready"), 32)
                pe.wait_ge(S("rope_ready"), 4 * (l + 1))
                h0 = 8 if l == 0 else 0
                soft(l, 8 if l == 0 else 16, 4 if l == 0 else 0,
                     lambda t: head(QK, 0, h0 + t), lambda t: head(QK, 8, h0 + t),
                     lambda t, kb: VT[:, kb, (h0 + t) * HD : (h0 + t + 1) * HD], False,
                     (lambda t: t < 8) if l == 1 else None)
                out_product(l, lambda kk: emptied(pe, ("o", l, kk)), MIX)

            def second_in():
                for s in range(10):
                    k = at["in2"] + s
                    have(k)
                    width = 32 if s == 9 else 256
                    w = slot(k, KC, width)
                    for half in range(1 if s == 9 else 2):
                        m = 2 * s + half
                        b = fill_begin(pe, ("u", m))
                        for kk in range(KC):
                            if m == 0:
                                pe.wait_ge(xn_ready, KC * 6 + kk + 1)
                            if s == 9:
                                ins = mm(b[64:96, 0:T], w[:, kk, :], xn[:, kk, :], kk == 0, kk == KC - 1)
                            else:
                                ins = mm(b[:, 0:T], w[:, kk, half * P : (half + 1) * P], xn[:, kk, :], kk == 0, kk == KC - 1)
                            if kk == 0:
                                release(ins)
                        fill_end(ins, ("u", m))
                    owed[0] += 1

            def gates(first, last):
                for m in range(first, last):
                    k = at["gates"] + m // 2
                    if m % 2 == 0:
                        have(k)
                    b = fill_begin(pe, ("gate", m))
                    for kk in range(KC):
                        ins = mm(b[:, 0:T], slot(k, KC, 256)[:, kk, (m % 2) * P : (m % 2 + 1) * P], xn[:, kk, :], kk == 0, kk == KC - 1)
                        if kk == 0:
                            release(ins)
                    fill_end(ins, ("gate", m))
                    owed[0] += m % 2

            def latent():
                pe.wait_ge(S("csq_ready"), 2)
                b = fill_begin(pe, ("mssq", 0))
                release(mm(b[:, 0:T], C("ones", P), TMPM[:, 0, :], True, False))
                fill_end(mm(b[:, 0:T], C("ones", P), TMPM[:, 1, :], False, True), ("mssq", 0))
                b = fill_begin(pe, ("mssq", 1))
                fill_end(mm(b[:, 0:T], C("ones", P), TMPM[:, 2, :], True, True), ("mssq", 1))
                kq = at["mla"]
                wq, wkv = slot(kq, 2, 768), slot(kq + 1, 1, 1024)
                have(kq)
                pe.wait_ge(S("cn_ready"), 3)
                for h in range(8):
                    b = fill_begin(pe, ("mq", h))
                    for kk in range(2):
                        ins = mm(b[0:96, 0:T], wq[:, kk, h * 96 : h * 96 + 96], CQN[:, kk, :], kk == 0, kk == 1)
                    fill_end(ins, ("mq", h))
                owed[0] += 1
                have(kq + 1)
                for h in range(8):
                    b = fill_begin(pe, ("mk", h))
                    fill_end(mm(b[0:64, 0:T], wkv[:, 0, h * P : h * P + 64], CKVN, True, True), ("mk", h))
                for j in range(2):
                    b = fill_begin(pe, ("mv", j))
                    fill_end(mm(b[:, 0:512].rearrange("p (a b) -> p a b", a=8), CKVN[:, j * P : (j + 1) * P],
                                wkv[:, 0, :].rearrange("p (a b) -> p a b", a=8)[:, :, 64:128], True, True), ("mv", j))
                owed[0] += 1
                gates(0, 2)
                for j in range(5):
                    b = fill_begin(pe, ("mrot", j))
                    if j < 4:
                        emptied(pe, ("mq", 2 * j))
                        emptied(pe, ("mq", 2 * j + 1))
                        src = QM[64:96, 2 * j : 2 * j + 2, :].rearrange("p a b -> p (a b)")
                    else:
                        emptied(pe, ("u", 18))
                        src = KR[64:96, :]
                    n = 512 if j < 4 else T
                    fill_end(mm(b[64:96, 0:n], C("turn_mla", 32)[64:96, :], src, True, True), ("mrot", j))
                gates(2, 6)
                pe.wait_ge(S("mrope_ready"), 2)
                for h in (5, 6, 7):
                    emptied(pe, ("mk", h))
                for j in range(2):
                    emptied(pe, ("mv", j))
                soft(2, 8, 0, lambda t: QM[0:96, t, :], lambda t: KM[0:96, t, :],
                     lambda t, kb: VM[:, kb, t * HD : (t + 1) * HD], True)

            def recurrence():
                pe.wait_ge(S("lora_loaded"), 48)
                pe.wait_ge(S("lora_in_ready"), 2)
                pe.wait_ge(S("shifted"), 15)
                for d in range(2):
                    for hp in range(4):
                        for j, name in enumerate(("lw", "la")):
                            b = fill_begin(pe, (name, d, hp))
                            ins = mm(b[:, 0:T], LORA[j][64 * d : 64 * d + 64, hp * P : (hp + 1) * P],
                                     US[64 * d : 64 * d + 64, 12 + j, :], True, True)
                            fill_end(ins, (name, d, hp))
                for hp in range(4):
                    b = fill_begin(pe, ("lg", hp))
                    fill_end(mm(b[:, 0:T], LORA[2][:, hp * P : (hp + 1) * P], US[:, 14, :], True, True), ("lg", hp))
                gates(6, 8)
                for j in range(2):
                    b = fill_begin(pe, ("kkss", j))
                    pe.wait_ge(S("kksq_ready"), 1)
                    fill_end(mm(b[:, 0:512], C("heads", P), sq[:, 2 * j : 2 * j + 2, :].rearrange("p a b -> p (a b)"), True, True),
                             ("kkss", j))
                for j in range(4):
                    c, half = j // 2, j % 2
                    b = fill_begin(pe, ("vtm", j))
                    for i in range(2):
                        ins = pe.transpose(b[:, i * P : (i + 1) * P], US[:, 8 + 2 * half + i, c * P : (c + 1) * P], ident)
                    fill_end(ins, ("vtm", j))
                gates(8, 16)
                pe.wait_ge(S("bkt_ready"), 2)
                for j in range(8):
                    d = j // 4
                    b = fill_begin(pe, ("bkt", j))
                    pe.transpose(b[:, 0:P], BT[:, j, d, :], ident)
                    fill_end(pe.transpose(b[:, P : 2 * P], KT[:, j, d, :], ident), ("bkt", j))
                pe.wait_ge(S("bonus_in_ready"), 4)
                for j in range(2):
                    b = fill_begin(pe, ("bonus", j))
                    fill_end(mm(b[:, 0:512], C("heads", P), US[:, 4 + 2 * j : 6 + 2 * j, :].rearrange("p a b -> p (a b)"), True, True),
                             ("bonus", j))
                for j in range(4):
                    emptied(pe, ("vtm", j))
                for j in range(4, 8):
                    emptied(pe, ("bkt", j))
                pe.wait_ge(S("ar_ready"), 2)
                for w, (d, c) in enumerate(WAVES):
                    for u in range(4):
                        j = 4 * d + u
                        for e in range(2):
                            ps = slice(64 * e, 64 * e + 64)
                            b = fill_begin(pe, ("gram", w, u, e))
                            ar = AR[ps, j, c, :, :].rearrange("p a b -> p (a b)")
                            mm(b[:, 0:T], BT[ps, j, c, :], ar, True, True)
                            fill_end(mm(b[:, T : 2 * T], KT[ps, j, c, :], ar, True, True), ("gram", w, u, e))
                    for l in range(7):
                        for u in range(4):
                            b = fill_begin(pe, ("W", w, l, u))
                            pe.wait_ge(S("level_ready"), 28 * w + 4 * l + u + 1)
                            if l:
                                emptied(pe, ("TT", w, l - 1, u) if l > 1 else ("W", w, 0, u))
                            for e in range(2):
                                if l:
                                    ins = mm(b[:, e * P : (e + 1) * P], LV[u][:, e, :], TNTT[u][:, 0, e, :], True, True)
                                else:
                                    ins = pe.transpose(b[:, e * P : (e + 1) * P], LV[u][:, e, :], ident)
                            fill_end(ins, ("W", w, l, u))
                        if l:
                            for u in range(4):
                                b = fill_begin(pe, ("TT", w, l, u))
                                emptied(pe, ("W", w, l, u))
                                for e in range(2):
                                    if l < 6:
                                        mm(b[:, e * P : (e + 1) * P], TNTT[u][:, 1, e, :], WW[u][:, e, :], True, True)
                                    ins = mm(b[:, (2 + e) * P : (3 + e) * P], WW[u][:, e, :], TNTT[u][:, 1, e, :], True, True)
                                fill_end(ins, ("TT", w, l, u))
                    for u in range(4):
                        j = 4 * d + u
                        b = fill_begin(pe, ("X", w, u))
                        if w >= 2:
                            emptied(pe, ("ST", w - 2, u))
                        if w >= 2:
                            mm(b[:, 0:P], AR[:, j, c, 0, :], ST[:, j, :], True, False, loose=True)
                        for e in range(2):
                            ins = mm(b[:, e * HD : (e + 1) * HD], M4[u][:, e, 2, :],
                                     VTM[:, c, u * P + e * HD : u * P + (e + 1) * HD], w < 2, True, loose=w >= 2)
                        fill_end(ins, ("X", w, u))
                    for u in range(4):
                        b = fill_begin(pe, ("U", w, u))
                        emptied(pe, ("X", w, u))
                        emptied(pe, ("TT", w, 6, u))
                        for e in range(2):
                            ins = mm(b[:, e * HD : (e + 1) * HD], TNTT[u][:, 1, e, :], XX[u][:, e * HD : (e + 1) * HD], True, True)
                        fill_end(ins, ("U", w, u))
                    for u in range(4):
                        j = 4 * d + u
                        b = fill_begin(pe, ("O", w, u))
                        emptied(pe, ("U", w, u))
                        if w >= 2:
                            mm(b[:, 0:P], ST[:, j, :], AR[:, j, c, 1, :], True, False, loose=True)
                        for e in range(2):
                            o = b[64 * e : 64 * e + 64, 0:P]
                            mm(o, VTM[:, c, u * P + e * HD : u * P + (e + 1) * HD], M4[u][:, e, 3, :], w < 2, False, loose=w >= 2)
                            ins = mm(o, UU[u][:, e * HD : (e + 1) * HD], M4[u][:, e, 1, :], False, True, loose=w >= 2)
                        fill_end(ins, ("O", w, u))
                    if w < 2:
                        for u in range(4):
                            b = fill_begin(pe, ("ST", w, u))
                            for e in range(2):
                                ps = slice(64 * e, 64 * e + 64)
                                cols = slice(u * P + e * HD, u * P + (e + 1) * HD)
                                mm(b[ps, 0:HD], BTM[:, d, cols], UU[u][:, e * HD : (e + 1) * HD], True, False)
                                ins = mm(b[ps, 0:HD], KTM[:, d, cols], VTM[:, c, cols], False, True)
                            fill_end(ins, ("ST", w, u))
                for name in ("gmean", "gvar"):
                    for j in range(2):
                        b = fill_begin(pe, (name, j))
                        if name == "gmean":
                            for u in range(4):
                                emptied(pe, ("O", 3, u))
                        else:
                            pe.wait_ge(S("ysq_ready"), 1)
                        src = YR if name == "gmean" else sq
                        fill_end(mm(b[:, 0:512], C("heads", P), src[:, 2 * j : 2 * j + 2, :].rearrange("p a b -> p (a b)"), True, True),
                                 (name, j))

            def branches_out():
                pe.wait_ge(S("y_rw_ready"), 2)
                for pair in range(4):
                    emptied(pe, ("o", 2, pair))
                for m in range(8):
                    for j, src in enumerate((YR, YM)):
                        k = at["br"] + 2 * (m // 4) + j
                        b = fill_begin(pe, ("br", j, m))
                        if m % 4 == 0:
                            have(k)
                        for kk in range(4):
                            ins = mm(b[:, 0:T], slot(k, 4, 512)[:, kk, (m % 4) * P : (m % 4 + 1) * P], src[:, kk, :], kk == 0, kk == 3)
                            if kk == 0:
                                release(ins)
                        fill_end(ins, ("br", j, m))
                        if m % 4 == 3:
                            owed[0] += 1
                out_product(2, lambda kk: pe.wait_ge(S("merged"), kk + 1), MG)

            def experts():
                def scores(h):
                    b = fill_begin(pe, ("sc", h))
                    emptied(pe, ("pq", 2 * h))
                    emptied(pe, ("pq", 2 * h + 1))
                    for tb in range(2):
                        for c in range(2):
                            at_ = (2 * tb + c) * P
                            ins = mm(b[:, at_ : at_ + P], QP[:, 2 * h + c, tb * P : (tb + 1) * P], KEYS[:, 2 * h + c, :], True, True)
                    fill_end(ins, ("sc", h))

                pe.wait_ge(S("keys_loaded"), 16)
                for h in range(8):
                    k = at["wq"] + h
                    have(k)
                    for c in range(2):
                        b = fill_begin(pe, ("pq", 2 * h + c))
                        for kk in range(KC):
                            if h + c == 0:
                                pe.wait_ge(xn_ready, KC * 7 + kk + 1)
                            ins = mm(b[:, 0:T], slot(k, KC, 256)[:, kk, c * P : (c + 1) * P], xn[:, kk, :], kk == 0, kk == KC - 1)
                            if kk == 0:
                                release(ins)
                        fill_end(ins, ("pq", 2 * h + c))
                    owed[0] += 1
                    if h:
                        scores(h - 1)
                scores(7)
                for j in range(4):
                    b = fill_begin(pe, ("htok", j))
                    for i in range(4):
                        ins = pe.transpose(b[:, i * P : (i + 1) * P], xn[:, 4 * (j % 2) + i, (j // 2) * P : (j // 2 + 1) * P], ident)
                        if j + i == 0:
                            release(ins)
                    fill_end(ins, ("htok", j))
                for j in range(4):
                    b = fill_begin(pe, ("back", j))
                    for i in range(4):
                        tb = i % 2
                        if j == 0:
                            pe.wait_ge(S("rows_used"), 8 * 16 * (3 + tb))
                        m = 2 * j + i // 2
                        ins = pe.transpose(b[:, i * P : (i + 1) * P], ACC[:, tb, m * P : (m + 1) * P], ident)
                        if i == 0:
                            release(ins)
                    fill_end(ins, ("back", j))

            def ple():
                pe.wait_ge(S("p_loaded"), 16)
                kp = at["pp"]
                for m in range(8):
                    k = at["pg"] + m // 2
                    if m % 2 == 0:
                        have(k)
                    b = fill_begin(pe, ("pg", m))
                    for kk in range(KC):
                        if m == 0:
                            pe.wait_ge(xn_ready, KC * 8 + kk + 1)
                        ins = mm(b[:, 0:T], slot(k, KC, 256)[:, kk, (m % 2) * P : (m % 2 + 1) * P], xn[:, kk, :], kk == 0, kk == KC - 1)
                    fill_end(ins, ("pg", m))
                    if m == 0:
                        have(kp)
                    b = fill_begin(pe, ("pp", m))
                    for kk in range(2):
                        ins = mm(b[:, 0:T], slot(kp, 2, 1024)[:, kk, m * P : (m + 1) * P], PIN[:, kk, :], kk == 0, kk == 1)
                    fill_end(ins, ("pp", m))

            pe.wait_ge(loaded_c, 16)
            for l in range(2):
                norm(3 * l)
                ffn(2 * l, 3 * l)
                norm(3 * l + 1)
                layer(l)
                norm(3 * l + 2)
                ffn(2 * l + 1, 3 * l + 2)
            norm(6)
            second_in()
            latent()
            recurrence()
            branches_out()
            norm(7)
            experts()
            norm(8)
            ple()
            norm(9)

        @block.scalar
        def _(act):
            chain = Chain(act_done)
            act.dma_start(xT[:, :, :], rows(A["xT"])).then_inc(loaded_x, 16)
            act.dma_start(con[:, 0:NFIRST], A["con"][:, 0:NFIRST]).then_inc(loaded_c, 16)
            act.dma_start(vec[:, :], A["vec"]).then_inc(loaded_v, 16)
            act.wait_ge(loaded_x, 16)
            act.wait_ge(loaded_c, 16)
            act.wait_ge(loaded_v, 16)

            def high(f, kind, g, i=0):
                k = at["ffn", f] + place(kind, g)
                act.wait_ge(slot_loaded[k % RING], 16 * (k // RING + 1) + 16 * i)
                order = 3 * (g - (1 if kind == "down" else 2)) + {"gate": 1, "up": 2, "down": 3}[kind]
                if FFN_SLOTS * f + order > 0:
                    act.wait_ge(pair_used, FFN_SLOTS * f + order + 6 * i)
                act.activation(whi(kind, g), ring[:, k % RING, :], ACT.Copy).then_inc(hi_ready, 1)

            def norm(n):
                f = {0: 0, 2: 1, 3: 2, 5: 3}.get(n)
                if f is not None and f > 0:
                    if n in (2, 5):
                        take(act, ("y", n // 3, 0))
                    high(f, "gate", 0)
                    high(f, "up", 0)
                act.preload_act_table(ACT.Sqrt)
                for m in range(4):
                    residual_done(act, n, [m])
                    act.activation(sq[:, 2 * m : 2 * m + 2, :], xT[:, 2 * m : 2 * m + 2, :], ACT.Square).then_inc(sq_ready, 1)
                src = take(act, ("ssq", n))
                give(act.activation(std[:, :], src[:, 0:T], ACT.Sqrt, bias=eps(0), scale=1.0 / D), ("ssq", n))
                if f is not None:
                    for k in range(KC):
                        act.wait_ge(S("xraw_ready"), KC * f + k + 1)
                        act.activation(xh[:, k, :], sq[:, k, :], ACT.Copy).then_inc(xh_ready, 1)

            def ffn(f):
                base = CHUNKS * f
                if f == 0:
                    high(f, "gate", 0)
                    high(f, "up", 0)
                high(f, "gate", 1)
                high(f, "up", 1)
                if f == 0:
                    act.dma_start(con[:, NFIRST:NCON], A["con"][:, NFIRST:NCON]).then_inc(S("masks_loaded"), 16)
                    act.dma_start(WF, rows(A["w_in_cd"][0])[:, :, 3 * D : 3 * D + 8]).then_inc(S("wf_loaded"), 16)
                    act.dma_start(small[0:8, 40:41], A["b_f"].rearrange("a n -> n a")).then_inc(S("bf_loaded"), 16)
                act.preload_act_table(ACT.Silu)

                def chunk(c, i=0):
                    act.wait_ge(gu_ready, base + c + 1 + 4 * i)
                    act.activation(sgate[:, c % 2, :], bank[4 + c % 2][:, 0:T], ACT.Silu).then_inc(silu_ready, 1)
                    act.wait_ge(hraw_ready, base + c + 1 + 4 * i)
                    act.activation(HH[:, c % 2, :], hT[:, c % 2, :], ACT.Copy).then_inc(hh_ready, 1)
                    for kind, g in splits_after(c):
                        high(f, kind, g, i)

                for c in range(3):
                    chunk(c)
                with act.Fori(0, (GROUPS - 3) // 2) as i:
                    for c in range(3, 7):
                        chunk(c, i)
                for c in range(CHUNKS - 3, CHUNKS):
                    chunk(c)

            def soft(l, n, both):
                base = unit_base[l]
                sm, pr, ptb = (None, PR2, PT2) if both else (SM, PR, PT)
                for t in range(n + 2):
                    if t < n:
                        act.wait_ge(S("max_ready"), base + t + 1)
                        src = take(act, ("s", l, t)) if both else sm[t % 2]
                        for qb, (a, w) in enumerate(((0, T), (T, T)) if both else ((0, P), (P, T))):
                            c = 2 * (t % 3) + qb
                            ins = act.activation(pr[t % 3][:, a : a + w], src[:, a : a + w], ACT.Exp,
                                                 bias=NM[:, c : c + 1], scale=SCALE[l], accum_out=RS[:, c : c + 1])
                            if not both:
                                ins.then_inc(S("exp_ready"), 1)
                        if both:
                            give(ins, ("s", l, t))
                    if t >= 2:
                        u = t - 2
                        b = take(act, ("pt", l, u))
                        w = 512 if both else 384
                        give(act.activation(ptb[u % 2][:, 0:w], b[:, 0:w], ACT.Copy), ("pt", l, u))

            def layer(l):
                if l == 0:
                    act.wait_ge(S("masks_loaded"), 16)
                for m in range(16):
                    b = take(act, ("qk", l, m))
                    give(act.activation(QK[:, m, :], b[:, 0:T], ACT.Copy), ("qk", l, m))
                for m in (13, 14, 15):
                    emptied(act, ("qk", l, m))
                first = 4 * l
                act.preload_act_table(ACT.Sqrt)

                def squares(i):
                    m = qk_pairs[l][i][0]
                    act.activation(HSQ[i % 2], QK[:, m : m + 2, :].rearrange("p a b -> p (a b)"),
                                   ACT.Square).then_inc(S("hsq_ready"), 1)

                squares(0)
                for i, (m, g, rope) in enumerate(qk_pairs[l]):
                    if i + 1 < len(qk_pairs[l]):
                        squares(i + 1)
                    b = take(act, ("hssq", l, i))
                    if i >= 2:
                        act.wait_ge(S("hn_ready"), first + i - 1)
                    give(act.activation(HSTD[i % 2], b[:, 0:512], ACT.Sqrt, bias=eps(0), scale=1.0 / HD), ("hssq", l, i))
                act.preload_act_table_set("natural_log_exp_and_others")
                if l == 1:
                    b = take(act, ("forget", 1))
                    act.wait_ge(S("bf_loaded"), 16)
                    chain.link(act, act.activation(FG[0:8, 0, :], b[0:8, 0:T], ACT.Abs, bias=small[0:8, 40:41]))
                    chain.link(act, act.activation(FG[0:8, 0, :], FG[0:8, 0, :], ACT.Exp, scale=-1.0))
                    act.activation(FG[0:8, 0, :], FG[0:8, 0, :], ACT.Ln, bias=C("one", 1)[0:8, :]).then_inc(S("fln_ready"), 1)
                else:
                    for t in range(8 + 1):
                        if t < 8:
                            act.wait_ge(S("z_ready"), t + 1)
                            zl, z = ZL[t % 2][:, 0:384], bank[4 + t % 2][:, 0:384]
                            act.activation(zl, z, ACT.Abs).then_inc(S("abs_ready"), 1)
                            act.wait_ge(S("abs_ready"), t + 1)
                            chain.link(act, act.activation(zl, zl, ACT.Exp, scale=-0.125))
                            act.activation(zl, zl, ACT.Ln, bias=C("one", 1)).then_inc(S("ln_ready"), 1)
                        if t >= 1:
                            u = t - 1
                            b = take(act, ("z", 0, u))
                            give(act.activation(PT[u % 2][:, 0:384], b[:, 0:384], ACT.Exp, scale=0.125), ("z", 0, u))
                soft(l, 8 if l == 0 else 16, False)

            def second_in():
                act.preload_act_table(ACT.Sigmoid)
                residual_done(act, 6)
                act.dma_start(LORA[0], A["rw_w2_2"][0].rearrange("d l n -> (d l) n")).then_inc(S("lora_loaded"), 16)
                act.dma_start(LORA[1], A["rw_a2_2"][0].rearrange("d l n -> (d l) n")).then_inc(S("lora_loaded"), 16)
                act.dma_start(LORA[2], A["rw_g2_2"][0]).then_inc(S("lora_loaded"), 16)
                for m in range(19):
                    b = take(act, ("u", m))[:, 0:T]
                    if m < 15:
                        dst = U0[:, m, 1 : T + 1]
                    elif m < 17:
                        dst = CQ[:, m - 15, :]
                    elif m == 17:
                        dst = CKV
                    else:
                        dst, b = KR[64:96, :], b[64:96, :]
                    give(act.activation(dst, b, ACT.Copy), ("u", m))

            def gates(first, last):
                for m in range(first, last):
                    b = take(act, ("gate", m))
                    give(act.activation(GATES[:, m, :], b[:, 0:T], ACT.Copy), ("gate", m))

            def latent():
                for m in (15, 16, 17):
                    emptied(act, ("u", m))
                act.activation(TMPM[:, 0:2, :], CQ, ACT.Square).then_inc(S("csq_ready"), 1)
                act.activation(TMPM[:, 2, :], CKV, ACT.Square).then_inc(S("csq_ready"), 1)
                for j, width in ((0, 256), (1, 128)):
                    b = take(act, ("mssq", j))
                    give(act.activation(TMPM[:, 3 + j, :], b[:, 0:T], ACT.Sqrt, bias=eps(0), scale=1.0 / width), ("mssq", j))
                act.wait_ge(S("angle_ready"), 2)
                act.activation(SINM[64:96, :], ANG[64:96, :], ACT.Sin).then_inc(S("trig_ready"), 1)
                act.activation(COSM[64:96, :], ANG2[64:96, :], ACT.Sin).then_inc(S("trig_ready"), 1)
                for h in range(8):
                    b = take(act, ("mq", h))
                    give(act.activation(QM[0:96, h, :], b[0:96, 0:T], ACT.Copy), ("mq", h))
                for h in range(8):
                    b = take(act, ("mk", h))
                    give(act.activation(KM[0:64, h, :], b[0:64, 0:T], ACT.Copy), ("mk", h))
                act.preload_act_table(ACT.Exp)
                gates(0, 6)
                soft(2, 8, True)

            def recurrence():
                act.preload_act_table(ACT.Sigmoid)
                act.wait_ge(S("shifted"), 15)
                act.activation(US[:, 12, :], US[:, 12, :], ACT.Tanh).then_inc(S("lora_in_ready"), 1)
                act.activation(US[:, 14, :], US[:, 14, :], ACT.Sigmoid).then_inc(S("lora_in_ready"), 1)
                for d in range(2):
                    for hp in range(4):
                        j = 4 * d + hp
                        b = take(act, ("lw", d, hp))
                        give(act.activation(CF[:, j, :, :].rearrange("p a b -> p (a b)"), b[:, 0:T], ACT.Sigmoid,
                                            bias=V("rw_w0_2", j)), ("lw", d, hp))
                        b = take(act, ("la", d, hp))
                        give(act.activation(RATE[:, j, :], b[:, 0:T], ACT.Sigmoid, bias=V("rw_a0_2", j)), ("la", d, hp))
                for hp in range(4):
                    b = take(act, ("lg", hp))
                    give(act.activation(G2[hp // 2][:, hp % 2, :], b[:, 0:T], ACT.Copy), ("lg", hp))
                gates(6, 8)
                act.wait_ge(S("kk_ready"), 4)
                act.activation(sq[:, 0:4, :], KK, ACT.Square).then_inc(S("kksq_ready"), 1)
                for j in range(2):
                    emptied(act, ("kkss", j))
                act.activation(sq[:, 4:8, :], sq[:, 4:8, :], ACT.Sqrt).then_inc(S("kkstd_ready"), 1)
                act.preload_act_table(ACT.Exp)
                act.wait_ge(S("decay_ready"), 1)
                for d, (q, q_in, s) in enumerate(((CF, CE, 1.0), (CE, CF, -1.0))):
                    js = slice(4 * d, 4 * d + 4)
                    act.activation(BT[:, js, :, :], q[:, js, :, :], ACT.Exp, scale=-s).then_inc(S("expd_ready"), 1)
                    act.activation(AR[:, js, :, 0, :], q_in[:, js, :, :], ACT.Exp, scale=s).then_inc(S("expd_ready"), 1)
                    act.activation(AR[:, js, :, 1, :], q[:, js, :, :], ACT.Exp, scale=s).then_inc(S("expd_ready"), 1)
                act.activation(SSC, SSC, ACT.Exp).then_inc(S("carry_ready"), 1)
                gates(8, 16)
                for m in (14, 15):
                    emptied(act, ("gate", m))
                act.activation(GATES, GATES, ACT.Sigmoid).then_inc(S("gates_ready"), 1)
                for w in range(4):
                    for l in range(1, 7):
                        for u in range(4):
                            b = take(act, ("W", w, l, u))
                            give(act.activation(WW[u].rearrange("p a b -> p (a b)"), b[:, 0:T], ACT.Copy), ("W", w, l, u))
                    for u in range(4):
                        b = take(act, ("X", w, u))
                        give(act.activation(XX[u], b[:, 0:P], ACT.Copy), ("X", w, u))
                    for u in range(4):
                        b = take(act, ("U", w, u))
                        give(act.activation(UU[u], b[:, 0:P], ACT.Copy), ("U", w, u))
                for j in range(2):
                    emptied(act, ("gmean", j))
                act.activation(sq[:, 0:4, :], YR, ACT.Square).then_inc(S("ysq_ready"), 1)
                for j in range(2):
                    b = take(act, ("gvar", j))
                    give(act.activation(sq[:, 4 + 2 * j : 6 + 2 * j, :].rearrange("p a b -> p (a b)"), b[:, 0:512], ACT.Sqrt,
                                        bias=eps(1), scale=1.0 / HD), ("gvar", j))
                act.dma_start(KEYS, A["sub_keys_t"].rearrange("h d k -> d h k")).then_inc(S("keys_loaded"), 16)

            def experts():
                for h in range(8 + 1):
                    if h < 8:
                        for m in (2 * h, 2 * h + 1):
                            b = take(act, ("pq", m))
                            give(act.activation(QP[:, m, :], b[:, 0:T], ACT.Copy), ("pq", m))
                    if h:
                        b = take(act, ("sc", h - 1))
                        give(act.activation(SC[:, :, 2 * h - 2 : 2 * h, :], b[:, 0:512].rearrange("p (t c k) -> p t c k", t=2, c=2),
                                            ACT.Copy), ("sc", h - 1))
                for j in range(4):
                    b = take(act, ("htok", j))
                    give(act.activation(HTOK[:, j // 2, (j % 2) * 512 : (j % 2 + 1) * 512], b[:, 0:512], ACT.Copy), ("htok", j))
                act.preload_act_table(ACT.Exp)
                for tb in range(2):
                    act.wait_ge(S("gate_in_ready"), tb + 1)
                    act.activation(PEX, PEX, ACT.Exp).then_inc(S("gate_exp_ready"), 1)
                act.preload_act_table(ACT.Gelu)
                for tb in range(2):
                    act.wait_ge(S("dots_ready"), 16 * (tb + 1))
                    act.activation(WT[:, tb, :], DOTS[:, tb, :], ACT.Gelu).then_inc(S("gelu_ready"), 1)

            def ple():
                act.preload_act_table(ACT.Sigmoid)
                for m in range(8):
                    b = take(act, ("pg", m))
                    give(act.activation(view(4096 + T * m, T), b[:, 0:T], ACT.Sigmoid), ("pg", m))

            for l in range(2):
                norm(3 * l)
                ffn(2 * l)
                norm(3 * l + 1)
                layer(l)
                norm(3 * l + 2)
                ffn(2 * l + 1)
            norm(6)
            second_in()
            latent()
            recurrence()
            norm(7)
            experts()
            norm(8)
            act.dma_start(PIN, rows(A["pT"])).then_inc(S("p_loaded"), 16)
            ple()
            norm(9)

        @block.vector
        def _(dve):
            chain = Chain(dve_done)
            link = lambda ins: chain.link(dve, ins)
            dve.wait_ge(loaded_x, 16)
            dve.wait_ge(loaded_c, 16)
            dve.wait_ge(loaded_v, 16)

            def low(f, kind, g, i=0):
                k = at["ffn", f] + place(kind, g)
                dve.wait_ge(hi_ready, FFN_SLOTS * f + place(kind, g) + 1 + 6 * i)
                dve.tensor_tensor(wlo(kind, g), ring[:, k % RING, :], whi(kind, g), ALU.subtract).then_inc(split_ready, 1)

            def norm(n):
                name, c0 = norm_g[n]
                f = {0: 0, 2: 1, 3: 2, 5: 3}.get(n)
                if f is not None and f > 0:
                    low(f, "gate", 0)
                emptied(dve, ("ssq", n))
                link(dve.reciprocal(rstd[:, :], std[:, :]))
                raw = xn if f is None else sq
                for k in range(KC + (0 if f is None else 2)):
                    if k < KC:
                        dve.scalar_tensor_tensor(out=raw[:, k, :], in0=xT[:, k, :], scalar=V(name, c0 + k), in1=rstd[:, :],
                                                 op0=ALU.mult, op1=ALU.mult).then_inc(xn_ready if f is None else S("xraw_ready"), 1)
                    if f is not None and k >= 2:
                        dve.wait_ge(xh_ready, KC * f + k - 1)
                        dve.tensor_tensor(xl[:, k - 2, :], sq[:, k - 2, :], xh[:, k - 2, :], ALU.subtract).then_inc(xn_ready, 1)
                if f is not None and f > 0:
                    low(f, "up", 0)

            def ffn(f):
                base = CHUNKS * f
                if f == 0:
                    low(f, "gate", 0)
                    low(f, "up", 0)
                low(f, "gate", 1)
                low(f, "up", 1)

                def chunk(c, i=0):
                    dve.wait_ge(silu_ready, base + c + 1 + 4 * i)
                    if base + c >= 2:
                        dve.wait_ge(h_ready, base + c - 1 + 4 * i)
                    dve.tensor_tensor(hT[:, c % 2, :], sgate[:, c % 2, :], bank[4 + c % 2][:, T : 2 * T],
                                      ALU.mult).then_inc(hraw_ready, 1)
                    dve.wait_ge(hh_ready, base + c + 1 + 4 * i)
                    dve.tensor_tensor(HL[:, c % 2, :], hT[:, c % 2, :], HH[:, c % 2, :], ALU.subtract).then_inc(h_ready, 1)
                    for kind, g in splits_after(c):
                        low(f, kind, g, i)

                for c in range(3):
                    chunk(c)
                with dve.Fori(0, (GROUPS - 3) // 2) as i:
                    for c in range(3, 7):
                        chunk(c, i)
                for c in range(CHUNKS - 3, CHUNKS):
                    chunk(c)
                for m in range(4):
                    dve.wait_ge(y_ready, 4 * f + m + 1)
                    xs = xT[:, 2 * m : 2 * m + 2, :].rearrange("p a b -> p (a b)")
                    dve.scalar_tensor_tensor(out=xs, in0=bank[m][:, :], scalar=0.5, in1=xs, op0=ALU.mult,
                                             op1=ALU.add).then_inc(x_ready, 1)

            def residual(label, done=True):
                for m in range(4):
                    b = take(dve, (*label, m))
                    xs = xT[:, 2 * m : 2 * m + 2, :].rearrange("p a b -> p (a b)")
                    give(dve.tensor_tensor(xs, xs, b[:, :], ALU.add), (*label, m))

            def mix_out(l, pair, dst):
                b = take(dve, ("o", l, pair))
                give(dve.tensor_copy(dst[:, pair, :], b[:, 0:T]), ("o", l, pair))

            def soft(l, n, pair0, both, mask_of, dst):
                base = unit_base[l]
                sm, pr = (None, PR2) if both else (SM, PR)
                for t in range(n + 5):
                    if t < n:
                        b = take(dve, ("s", l, t))
                        mx = MX[:, 2 * (t % 3) : 2 * (t % 3) + 2]
                        if both:
                            link(dve.tensor_reduce(mx, b[:, 0:512].rearrange("p (a b) -> p a b", a=2), AX.X, ALU.max))
                        else:
                            mask = mask_of(t)
                            dve.tensor_tensor_reduce(sm[t % 2][:, 0:P], b[:, 0:P], mask[:, 0:P], 1.0, -3.0e38,
                                                     ALU.add, ALU.max, mx[:, 0:1])
                            give(dve.tensor_tensor_reduce(sm[t % 2][:, P : 3 * P], b[:, P : 3 * P], mask[:, P : 3 * P], 1.0,
                                                          -3.0e38, ALU.add, ALU.max, mx[:, 1:2]), ("s", l, t))
                            emptied(dve, ("s", l, t))
                        dve.tensor_scalar(NM[:, 2 * (t % 3) : 2 * (t % 3) + 2], mx, -SCALE[l], None, ALU.mult)\
                           .then_inc(S("max_ready"), 1)
                    if 1 <= t <= n:
                        u = t - 1
                        if both:
                            emptied(dve, ("s", l, u))
                        else:
                            dve.wait_ge(S("exp_ready"), 2 * (base + u + 1))
                        c = 2 * (u % 3)
                        link(dve.reciprocal(RI[:, c : c + 2], RS[:, c : c + 2]))
                        for qb, (a, w) in enumerate(((0, T), (T, T)) if both else ((0, P), (P, T))):
                            v = pr[u % 3][:, a : a + w]
                            ins = dve.tensor_scalar(v, v, RI[:, c + qb : c + qb + 1], None, ALU.mult)
                        ins.then_inc(S("weights_ready"), 1)
                    if t >= 4 and t % 2:
                        mix_out(l, pair0 + (t - 4) // 2, dst)

            def layer(l):
                if l == 0:
                    dve.wait_ge(S("masks_loaded"), 16)
                for j in range(8):
                    b = take(dve, ("v", l, j))
                    give(dve.tensor_copy(VT[:, j % 2, (j // 2) * 256 : (j // 2 + 1) * 256], b[:, 0:T]), ("v", l, j))
                    for i in with_values(l, j):
                        m, g, rope = qk_pairs[l][i]
                        emptied(dve, ("hssq", l, i))
                        link(dve.reciprocal(HSTD[i % 2], HSTD[i % 2]))
                        qk = QK[:, m : m + 2, :].rearrange("p a b -> p (a b)")
                        dve.scalar_tensor_tensor(out=qk, in0=qk, scalar=V(g), in1=HSTD[i % 2], op0=ALU.mult,
                                                 op1=ALU.mult).then_inc(S("hn_ready"), 1)
                if l == 1:
                    b = take(dve, ("forget", 1))
                    dve.wait_ge(S("bf_loaded"), 16)
                    dve.wait_ge(S("fln_ready"), 1)
                    give(dve.tensor_scalar(FG[0:8, 1, :], b[0:8, 0:T], small[0:8, 40:41], 0.0, ALU.add, ALU.min), ("forget", 1))
                    emptied(dve, ("forget", 1))
                    link(dve.tensor_tensor(FG[0:8, 2, :], FG[0:8, 1, :], FG[0:8, 0, :], ALU.subtract))
                    link(dve.memset(FG[0:8, 1, :], 1.0))
                    link(dve.tensor_tensor_scan(FG[0:8, 3, :], FG[0:8, 1, :], FG[0:8, 2, :], 0.0, ALU.mult, ALU.add))
                    dve.tensor_scalar(FG[0:8, 0, :], FG[0:8, 3, :], 8.0, None, ALU.mult).then_inc(S("sums_ready"), 1)
                    dve.tensor_scalar(FG[0:8, 1, :], FG[0:8, 3, :], -8.0, None, ALU.mult).then_inc(S("sums_ready"), 1)
                roped = 4 * l
                for i, (m, g, rope) in enumerate(qk_pairs[l]):
                    if rope:
                        b = take(dve, ("rot", l, i))
                        qk = QK[:, m : m + 2, :]
                        table = lambda name: C(name, T).unsqueeze(1).broadcast_to([P, 2, T])
                        rot = ROT.rearrange("p (a b) -> p a b", a=2)
                        if roped:
                            dve.wait_ge(S("rope_ready"), roped)
                        roped += 1
                        give(dve.tensor_tensor(rot, b[:, 0:512].rearrange("p (a b) -> p a b", a=2), table("sin"), ALU.mult),
                             ("rot", l, i))
                        link(dve.tensor_tensor(qk, qk, table("cos"), ALU.mult))
                        emptied(dve, ("rot", l, i))
                        dve.tensor_tensor(qk, qk, rot, ALU.add).then_inc(S("rope_ready"), 1)
                if l == 0:
                    for t in range(8 + 4):
                        if t < 8:
                            dve.wait_ge(S("abs_ready"), t + 1)
                            z, r, zl = bank[4 + t % 2][:, 0:384], ZR[t % 2][:, 0:384], ZL[t % 2][:, 0:384]
                            link(dve.tensor_scalar(r, z, 0.0, 0.125, ALU.max, ALU.mult))
                            dve.wait_ge(S("ln_ready"), t + 1)
                            dve.tensor_tensor(zl, zl, r, ALU.add).then_inc(S("softplus_ready"), 1)
                        if t >= 3 and (t - 3) % 2:
                            mix_out(0, (t - 3) // 2, MIX)
                causal = lambda t: C("causal", 384)
                soft(l, 8 if l == 0 else 16, 4 if l == 0 else 0, False,
                     causal if l == 0 else lambda t: C("causal" if t < 8 else "dilated", 384), MIX)
                residual(("y", l))

            def second_in():
                residual_done(dve, 6)
                link(dve.memset(U0[:, :, 0:1], 0.0))
                link(dve.memset(U0[:, :, T + 1 : T + 2], 0.0))
                for g in range(3):
                    ms = slice(5 * g, 5 * g + 5)
                    for m in range(5 * g + 1, 5 * g + 5):
                        emptied(dve, ("u", m))
                    link(dve.tensor_tensor(US[:, ms, :], U0[:, ms, 0:T], U0[:, ms, 2 : T + 2], ALU.add))
                    link(dve.scalar_tensor_tensor(out=US[:, ms, :], in0=US[:, ms, :], scalar=0.5, in1=U0[:, ms, 1 : T + 1],
                                                  op0=ALU.mult, op1=ALU.subtract))
                    for m in range(5 * g, 5 * g + 5):
                        dve.scalar_tensor_tensor(out=US[:, m, :], in0=US[:, m, :], scalar=V("rw_mu_2", m),
                                                 in1=U0[:, m, 1 : T + 1], op0=ALU.mult, op1=ALU.add).then_inc(S("shifted"), 1)

            def latent():
                r = slice(64, 96)
                dve.wait_ge(S("pos_loaded"), 16)
                link(dve.tensor_copy(POSF[r, :], POS[r, :]))
                link(dve.tensor_scalar(POSF[r, :], POSF[r, :], C("inv", 1)[r, :], None, ALU.mult))
                whole, hi, lo = 12582912.0, 6.28125, 0.0019353071795864769
                for dst, quarter in ((ANG, 0.0), (ANG2, 0.25)):
                    link(dve.tensor_scalar(dst[r, :], POSF[r, :], 1.0 / (2 * np.pi), quarter, ALU.mult, ALU.add))
                    link(dve.tensor_scalar(dst[r, :], dst[r, :], whole, None, ALU.add))
                    link(dve.tensor_scalar(dst[r, :], dst[r, :], -whole, None, ALU.add))
                    link(dve.scalar_tensor_tensor(out=COSM[r, :], in0=dst[r, :], scalar=-hi, in1=POSF[r, :],
                                                  op0=ALU.mult, op1=ALU.add))
                    link(dve.scalar_tensor_tensor(out=dst[r, :], in0=dst[r, :], scalar=-lo, in1=COSM[r, :],
                                                  op0=ALU.mult, op1=ALU.add))
                    link(dve.tensor_scalar(dst[r, :], dst[r, :], quarter * 2 * np.pi, 3.1415925, ALU.add, ALU.min))
                    dve.tensor_scalar(dst[r, :], dst[r, :], -3.1415925, None, ALU.max).then_inc(S("angle_ready"), 1)
                for j in range(2):
                    emptied(dve, ("mssq", j))
                link(dve.reciprocal(TMPM[:, 3:5, :], TMPM[:, 3:5, :]))
                for dst, src, g, j in ((CQN[:, 0, :], CQ[:, 0, :], V("mla_g_qa_2", 0), 3), (CQN[:, 1, :], CQ[:, 1, :], V("mla_g_qa_2", 1), 3),
                                       (CKVN, CKV, V("mla_g_kva_2"), 4)):
                    dve.scalar_tensor_tensor(out=dst, in0=src, scalar=g, in1=TMPM[:, j, :], op0=ALU.mult,
                                             op1=ALU.mult).then_inc(S("cn_ready"), 1)
                for j in range(2):
                    b = take(dve, ("mv", j))
                    give(dve.tensor_copy(VM[:, j, :], b[:, 0:512]), ("mv", j))
                dve.wait_ge(S("trig_ready"), 2)
                dve.wait_ge(S("cn_ready"), 3)
                sin2 = SINM[r, :].unsqueeze(1).broadcast_to([32, 2, T])
                for j in range(4):
                    b = take(dve, ("mrot", j))
                    give(dve.tensor_tensor(TMPM[r, 2 * j : 2 * j + 2, :], b[r, 0:512].rearrange("p (a b) -> p a b", a=2), sin2, ALU.mult),
                         ("mrot", j))
                link(dve.tensor_tensor(QM[r, :, :], QM[r, :, :], COSM[r, :].unsqueeze(1).broadcast_to([32, 8, T]), ALU.mult))
                for j in range(2, 4):
                    emptied(dve, ("mrot", j))
                dve.tensor_tensor(QM[r, :, :], QM[r, :, :], TMPM[r, :, :], ALU.add).then_inc(S("mrope_ready"), 1)
                b = take(dve, ("mrot", 4))
                give(dve.tensor_tensor(POSF[r, :], b[r, 0:T], SINM[r, :], ALU.mult), ("mrot", 4))
                emptied(dve, ("u", 18))
                link(dve.tensor_tensor(KR[r, :], KR[r, :], COSM[r, :], ALU.mult))
                emptied(dve, ("mrot", 4))
                dve.tensor_tensor(KM[r, :, :], KR[r, :].unsqueeze(1).broadcast_to([32, 8, T]),
                                  POSF[r, :].unsqueeze(1).broadcast_to([32, 8, T]), ALU.add).then_inc(S("mrope_ready"), 1)
                soft(2, 8, 0, True, None, YM)

            def recurrence():
                flat = lambda v: v.rearrange("p a b -> p (a b)")
                for hp in range(4):
                    emptied(dve, ("lw", 1, hp))
                    emptied(dve, ("lw", 0, hp))
                link(dve.tensor_scalar(CE, CF, -DECAY, None, ALU.mult))
                for j in range(8):
                    for c in range(2):
                        ins = dve.tensor_tensor_scan(CF[:, j, c, :], C("ones", P), CE[:, j, c, :], 0.0, ALU.mult, ALU.add)
                link(ins)
                link(dve.tensor_tensor(CE, CF, CE, ALU.subtract))
                dve.tensor_copy(REF[:, 0:4, :], CF[:, 0:4, :, 63])
                link(dve.tensor_copy(REF[:, 4:8, :], CE[:, 4:8, :, 64]))
                for buf in (CF, CE):
                    ins = dve.tensor_tensor(buf, buf, REF.unsqueeze(3).broadcast_to([P, 8, 2, P]), ALU.subtract)
                link(ins)
                dve.tensor_tensor(SSC, CF[:, :, 0, P - 1], REF[:, :, 1], ALU.add).then_inc(S("decay_ready"), 1)
                for hp in range(4):
                    dve.tensor_scalar(KK[:, hp, :], US[:, 4 + hp, :], V("rw_k_k_2", hp), None, ALU.mult).then_inc(S("kk_ready"), 1)
                for j in range(2):
                    b = take(dve, ("kkss", j))
                    give(dve.tensor_scalar(flat(sq[:, 4 + 2 * j : 6 + 2 * j, :]), b[:, 0:512], 1e-24, None, ALU.max), ("kkss", j))
                dve.wait_ge(S("kkstd_ready"), 1)
                link(dve.reciprocal(sq[:, 4:8, :], sq[:, 4:8, :]))
                link(dve.tensor_tensor(KK, KK, sq[:, 4:8, :], ALU.mult))
                for hp in range(4):
                    emptied(dve, ("la", 0, hp))
                    emptied(dve, ("la", 1, hp))
                for j in range(8):
                    link(dve.tensor_scalar(KD[:, j, :], RATE[:, j, :], 1.0, V("rw_k_a_2", j % 4), ALU.subtract, ALU.mult))
                    ins = dve.scalar_tensor_tensor(out=KD[:, j, :], in0=KD[:, j, :], scalar=1.0, in1=US[:, 4 + j % 4, :],
                                                   op0=ALU.add, op1=ALU.mult)
                link(ins)
                dve.wait_ge(S("expd_ready"), 6)
                link(dve.tensor_tensor(KT.rearrange("p j c t -> p j (c t)"), BT.rearrange("p j c t -> p j (c t)"), KD, ALU.mult))
                for d in range(2):
                    js = slice(4 * d, 4 * d + 4)
                    kk4 = KK.rearrange("p h (c t) -> p h c t", c=2)
                    r4 = US[:, 0:4, :].rearrange("p h (c t) -> p h c t", c=2)
                    ins = dve.tensor_tensor(RATE[:, js, :], RATE[:, js, :], KK, ALU.mult)
                    dve.tensor_tensor(AR[:, js, :, 0, :], AR[:, js, :, 0, :], kk4, ALU.mult)
                    dve.tensor_tensor(AR[:, js, :, 1, :], AR[:, js, :, 1, :], r4, ALU.mult).then_inc(S("ar_ready"), 1)
                dve.wait_ge(S("ar_ready"), 2)
                bt = BT.rearrange("p j c t -> p (j c t)")
                dve.scalar_tensor_tensor(out=bt, in0=bt, scalar=-1.0, in1=RATE.rearrange("p j t -> p (j t)"),
                                         op0=ALU.mult, op1=ALU.mult).then_inc(S("bkt_ready"), 2)
                link(dve.tensor_tensor(US[:, 4:8, :], KD[:, 0:4, :], KD[:, 4:8, :], ALU.add))
                for hp in range(4):
                    dve.scalar_tensor_tensor(out=US[:, 4 + hp, :], in0=US[:, hp, :], scalar=V("rw_r_k_2", hp),
                                             in1=US[:, 4 + hp, :], op0=ALU.mult, op1=ALU.mult).then_inc(S("bonus_in_ready"), 1)
                for j in range(4):
                    b = take(dve, ("vtm", j))
                    give(dve.tensor_copy(VTM[:, j // 2, (j % 2) * T : (j % 2 + 1) * T], b[:, 0:T]), ("vtm", j))
                for j in range(8):
                    d, hp = j // 4, j % 4
                    b = take(dve, ("bkt", j))
                    dve.tensor_copy(BTM[:, d, hp * P : (hp + 1) * P], b[:, 0:P])
                    give(dve.tensor_copy(KTM[:, d, hp * P : (hp + 1) * P], b[:, P : 2 * P]), ("bkt", j))
                for j in range(2):
                    b = take(dve, ("bonus", j))
                    give(dve.tensor_tensor(flat(US[:, 2 * j : 2 * j + 2, :]), b[:, 0:512], flat(US[:, 8 + 2 * j : 10 + 2 * j, :]),
                                           ALU.mult), ("bonus", j))
                for j in range(2):
                    emptied(dve, ("bonus", j))
                link(dve.memset(ST, 0.0))
                dve.wait_ge(S("carry_ready"), 1)
                eye = ident.unsqueeze(1).broadcast_to([P, 2, P])
                for w, (d, c) in enumerate(WAVES):
                    seen = C("seen", 2 * P, 2 * P * d).rearrange("p (a b) -> p a b", a=2).unsqueeze(1).broadcast_to([P, 2, 2, P])
                    for u in range(4):
                        for e in range(2):
                            b = take(dve, ("gram", w, u, e))
                            give(dve.tensor_tensor(M4[u][:, e, :, :].rearrange("p (k a) t -> p k a t", k=2),
                                                   b[:, 0:512].rearrange("p (k a t) -> p k a t", k=2, a=2), seen, ALU.mult),
                                 ("gram", w, u, e))
                    for l in range(7):
                        for u in range(4):
                            if l == 0:
                                dve.wait_ge(S("level_ready"), 28 * w + u + 1)
                                dve.tensor_tensor(TNTT[u][:, 1, :, :], LV[u], eye, ALU.add)
                                b = take(dve, ("W", w, 0, u))
                                give(dve.tensor_tensor(TNTT[u][:, 0, :, :], b[:, 0:T].rearrange("p (a b) -> p a b", a=2), eye, ALU.add),
                                     ("W", w, 0, u))
                            else:
                                b = take(dve, ("TT", w, l, u))
                                half = TNTT[u].rearrange("p a e t -> p (a e t)")
                                lo = 0 if l < 6 else 2 * P
                                emptied(dve, ("TT", w, l - 1, u) if l > 1 else ("W", w, 0, u))
                                give(dve.tensor_tensor(half[:, lo:512], half[:, lo:512], b[:, lo:512], ALU.add), ("TT", w, l, u))
                    for u in range(4):
                        b = take(dve, ("O", w, u))
                        y = YR[:, u, c * P : (c + 1) * P]
                        if w < 2:
                            ins = dve.tensor_copy(y, b[:, 0:P])
                        else:
                            ins = dve.tensor_tensor(y, y, b[:, 0:P], ALU.add)
                        give(ins, ("O", w, u))
                    if w < 2:
                        for u in range(4):
                            j = 4 * d + u
                            b = take(dve, ("ST", w, u))
                            for e in range(2):
                                ps = slice(64 * e, 64 * e + 64)
                                ins = dve.tensor_scalar(ST[ps, j, ps], b[ps, 0:HD], SSC[ps, j : j + 1], None, ALU.mult)
                            give(ins, ("ST", w, u))
                for j in range(2):
                    b = take(dve, ("gmean", j))
                    ys = flat(YR[:, 2 * j : 2 * j + 2, :])
                    for u in range(4):
                        emptied(dve, ("O", 3, u))
                    give(dve.scalar_tensor_tensor(out=ys, in0=b[:, 0:512], scalar=-1.0 / HD, in1=ys, op0=ALU.mult, op1=ALU.add),
                         ("gmean", j))
                for j in range(2):
                    emptied(dve, ("gvar", j))
                link(dve.reciprocal(sq[:, 4:8, :], sq[:, 4:8, :]))
                link(dve.tensor_tensor(YR, YR, sq[:, 4:8, :], ALU.mult))
                for hp in range(4):
                    ins = dve.tensor_scalar(YR[:, hp, :], YR[:, hp, :], V("rw_gn_w_2", hp), V("rw_gn_b_2", hp), ALU.mult, ALU.add)
                link(ins)
                link(dve.tensor_tensor(YR, YR, US[:, 0:4, :], ALU.add))
                for hp in range(4):
                    emptied(dve, ("lg", hp))
                dve.tensor_tensor(YR[:, 0:2, :], YR[:, 0:2, :], G2[0][:, :, :], ALU.mult).then_inc(S("y_rw_ready"), 1)
                dve.tensor_tensor(YR[:, 2:4, :], YR[:, 2:4, :], G2[1][:, :, :], ALU.mult).then_inc(S("y_rw_ready"), 1)

            def branches_out():
                dve.wait_ge(S("gates_ready"), 1)
                for m in range(8):
                    b = take(dve, ("br", 0, m))
                    give(dve.tensor_tensor(MG[:, m, :], GATES[:, m, :], b[:, 0:T], ALU.mult), ("br", 0, m))
                    b = take(dve, ("br", 1, m))
                    give(dve.tensor_tensor(MT[m % 2], GATES[:, 8 + m, :], b[:, 0:T], ALU.mult), ("br", 1, m))
                    emptied(dve, ("br", 1, m))
                    dve.tensor_tensor(MG[:, m, :], MG[:, m, :], MT[m % 2], ALU.add).then_inc(S("merged"), 1)
                residual(("y", 2))

            def top16(scores, scratch, vals, idx):
                n = len(scores)
                for r in range(2):
                    src = scratch if r else scores
                    lo = slice(8 * r, 8 * r + 8)
                    for j in range(n):
                        ins = dve.max(vals[j][:, lo], src[j])
                    link(ins)
                    for j in range(n):
                        ins = dve.max_index(idx[j][:, lo], vals[j][:, lo], src[j])
                        if r == 0:
                            ins = dve.match_replace(scratch[j], vals[j][:, lo], src[j], -3.0e38)
                    link(ins)

            def best_keys(h):
                lists = [(tb, c) for tb in range(2) for c in range(2)]
                top16([SC[:, tb, 2 * h + c, :] for tb, c in lists], [SCR[:, tb, c, :] for tb, c in lists],
                      [TV[:, tb, 2 * h + c, :] for tb, c in lists], [TI[:, tb, 2 * h + c, :] for tb, c in lists])

            def best_sums(tb, heads):
                hs = slice(heads[0], heads[-1] + 1)
                tv = TV[:, tb, :, :].rearrange("p (h c) k -> p h c k", c=2)
                n = len(heads)
                link(dve.tensor_tensor(CAND[:, hs, :].rearrange("p h (a b) -> p h a b", a=16),
                                       tv[:, hs, 0, :].unsqueeze(3).broadcast_to([P, n, 16, 16]),
                                       tv[:, hs, 1, :].unsqueeze(2).broadcast_to([P, n, 16, 16]), ALU.add))
                top16([CAND[:, h, :] for h in heads], [CSCR[:, h, :] for h in heads],
                      [BV[:, h, :] for h in heads], [BP[:, h, :] for h in heads])

            def rows_of(tb):
                link(dve.tensor_copy(TIF[:, tb, :, :], TI[:, tb, :, :]))
                ti = TIF[:, tb, :, :].rearrange("p (h c) k -> p h c k", c=2)
                bp = BP.rearrange("p h e -> p (h e)")
                count = C("count", 16).unsqueeze(1).broadcast_to([P, P, 16])
                for half, (op, n, dst) in enumerate(((ALU.logical_shift_right, 4, E0), (ALU.bitwise_and, 15, E1))):
                    link(dve.tensor_scalar(BI, bp, n, None, op))
                    link(dve.tensor_copy(BF, BI))
                    link(dve.tensor_tensor(EQ, BF.unsqueeze(2).broadcast_to([P, P, 16]), count, ALU.is_equal))
                    eq4 = EQ.rearrange("p (h e) i -> p h e i", h=8)
                    link(dve.tensor_tensor(eq4, eq4, ti[:, :, half, :].unsqueeze(2).broadcast_to([P, 8, 16, 16]), ALU.mult))
                    link(dve.tensor_reduce(dst, EQ, AX.X, ALU.add))
                link(dve.scalar_tensor_tensor(out=E0, in0=E0, scalar=float(N_KEYS), in1=E1, op0=ALU.mult, op1=ALU.add))
                dve.tensor_scalar(EIDX[:, tb, :], E0, float(N_KEYS * N_KEYS - 1), None, ALU.min).then_inc(S("rows_known"), 1)
                if tb:
                    dve.wait_ge(S("gate_exp_ready"), tb)
                    gates(0)
                dve.tensor_tensor(PEX, BV, BV[:, :, 0:1].broadcast_to([P, 8, 16]), ALU.subtract).then_inc(S("gate_in_ready"), 1)

            def gates(tb):
                dve.wait_ge(S("gate_exp_ready"), tb + 1)
                link(dve.tensor_reduce(SUM8[:, 0:8], PEX, AX.X, ALU.add))
                link(dve.reciprocal(SUM8[:, 8:16], SUM8[:, 0:8]))
                link(dve.tensor_tensor(GATE[:, tb, :].rearrange("p (h e) -> p h e", h=8), PEX,
                                       SUM8[:, 8:16].unsqueeze(2).broadcast_to([P, 8, 16]), ALU.mult))

            def experts():
                for h in range(8):
                    emptied(dve, ("sc", h))
                    best_keys(h)
                    best_sums(0, [h])
                rows_of(0)
                for j in range(4):
                    emptied(dve, ("htok", j))
                used = S("rows_used")

                def dots(tb, first, n):
                    q = tb
                    with dve.Fori(0, n) as i:
                        for j in range(8):
                            dve.wait_ge(S(f"row{j}_loaded"), 16 * (16 * q + first + 1) + 16 * i)
                            if j >= 2:
                                dve.wait_ge(used, 8 * (16 * q + first) + j - 1 + 8 * i)
                            dve.tensor_tensor_reduce(JUNK[j % 2], GR[:, j, :], HTOK[:, tb, :], 1.0, 0.0, ALU.mult, ALU.add,
                                                     DSTAGE[:, j : j + 1]).then_inc(used, 1)
                        dve.wait_ge(used, 8 * (16 * q + first + 1) + 8 * i)
                        dve.tensor_copy(DOTS[:, tb, bass.ds(i * 8 + 8 * first, 8)], DSTAGE).then_inc(S("dots_ready"), 1)
                        dve.wait_ge(S("dots_ready"), 16 * tb + first + 1 + i)

                dots(0, 0, 4)
                best_sums(1, list(range(8)))
                dots(0, 4, 4)
                rows_of(1)
                dots(0, 8, 8)
                gates(1)
                dots(1, 0, 16)
                link(dve.memset(ACC, 0.0))
                for tb in range(2):
                    q = 2 + tb
                    dve.wait_ge(S("gelu_ready"), tb + 1)
                    link(dve.tensor_tensor(WT[:, tb, :], WT[:, tb, :], GATE[:, tb, :], ALU.mult))
                    with dve.Fori(0, 16) as i:
                        dve.wait_ge(used, 8 * (16 * q) + 8 * i)
                        dve.tensor_copy(WSTAGE, WT[:, tb, bass.ds(i * 8, 8)]).then_inc(S("wstage"), 1)
                        dve.wait_ge(S("wstage"), 16 * tb + 1 + i)
                        for j in range(8):
                            dve.wait_ge(S(f"row{j}_loaded"), 16 * (16 * q + 1) + 16 * i)
                            if j:
                                dve.wait_ge(used, 8 * (16 * q) + j + 8 * i)
                            dve.scalar_tensor_tensor(out=ACC[:, tb, :], in0=GR[:, j, :], scalar=WSTAGE[:, j : j + 1],
                                                     in1=ACC[:, tb, :], op0=ALU.mult, op1=ALU.add).then_inc(used, 1)
                residual(("back",))

            def ple():
                for m in range(8):
                    b = take(dve, ("pp", m))
                    emptied(dve, ("pg", m))
                    s = view(4096 + T * m, T)
                    give(dve.tensor_tensor(s, s, b[:, 0:T], ALU.mult), ("pp", m))
                    emptied(dve, ("pp", m))
                    ins = dve.tensor_tensor(xT[:, m, :], xT[:, m, :], s, ALU.add)
                    if m % 2:
                        ins.then_inc(x_ready, 1)

            for l in range(2):
                norm(3 * l)
                ffn(2 * l)
                norm(3 * l + 1)
                layer(l)
                norm(3 * l + 2)
                ffn(2 * l + 1)
            norm(6)
            second_in()
            latent()
            recurrence()
            branches_out()
            norm(7)
            experts()
            norm(8)
            ple()
            norm(9)

        @block.gpsimd
        def _(pool):
            chain = Chain(pool_done)
            link = lambda ins: chain.link(pool, ins)

            def keep_before(buf, sem_):
                for a in (0, T):
                    v = buf[:, a : a + P]
                    pool.affine_select(out=v, in_=v, pattern=[[1, P]], compare_op=ALU.is_gt, fill=0.0, base=0,
                                       channel_multiplier=-1).then_inc(sem_, 1)

            for t in range(8 + 1):
                if t < 8:
                    pool.wait_ge(S("softplus_ready"), t + 1)
                    keep_before(ZL[t % 2], S("keep_ready"))
                if t >= 1:
                    emptied(pool, ("z", 0, t - 1))
                    keep_before(PT[(t - 1) % 2], S("stick_ready"))
            residual_done(pool, 4)
            link(pool.memset(FL[0:2, :, :], 1.0))
            link(pool.memset(FR[0:2, :, :], 1.0))
            pool.wait_ge(S("sums_ready"), 2)
            pool.dma_start(FL[0:1, :, :], FG[0:8, 0, :]).then_inc(S("forget_ready"), 16)
            pool.dma_start(FR[1:2, :, :], FG[0:8, 1, :]).then_inc(S("forget_ready"), 16)
            residual_done(pool, 6)
            pool.wait_ge(S("masks_loaded"), 16)
            pool.dma_start(POS[64:96, :], A["positions"].partition_broadcast(32)).then_inc(S("pos_loaded"), 16)
            for w, (d, c) in enumerate(WAVES):
                for l in range(7):
                    for u in range(4):
                        if l == 0:
                            emptied(pool, ("gram", w, u, 0))
                            emptied(pool, ("gram", w, u, 1))
                        else:
                            b, n = fill_of["W", w, l - 1, u]
                            pool.wait_ge(full[b], n)
                            if l == 1:
                                emptied(pool, ("W", w, 0, u))
                        mask = C("level", P, (7 * d + l) * P).unsqueeze(1).broadcast_to([P, 2, P])
                        pool.tensor_tensor(LV[u], M4[u][:, :, 0, :], mask, ALU.mult).then_inc(S("level_ready"), 1)
            used = S("rows_used")
            for h in range(8):
                emptied(pool, ("sc", h))
            def gather(q, table, i, half, fresh):
                tb = q % 2
                stage = STAGE[:, 8 * half : 8 * half + 8]
                if not fresh:
                    row_free = pool.snap(free_rows)
                pool.tensor_copy(stage, EIDX[:, tb, bass.ds(i * 16 + 8 * half, 8)]).then_inc(S("staged"), 1)
                pool.wait_ge(S("staged"), 16 * q + half + 1 + 2 * i)
                for j in range(8):
                    if not fresh:
                        if j:
                            row_free = pool.snap(free_rows)
                        pool.wait_ge(used, row_free)
                        pool.reg_add(free_rows, free_rows, 1)
                    pool.indirect_dma_start(out=GR[:, j, :], out_offset=None, in_=A[table][0],
                                            in_offset=bass.IndirectOffsetOnAxis(ap=stage[:, j : j + 1], axis=0))\
                        .then_inc(S(f"row{j}_loaded"), 16)

            pool.wait_ge(S("rows_known"), 1)
            free_rows = pool.alloc_register("free_rows")
            pool.reg_mov(free_rows, 1)
            gather(0, "peer_u_2", 0, 0, True)
            gather(0, "peer_u_2", 0, 1, False)
            with pool.Fori(1, 8) as i:
                for half in range(2):
                    gather(0, "peer_u_2", i, half, False)
            pool.wait_ge(S("rows_known"), 2)
            for q, table in ((1, "peer_u_2"), (2, "peer_v_2"), (3, "peer_v_2")):
                with pool.Fori(0, 8) as i:
                    for half in range(2):
                        gather(q, table, i, half, False)
            pool.wait_ge(xn_ready, 10 * KC)
            pool.dma_start(rows(out), xn[:, :, :]).then_inc(S("stored"), 16)
            pool.wait_ge(S("stored"), 16)


def kernel(**inputs):
    import concourse.bacc as bacc
    from concourse.bass_utils import run_bass_kernel_spmd

    arrays = {}
    take = lambda name: np.ascontiguousarray(np.asarray(inputs[name]))
    arrays["xT"] = np.ascontiguousarray(take("x")[0].T)
    arrays["pT"] = np.ascontiguousarray(take("p_2")[0, 0].T)
    arrays["positions"] = take("positions_2")[0]
    keys = take("peer_sub_keys_2")[0].reshape(16, N_KEYS, P)
    arrays["sub_keys_t"] = np.ascontiguousarray(keys.transpose(0, 2, 1))
    arrays["con"] = constants()
    arrays["vec"] = pack_vectors(inputs)
    for name in ("ffn1_w_gate", "ffn1_w_up", "ffn1_w_down", "ffn2_w_gate", "ffn2_w_up", "ffn2_w_down", "w_in_ab",
                 "w_in_cd", "b_f", "w_out", "w_in_2", "rw_w2_2", "rw_a2_2", "rw_g2_2", "mla_w_qup_2", "mla_w_kvup_2",
                 "w_br_rwkv_2", "w_br_mla_2", "w_out_2", "peer_w_q_2", "peer_u_2", "peer_v_2", "w_ple_gate_2",
                 "w_ple_proj_2"):
        arrays[name] = take(name)

    nc = bacc.Bacc("TRN2", target_bir_lowering=False, num_devices=1)
    aps = {
        name: nc.dram_tensor(name, a.shape, mybir.dt.from_np(a.dtype), kind="ExternalInput").ap()
        for name, a in arrays.items()
    }
    out = nc.dram_tensor("out", (D, T), F32, kind="ExternalOutput").ap()
    build(nc, aps, out)
    r = run_bass_kernel_spmd(nc, [arrays], core_ids=[0])
    return np.ascontiguousarray(r.results[0]["out"].T)[None]
```

```python
from contextlib import ExitStack

import concourse.bass as bass
import numpy as np
from concourse import mybir

F32 = mybir.dt.float32
U32 = mybir.dt.uint32
F32R = mybir.dt.float32r
I32 = mybir.dt.int32
ACT = mybir.ActivationFunctionType
ALU = mybir.AluOpType
AX = mybir.AxisListType

P = 128
T = 256
D = 1024
KC = D // P
HD = 64
DFF = 2816
GROUPS = DFF // 256
CHUNKS = DFF // P
EPS = 1e-6
N_KEYS = 128
NEG = -1.0e30
DECAY = float(np.exp(-0.5))
GN_EPS = 64e-5

VEC = {}
_n = 0
for _name, _w in (
    ("norm_ffn1", 16), ("norm_mix", 16), ("norm_ffn2", 16), ("g_mix_2", 8), ("g_ffn_2", 8), ("g_ple_2", 8),
    ("g_final_2", 8), ("rw_mu_2", 15), ("rw_w0_2", 8), ("rw_a0_2", 8), ("rw_k_k_2", 4), ("rw_k_a_2", 4),
    ("rw_r_k_2", 4), ("rw_gn_w_2", 4), ("rw_gn_b_2", 4), ("mla_g_qa_2", 2), ("mla_g_kva_2", 1),
    ("g_q_b", 1), ("g_k_b", 1), ("g_q_c", 1), ("g_k_c", 1), ("g_q_d", 1), ("g_k_d", 1),
):
    VEC[_name] = _n
    _n += _w
NVEC = _n

CON = {}
_n = 0
for _name, _w in (
    ("ones", 128), ("eps", 4), ("ident", 128), ("heads", 128), ("suffix", 128), ("after", 128), ("causal", 384),
    ("dilated", 384), ("cos", 256), ("sin", 256), ("turn", 128), ("turn_mla", 32), ("seen", 512),
    ("level", 2 * 7 * 128), ("inv", 1), ("count", 16), ("one", 1),
):
    CON[_name] = _n
    _n += _w
NCON = _n
NFIRST = CON["ident"]


def constants():
    c = np.zeros((P, NCON), np.float32)

    def put(name, value):
        value = np.asarray(value, np.float32)
        c[: value.shape[0], CON[name] : CON[name] + value.shape[1]] = value

    i = np.arange(P)
    row, col = i[:, None], i[None, :]
    put("ident", row == col)
    put("ones", np.ones((P, P)))
    put("heads", (row // HD) == (col // HD))
    put("suffix", -8.0 * (row >= col))
    put("after", -8.0 * np.ones((P, P)))
    tri = np.where(col <= row, 0.0, NEG)
    put("causal", np.concatenate([tri, np.zeros((P, P)), tri], 1))

    def branches(dist):
        n = ((dist >= 0) & (dist <= 128)).astype(int) + ((dist >= 0) & (dist % 4 == 0)) + ((dist >= 0) & (dist % 16 == 0))
        return np.where(n > 0, 8.0 * np.log(np.maximum(n, 1)), NEG)

    put("dilated", np.concatenate([branches(row - col), branches(128 + row - col), branches(row - col)], 1))
    inv = (1.0 / (np.float32(10000.0) ** (np.arange(0, HD, 2, dtype=np.float32) / np.float32(HD)))).astype(np.float32)
    ang = (np.arange(T, dtype=np.float32)[:, None] * inv[None, :]).astype(np.float32).astype(np.float64)
    put("cos", np.tile(np.cos(ang).T, (4, 1)))
    put("sin", np.tile(np.sin(ang).T, (4, 1)))
    turn = np.zeros((P, P))
    for h in (0, HD):
        for j in range(32):
            turn[h + 32 + j, h + j] = -1.0
            turn[h + j, h + 32 + j] = 1.0
    put("turn", turn)
    turn = np.zeros((P, 32))
    for j in range(16):
        turn[64 + 16 + j, j] = -1.0
        turn[64 + j, 16 + j] = 1.0
    put("turn_mla", turn)
    put("seen", np.concatenate([row < col, row <= col, row > col, row >= col], 1))
    level = np.zeros((P, 2, 7, P))
    for l in range(7):
        n = 1 << l
        same = (row // (2 * n)) == (col // (2 * n))
        level[:, 0, l] = same & (row // n < col // n)
        level[:, 1, l] = same & (row // n > col // n)
    put("level", level.reshape(P, -1))
    inv2 = (np.float32(10000.0) ** (-np.arange(0, 32, 2, dtype=np.float32) / np.float32(32))).astype(np.float32)
    v = np.zeros((P, 1))
    v[64:96, 0] = np.tile(inv2, 2)
    put("inv", v)
    put("eps", np.tile(np.array([[EPS, GN_EPS, 1e-24, 0.0]]), (P, 1)))
    put("count", np.tile(np.arange(16)[None, :], (P, 1)))
    put("one", np.ones((P, 1)))
    return c


def pack_vectors(inputs):
    v = np.zeros((P, NVEC), np.float32)
    for name, at in VEC.items():
        a = np.asarray(inputs[name])
        if name.startswith("g_") and a.size == HD:
            v[:HD, at : at + 1] = a.reshape(HD, 1)
            v[HD:, at : at + 1] = a.reshape(HD, 1)
        else:
            w = a.size // P
            v[:, at : at + w] = a.reshape(w, P).T
    return v


def build(nc, A, out):
    ctx = ExitStack()
    with ctx:
        sb = lambda name, shape, dt=F32: ctx.enter_context(nc.sbuf_tensor(name + "_sb", shape, dt))
        sem = lambda name: ctx.enter_context(nc.semaphore(name))

        xT = sb("xT", [P, KC, T])
        xn_at = nc.sbuf_base
        xn = sb("xn", [P, KC, T])
        sq_at = nc.sbuf_base
        sq = sb("sq", [P, KC, T])
        RING = 6
        ring = sb("ring", [P, RING, 2048])
        con = sb("con", [P, NCON])
        vec = sb("vec", [P, NVEC])
        rstd = sb("rstd", [P, T])
        std = sb("std", [P, T])
        sgate = sb("sgate", [P, 2, T])
        hT = sb("hT", [P, 2, T])
        small = sb("small", [P, 256])
        ARENA = 28416
        arena_at = nc.sbuf_base
        arena = sb("arena", [P, ARENA])
        bank = [ctx.enter_context(nc.psum_tensor(f"bank{b}", [P, 512], F32)) for b in range(8)]

        def view(at, *shape, dt=None):
            n = int(np.prod(shape))
            assert at + n <= ARENA
            v = arena[:, at : at + n]
            if dt is not None:
                v = v.bitcast(dt)
            names = "abcde"[: len(shape)]
            if len(shape) == 1:
                return v
            return v.rearrange(f"p ({' '.join(names)}) -> p {' '.join(names)}", **{n_: s for n_, s in zip(names[1:], shape[1:])})

        C = lambda name, w, off=0: con[:, CON[name] + off : CON[name] + off + w]
        V = lambda name, c=0: vec[:, VEC[name] + c : VEC[name] + c + 1]
        ident = C("ident", P)
        eps = lambda j: C("eps", 1, j)

        loaded_x, loaded_c, loaded_v = sem("loaded_x"), sem("loaded_c"), sem("loaded_v")
        slot_loaded = [sem(f"slot{i}_loaded") for i in range(RING)]
        slot_free = sem("slot_free")
        sq_ready, xn_ready = sem("sq_ready"), sem("xn_ready")
        x_ready, y_ready = sem("x_ready"), sem("y_ready")
        gu_ready, silu_ready, h_ready = sem("gu_ready"), sem("silu_ready"), sem("h_ready")
        full = [sem(f"bank{b}_full") for b in range(8)]
        free = [sem(f"bank{b}_free") for b in range(8)]
        dve_done, act_done, pool_done = sem("dve_done"), sem("act_done"), sem("pool_done")
        named = {}

        def S(name):
            if name not in named:
                named[name] = sem(name)
            return named[name]

        SCALE = {0: 0.125, 1: 0.125, 2: 96.0 ** -0.5}

        fast = lambda name, shape, at_: nc.alloc_sbuf_tensor_at(name + "_sb", shape, F32R, offset=at_)
        hi_ready, split_ready, pair_used = sem("hi_ready"), sem("split_ready"), sem("pair_used")
        xh_ready, hraw_ready, hh_ready = sem("xh_ready"), sem("hraw_ready"), sem("hh_ready")
        xh = fast("xh", [P, KC, T], xn_at)
        xl = fast("xl", [P, KC, T], sq_at)
        PAIR = {("gate", 0): 8192, ("up", 0): 12288, ("gate", 1): 0, ("up", 1): 4096, ("down", 0): 16384, ("down", 1): 16384}
        parts = fast("parts", [P, 26112], arena_at)
        whi = lambda kind, g: parts[:, PAIR[kind, g % 2] : PAIR[kind, g % 2] + 2048]
        wlo = lambda kind, g: parts[:, PAIR[kind, g % 2] + 2048 : PAIR[kind, g % 2] + 4096]
        HH = fast("h_high", [P, 2, T], arena_at + 4 * 20480)
        HL = fast("h_low", [P, 2, T], arena_at + 4 * 20992)
        FFN_SLOTS = 3 * GROUPS
        QKV_SLOTS = 12
        SPLIT0, _split = {}, 0
        for _phase, _count in ((("ffn", 0), FFN_SLOTS), (("qkv", 0), QKV_SLOTS), (("ffn", 1), FFN_SLOTS),
                               (("ffn", 2), FFN_SLOTS), (("qkv", 1), QKV_SLOTS), (("ffn", 3), FFN_SLOTS)):
            SPLIT0[_phase] = _split
            _split += _count
        qhi = lambda s: parts[:, (22016, 8192, 12288)[s % 3] :][:, 0:2048]
        qlo = lambda s: parts[:, (24064, 10240, 14336)[s % 3] :][:, 0:2048]

        def splits_after(c):
            g = c // 2
            return [("down", g)] if c % 2 == 0 else [("gate", g + 2), ("up", g + 2)] if g + 2 < GROUPS else []

        def place(kind, g):
            if kind == "down":
                return 3 * g + 4 if g < GROUPS - 1 else FFN_SLOTS - 1
            return (max(3 * g - 1, 0)) + (kind == "up")

        fill_of, fills = {}, [0] * 8

        def plan(label, b):
            fills[b] += 1
            assert label not in fill_of, label
            fill_of[label] = (b, fills[b])

        def fill_begin(pe, label):
            b, n = fill_of[label]
            if n > 1:
                pe.wait_ge(free[b], n - 1)
            return bank[b]

        def fill_end(ins, label):
            ins.then_inc(full[fill_of[label][0]], 1)

        def take(eng, label):
            b, n = fill_of[label]
            eng.wait_ge(full[b], n)
            return bank[b]

        def give(ins, label):
            ins.then_inc(free[fill_of[label][0]], 1)

        def emptied(eng, label):
            b, n = fill_of[label]
            eng.wait_ge(free[b], n)

        class Chain:

            def __init__(self, s):
                self.s, self.n = s, 0

            def link(self, eng, ins):
                ins.then_inc(self.s, 1)
                self.n += 1
                eng.wait_ge(self.s, self.n)

        at = {}
        k = 0
        for l in range(2):
            at["ffn", 2 * l] = k; k += 3 * GROUPS
            at["qkv", l] = k; k += 12
            at["wo", l] = k; k += 4
            at["ffn", 2 * l + 1] = k; k += 3 * GROUPS
        at["in2"] = k; k += 10
        at["mla"] = k; k += 2
        at["gates"] = k; k += 8
        at["br"] = k; k += 4
        at["wo", 2] = k; k += 4
        at["wq"] = k; k += 8
        at["pp"] = k; k += 1
        at["pg"] = k; k += 4
        split_at = [(at[phase], FFN_SLOTS if phase[0] == "ffn" else QKV_SLOTS) for phase in SPLIT0]

        def freed(k):
            before = sum(min(max(k - a, 0), n) for a, n in split_at)
            if any(a <= k < a + n for a, n in split_at):
                return split_ready, before + 1
            return slot_free, k - before + 1

        slot = lambda k, *shape: ring[:, k % RING, 0 : int(np.prod(shape))].rearrange("p (k n) -> p k n", k=shape[0])

        ffn_w = [
            (A["ffn1_w_gate"][0], A["ffn1_w_up"][0], A["ffn1_w_down"][0]),
            (A["ffn2_w_gate"][0], A["ffn2_w_up"][0], A["ffn2_w_down"][0]),
            (A["ffn1_w_gate"][1], A["ffn1_w_up"][1], A["ffn1_w_down"][1]),
            (A["ffn2_w_gate"][1], A["ffn2_w_up"][1], A["ffn2_w_down"][1]),
        ]
        norm_g = [("norm_ffn1", 0), ("norm_mix", 0), ("norm_ffn2", 0), ("norm_ffn1", 8), ("norm_mix", 8),
                  ("norm_ffn2", 8), ("g_mix_2", 0), ("g_ffn_2", 0), ("g_ple_2", 0), ("g_final_2", 0)]
        rows = lambda w: w.rearrange("(k p) n -> p k n", p=P)

        QK = view(0, 16, T)
        VT = view(4096, 2, D)
        MIX = view(6144, KC, T)
        SM = [view(8192 + 512 * j, 512) for j in range(2)]
        PR = [view(a, 512) for a in (9216, 9728, 15872)]
        PT = [view(10240 + 512 * j, 512) for j in range(2)]
        ZR = [view(11264 + 512 * j, 512) for j in range(2)]
        ZL = [view(12288 + 512 * j, 512) for j in range(2)]
        HSQ = [view(26112 + 512 * j, 512) for j in range(2)]
        HSTD = [view(27136 + 512 * j, 512) for j in range(2)]
        ROT = view(6144, 512)
        WF = view(ARENA - KC * 8, KC, 8)
        FG = view(16448, 4, T)
        FL = view(17472, 8, T)
        FR = view(19520, 8, T)
        MX, NM, RS, RI = (small[:, 128 + 6 * j : 134 + 6 * j] for j in range(4))

        unit_base = {0: 0, 1: 8, 2: 24}

        qk_pairs = {
            0: [(4, "g_q_b", 1), (6, "g_q_b", 1), (12, "g_k_b", 1), (14, "g_k_b", 1)],
            1: [(4, "g_q_d", 1), (6, "g_q_d", 1), (12, "g_k_d", 1), (14, "g_k_d", 1),
                (0, "g_q_c", 0), (2, "g_q_c", 0), (8, "g_k_c", 0), (10, "g_k_c", 0)],
        }
        QK_STEPS = (4, 6, 12, 14, 0, 2, 8, 10)

        def chunks_of(l, s):
            if s < 4:
                return [("v", l, 2 * s), ("v", l, 2 * s + 1)]
            return [("qk", l, QK_STEPS[s - 4]), ("qk", l, QK_STEPS[s - 4] + 1)]

        def norms_at(l, s):
            n = len(qk_pairs[l])
            return [i for i in ([s - 5] if s < 11 else [6, 7]) if 0 <= i < n]

        def turns_at(s):
            return [s - 7] if 0 <= s - 7 < 4 else []

        def plan_norm(n):
            plan(("ssq", n), 7)

        def plan_layer(l):
            for s in range(QKV_SLOTS):
                for j, label in enumerate(chunks_of(l, s)):
                    plan(label, 4 + (2 * s + j) % 3)
                for i in norms_at(l, s):
                    plan(("hssq", l, i), i % 2)
                for i in turns_at(s):
                    plan(("rot", l, i), 2 + i % 2)
            if l == 1:
                plan(("forget", l), 7)
            if l == 0:
                for t in range(8 + 2):
                    if t < 8:
                        plan(("z", l, t), 4 + t % 2)
                    if t >= 2 and t % 2 == 0:
                        plan(("o", l, (t - 2) // 2), (t - 2) // 2 % 4)
                plan_soft(l, 8, 4)
            else:
                plan_soft(l, 16, 0)
            for m in range(4):
                plan(("y", l, m), m)

        def plan_soft(l, n, pair0):
            for t in range(n + 3):
                if t < n:
                    plan(("s", l, t), 4 + t % 2)
                if 2 <= t < n + 2:
                    plan(("pt", l, t - 2), 6 + t % 2)
                if t >= 3 and t % 2:
                    plan(("o", l, pair0 + (t - 3) // 2), (pair0 + (t - 3) // 2) % 4)

        US = view(0, 15, T)
        GATES = view(3840, 16, T)
        YM = view(7936, 4, T)
        YR = view(8960, 4, T)
        U0 = view(9984, 15, T + 2)
        CQ = view(13856, 2, T)
        CKV = view(14368, T)
        KR = view(14624, T)
        CQN = view(14880, 2, T)
        CKVN = view(15392, T)
        QM = view(15648, 8, T)
        KM = view(17696, 8, T)
        VM = view(19744, 2, 512)
        COSM = view(20768, T)
        SINM = view(21024, T)
        PR2 = [view(21280 + 512 * j, 512) for j in range(3)]
        PT2 = [view(23328 + 512 * j, 512) for j in range(2)]
        TMPM = view(24352, 8, T)
        ANG = view(26400, T)
        ANG2 = view(26656, T)
        POS = view(26912, T, dt=I32)
        POSF = view(27168, T)
        AR = view(9984, 8, 2, 2, P)
        BT = view(14080, 8, 2, P)
        KT = view(16128, 8, 2, P)
        CF = view(18176, 8, 2, P)
        CE = view(20224, 8, 2, P)
        RATE = view(22272, 8, T)
        KD = view(24320, 8, T)
        KK = view(26368, 4, T)
        G2 = [sgate, hT]
        VTM = view(27392, 2, 512)
        BTM = sq[:, 0:4, :].rearrange("p a b -> p (a b)").rearrange("p (d n) -> p d n", d=2)
        KTM = sq[:, 4:8, :].rearrange("p a b -> p (a b)").rearrange("p (d n) -> p d n", d=2)
        UNIT = 18176
        M4 = [view(UNIT + 2048 * u, 2, 4, P) for u in range(4)]
        LV = [view(UNIT + 2048 * u + 1024, 2, P) for u in range(4)]
        WW = [view(UNIT + 2048 * u + 1280, 2, P) for u in range(4)]
        TNTT = [view(UNIT + 2048 * u + 1536, 2, 2, P) for u in range(4)]
        SSC = small[:, 16:24]
        REF = small[:, 24:40].rearrange("p (a c) -> p a c", c=2)
        XX = [view(26368 + 128 * u, P) for u in range(4)]
        UU = [view(26880 + 128 * u, P) for u in range(4)]
        ST = view(1024, 8, P)
        LORA = [view(8960, 512), view(9472, 512), view(27648, 512)]
        MG = view(9984, 8, T)
        MT = view(12032, 8, T)
        WAVES = [(0, 0), (1, 1), (0, 1), (1, 0)]

        HTOK = view(0, 2, D)
        ACC = view(2048, 2, D)
        QP = view(4096, 16, T)
        SC = [view(8192, 16, P), view(16384, 16, P)]
        GB = 8
        GR = view(4096, GB, D)
        SCR = view(12288, 4, P)
        TV = view(12800, 2, 16, 16)
        TI = view(13312, 2, 16, 16, dt=U32)
        TIF = view(13824, 2, 16, 16)
        CAND = view(15104, 2, 256)
        CSCR = view(15616, 2, 256)
        BV = view(19200, 8, 16)
        BP = view(19328, 8, 16, dt=U32)
        BI = view(18432, 2, P, dt=U32)
        BF = view(18688, 2, P)
        EQ = view(19712, 2, 32, 16)
        ACC2 = view(20736, D)
        E0 = view(21760, P)
        E1 = view(21888, P)
        EIDX = view(22016, 2, P, dt=U32)
        GATE = view(22272, 2, P)
        DOTS = view(22528, 2, P)
        WT = view(22784, 2, P)
        PEX = view(23040, 8, 16)
        STAGE = sb("stage", [P, 16], U32)
        DSTAGE = small[:, 80:88]
        WSTAGE = small[:, 96:104]
        SUM8 = small[:, 112:128]
        JUNK = [view(23168 + D * j, D) for j in range(2)]
        PIN = view(25216, 2, T)
        KEYS = view(25728, 16, P)
        PLE = view(25728, 8, T)

        plan_norm(0)
        plan_norm(1)
        plan_layer(0)
        plan_norm(2)
        plan_norm(3)
        plan_norm(4)
        plan_layer(1)
        plan_norm(5)
        plan_norm(6)
        for m in range(19):
            plan(("u", m), m % 4)
        plan(("mssq", 0), 4)
        plan(("mssq", 1), 5)
        for h in range(8):
            plan(("mq", h), h % 4)
        for h in range(8):
            plan(("mk", h), h % 4)
        for j in range(2):
            plan(("mv", j), 4 + j)
        for m in range(0, 2):
            plan(("gate", m), m % 4)
        for j in range(5):
            plan(("mrot", j), 6 + j % 2)
        for m in range(2, 6):
            plan(("gate", m), m % 4)
        plan_soft(2, 8, 0)
        for d in range(2):
            for hp in range(4):
                plan(("lw", d, hp), 0 + hp % 4)
                plan(("la", d, hp), 4 + hp % 2)
        for hp in range(4):
            plan(("lg", hp), 6 + hp % 2)
        for m in range(6, 8):
            plan(("gate", m), 6 + m % 2)
        for j in range(2):
            plan(("kkss", j), 4 + j)
        for j in range(4):
            plan(("vtm", j), 0 + j)
        for m in range(8, 16):
            plan(("gate", m), 6 + m % 2)
        for j in range(8):
            plan(("bkt", j), 4 + j % 4)
        for j in range(2):
            plan(("bonus", j), j)
        for w in range(4):
            for u in range(4):
                for e in range(2):
                    plan(("gram", w, u, e), 4 * e + u)
            for l in range(7):
                for u in range(4):
                    plan(("W", w, l, u), u)
                if l:
                    for u in range(4):
                        plan(("TT", w, l, u), 4 + u)
            for u in range(4):
                plan(("X", w, u), u)
            for u in range(4):
                plan(("U", w, u), 4 + u)
            for u in range(4):
                plan(("O", w, u), u)
            if w < 2:
                for u in range(4):
                    plan(("ST", w, u), 4 + u)
        for j in range(2):
            plan(("gmean", j), j)
        for j in range(2):
            plan(("gvar", j), 2 + j)
        for m in range(8):
            plan(("br", 1, m), 4 + m % 4)
        for m in range(8):
            plan(("br", 0, m), m % 4)
        for m in range(4):
            plan(("y", 2, m), m)
        plan_norm(7)
        for h in range(8 + 1):
            if h < 8:
                plan(("pq", 2 * h), 2 * h % 4)
                plan(("pq", 2 * h + 1), (2 * h + 1) % 4)
            if h:
                plan(("sc", h - 1), 4 + (h - 1) % 2)
        for j in range(4):
            plan(("htok", j), 6 + j % 2)
        for m in range(8):
            plan(("pp", m), m % 4)
        for j in range(4):
            plan(("back", j), 4 + j)
        plan_norm(8)
        for m in range(8):
            plan(("pg", m), m % 4)
        plan_norm(9)

        def residual_done(eng, n, pairs=range(4)):
            for m in pairs:
                if n in (1, 3, 4, 6, 9):
                    eng.wait_ge(x_ready, 4 * {1: 0, 3: 1, 4: 2, 6: 3, 9: 4}[n] + m + 1)
                elif n:
                    emptied(eng, {2: ("y", 0, m), 5: ("y", 1, m), 7: ("y", 2, m), 8: ("back", m)}[n])

        block = ctx.enter_context(nc.Block())

        @block.sync
        def _(sp):
            def fetch(k, dst, src, i=0, wait=True):
                if wait and k >= RING:
                    who, n = freed(k - RING)
                    sp.wait_ge(who, n + RING * i)
                sp.dma_start(dst, src).then_inc(slot_loaded[k % RING], 16)

            def ffn(f):
                gate, up, down = ffn_w[f]

                def part(kind, g, i=0):
                    k = at["ffn", f] + place(kind, g)
                    n0 = i * 512 + g * 256
                    if kind == "down":
                        fetch(k, slot(k, 2, D), down[bass.ds(n0, 256), :].rearrange("(k p) n -> p k n", p=P), i)
                    else:
                        fetch(k, slot(k, KC, 256), rows(gate if kind == "gate" else up)[:, :, bass.ds(n0, 256)], i)

                def triple(g, i=0):
                    part("gate", g, i)
                    part("up", g, i)
                    part("down", g - 1, i)

                for g in range(2):
                    part("gate", g)
                    part("up", g)
                part("down", 0)
                triple(2)
                with sp.Fori(0, (GROUPS - 3) // 2) as i:
                    triple(3, i)
                    triple(4, i)
                part("down", GROUPS - 1)

            def square(k0, w, n):
                for s in range(n):
                    fetch(k0 + s, slot(k0 + s, KC, 256), rows(w)[:, :, s * 256 : (s + 1) * 256])

            sp.wait_ge(loaded_x, 16)
            for l, w_in in ((0, A["w_in_ab"][0]), (1, A["w_in_cd"][0])):
                ffn(2 * l)
                for s in range(QKV_SLOTS):
                    n0 = 2 * D + 256 * s if s < 4 else QK_STEPS[s - 4] * P
                    fetch(at["qkv", l] + s, slot(at["qkv", l] + s, KC, 256), rows(w_in)[:, :, n0 : n0 + 256])
                square(at["wo", l], A["w_out"][l], 4)
                ffn(2 * l + 1)
            w2 = A["w_in_2"][0]
            cols = [(256 * s, 256 * s + 256) for s in range(9)] + [(2304, 2336)]
            for s, (a, b) in enumerate(cols):
                k = at["in2"] + s
                fetch(k, slot(k, KC, b - a), rows(w2)[:, :, a:b])
            k = at["mla"]
            fetch(k, slot(k, 2, 768), rows(A["mla_w_qup_2"][0]))
            fetch(k + 1, slot(k + 1, 1, 1024), rows(A["mla_w_kvup_2"][0]))
            for s in range(8):
                k = at["gates"] + s
                fetch(k, slot(k, KC, 256), rows(w2)[:, :, 2336 + 256 * s : 2592 + 256 * s])
            k = at["br"]
            for j, w in enumerate((A["w_br_mla_2"][0], A["w_br_rwkv_2"][0])):
                for s in range(2):
                    fetch(k + 2 * j + s, slot(k + 2 * j + s, 4, 512), rows(w)[:, :, s * 512 : (s + 1) * 512])
            square(at["wo", 2], A["w_out_2"][0], 4)
            square(at["wq"], A["peer_w_q_2"][0], 8)
            k = at["pp"]
            fetch(k, slot(k, 2, 1024), rows(A["w_ple_proj_2"][0]))
            square(at["pg"], A["w_ple_gate_2"][0], 4)
            for m in range(4):
                sp.wait_ge(xn_ready, KC * 9 + 2 * m + 2)
                sp.dma_start(rows(out)[:, 2 * m : 2 * m + 2, :], xn[:, 2 * m : 2 * m + 2, :]).then_inc(S("stored"), 16)
            sp.wait_ge(S("stored"), 4 * 16)

        @block.tensor
        def _(pe):
            owed = [0]
            owed_pairs = [0]

            def mm(dst, lhsT, rhs, start, stop_, loose=False):
                return pe.matmul(dst, lhsT, rhs, start=start, stop=stop_, skip_group_check=loose)

            def mm3(dst, w_hi, w_lo, x_hi, x_lo, start, stop_, loose=False):
                first = mm(dst, w_hi, x_hi, start, False, loose)
                mm(dst, w_lo, x_hi, False, False, loose)
                return first, mm(dst, w_hi, x_lo, False, stop_, loose)

            def release(ins):
                assert not (owed[0] and owed_pairs[0])
                for n, who in ((owed, slot_free), (owed_pairs, pair_used)):
                    if n[0]:
                        ins.then_inc(who, n[0])
                        n[0] = 0

            def have(k, i=0):
                pe.wait_ge(slot_loaded[k % RING], 16 * (k // RING + 1) + 16 * i)

            def norm(n):
                dst = fill_begin(pe, ("ssq", n))
                for k in range(KC):
                    if k % 2 == 0:
                        pe.wait_ge(sq_ready, 4 * n + k // 2 + 1)
                    ins = mm(dst[:, 0:T], C("ones", P), sq[:, k, :], k == 0, k == KC - 1)
                    if k == 0:
                        release(ins)
                fill_end(ins, ("ssq", n))

            def ffn(f, n):
                base, base_s = CHUNKS * f, SPLIT0["ffn", f]

                def gate_up(c, i):
                    b, s, g = bank[4 + c % 2], c % 2, c // 2
                    if c >= 2:
                        pe.wait_ge(hraw_ready, base + c - 1 + 4 * i)
                    for j, kind in enumerate(("gate", "up")):
                        if s == 0:
                            pe.wait_ge(split_ready, base_s + place(kind, g) + 1 + 6 * i)
                        hi = whi(kind, g).rearrange("p (k n) -> p k n", k=KC)
                        lo = wlo(kind, g).rearrange("p (k n) -> p k n", k=KC)
                        cols = slice(s * P, (s + 1) * P)
                        for kk in range(KC):
                            if c == 0 and j == 0:
                                pe.wait_ge(xn_ready, KC * n + kk + 1)
                            _, ins = mm3(b[:, j * T : (j + 1) * T], hi[:, kk, cols], lo[:, kk, cols],
                                         xh[:, kk, :], xl[:, kk, :], kk == 0, kk == KC - 1)
                        if s == 1 and j == 0:
                            ins.then_inc(pair_used, 1)
                    ins.then_inc(gu_ready, 1)
                    if s == 1:
                        owed_pairs[0] += 1

                def down(c, i):
                    g = c // 2
                    if c % 2 == 0:
                        pe.wait_ge(split_ready, base_s + place("down", g) + 1 + 6 * i)
                    pe.wait_ge(h_ready, base + c + 1 + 4 * i)
                    hi = whi("down", g).rearrange("p (k n) -> p k n", k=2)[:, c % 2, :]
                    lo = wlo("down", g).rearrange("p (k n) -> p k n", k=2)[:, c % 2, :]
                    for m in range(KC):
                        cols = slice(m * P, (m + 1) * P)
                        first, ins = mm3(bank[m // 2][:, (m % 2) * T : (m % 2 + 1) * T], hi[:, cols], lo[:, cols],
                                         HH[:, c % 2, :], HL[:, c % 2, :], c == 0 and m % 2 == 0, c == CHUNKS - 1, loose=True)
                        if m == 0:
                            release(first)
                        if c == CHUNKS - 1 and m % 2:
                            ins.then_inc(y_ready, 1)
                    if c == CHUNKS - 1:
                        owed_pairs[0] += 1
                    elif c % 2 == 1:
                        ins.then_inc(pair_used, 1)

                def group(g, i=0):
                    for s in range(2):
                        c = 2 * g + s
                        gate_up(c, i)
                        if c > 0:
                            down(c - 1, i)

                group(0)
                group(1)
                with pe.Fori(0, (GROUPS - 3) // 2) as i:
                    group(2, i)
                    group(3, i)
                group(GROUPS - 1)
                down(CHUNKS - 1, 0)

            def out_product(l, n_wait, src):
                for m in range(KC):
                    k = at["wo", l] + m // 2
                    b = fill_begin(pe, ("y", l, m // 2)) if m % 2 == 0 else bank[fill_of["y", l, m // 2][0]]
                    if m % 2 == 0:
                        have(k)
                    for kk in range(KC):
                        if m == 0:
                            n_wait(kk)
                        ins = mm(b[:, (m % 2) * T : (m % 2 + 1) * T], slot(k, KC, 256)[:, kk, (m % 2) * P : (m % 2 + 1) * P],
                                 src[:, kk, :], kk == 0, kk == KC - 1)
                        if kk == 0:
                            release(ins)
                    if m % 2:
                        fill_end(ins, ("y", l, m // 2))
                        owed[0] += 1

            def soft(l, n, pair0, q_of, k_of, v_of, both, extra=None):
                base = unit_base[l]
                for t in range(n + 3):
                    if t < n:
                        b = fill_begin(pe, ("s", l, t))
                        if both:
                            for qb in range(2):
                                ins = mm(b[:, qb * T : (qb + 1) * T], q_of(t)[:, qb * P : (qb + 1) * P], k_of(t), True, True)
                        else:
                            for a, w, qb in ((0, P, 0), (P, T, 1)):
                                ext = extra is not None and extra(t)
                                ins = mm(b[:, a : a + w], q_of(t)[:, qb * P : (qb + 1) * P], k_of(t)[:, 0:w], True, not ext)
                                if ext:
                                    ins = mm(b[:, a : a + w], FL[0:2, t, qb * P : (qb + 1) * P], FR[0:2, t, 0:w], False, True)
                        fill_end(ins, ("s", l, t))
                    if 2 <= t < n + 2:
                        u = t - 2
                        b = fill_begin(pe, ("pt", l, u))
                        pe.wait_ge(S("weights_ready"), base + u + 1)
                        pr = (PR2 if both else PR)[u % 3]
                        moves = ((0, 0), (P, 2 * P), (2 * P, P), (3 * P, 3 * P)) if both else ((0, 0), (P, P), (2 * P, 2 * P))
                        for src, dst in moves:
                            ins = pe.transpose(b[:, dst : dst + P], pr[:, src : src + P], ident)
                        fill_end(ins, ("pt", l, u))
                    if t >= 3:
                        u = t - 3
                        pair = ("o", l, pair0 + u // 2)
                        b = fill_begin(pe, pair) if u % 2 == 0 else bank[fill_of[pair][0]]
                        emptied(pe, ("pt", l, u))
                        ptb = (PT2 if both else PT)[u % 2]
                        o = b[(u % 2) * HD : (u % 2 + 1) * HD, 0:T]
                        mm(o, v_of(u, 0), ptb[:, 0:T], True, False)
                        if both:
                            ins = mm(o, v_of(u, 1), ptb[:, T : 2 * T], False, True)
                        else:
                            ins = mm(o[:, P:T], v_of(u, 1), ptb[:, T : T + P], False, True)
                        if u % 2:
                            fill_end(ins, pair)


            head = lambda buf, c0, h: buf[(h % 2) * HD : (h % 2 + 1) * HD, c0 + h // 2, :]

            def stick():
                for t in range(8 + 2):
                    if t < 8:
                        b = fill_begin(pe, ("z", 0, t))
                        q, k = head(QK, 0, t), head(QK, 8, t)
                        ins = mm(b[:, 0:T], k[:, 0:P], q, True, False, loose=True)
                        release(ins)
                        mm(b[:, T : T + P], k[:, P:T], q[:, P:T], False, False, loose=True).then_inc(S("z_ready"), 1)
                    if 1 <= t <= 8:
                        u = t - 1
                        b, lg = bank[4 + u % 2], ZL[u % 2]
                        pe.wait_ge(S("keep_ready"), 2 * u + 2)
                        mm(b[:, 0:T], C("suffix", P), lg[:, 0:T], False, False, loose=True)
                        mm(b[:, P:T], C("after", P), lg[:, T : T + P], False, True, loose=True)
                        fill_end(mm(b[:, T : T + P], C("suffix", P), lg[:, T : T + P], False, True, loose=True), ("z", 0, u))
                    if t >= 2:
                        u = t - 2
                        pair = ("o", 0, u // 2)
                        b = fill_begin(pe, pair) if u % 2 == 0 else bank[fill_of[pair][0]]
                        pe.wait_ge(S("stick_ready"), 2 * u + 2)
                        o = b[(u % 2) * HD : (u % 2 + 1) * HD, 0:T]
                        mm(o, VT[:, 0, u * HD : (u + 1) * HD], PT[u % 2][:, 0:T], True, False)
                        ins = mm(o[:, P:T], VT[:, 1, u * HD : (u + 1) * HD], PT[u % 2][:, T : T + P], False, True)
                        if u % 2:
                            fill_end(ins, pair)

            def layer(l):
                if l == 0:
                    pe.wait_ge(S("masks_loaded"), 16)
                first = 4 * l
                for s in range(QKV_SLOTS):
                    pe.wait_ge(split_ready, SPLIT0["qkv", l] + s + 1)
                    w_hi = qhi(s).rearrange("p (k n) -> p k n", k=KC)
                    w_lo = qlo(s).rearrange("p (k n) -> p k n", k=KC)
                    for half, label in enumerate(chunks_of(l, s)):
                        b = fill_begin(pe, label)
                        cols = slice(half * P, (half + 1) * P)
                        for kk in range(KC):
                            if s == 0 and half == 0:
                                pe.wait_ge(xn_ready, KC * (1 + 3 * l) + kk + 1)
                            if s < 4:
                                head_, ins = mm3(b[:, 0:T], xh[:, kk, cols], xl[:, kk, cols], w_hi[:, kk, :], w_lo[:, kk, :],
                                                 kk == 0, kk == KC - 1)
                            else:
                                head_, ins = mm3(b[:, 0:T], w_hi[:, kk, cols], w_lo[:, kk, cols], xh[:, kk, :], xl[:, kk, :],
                                                 kk == 0, kk == KC - 1)
                            if kk == 0:
                                release(head_)
                        fill_end(ins, label)
                    owed_pairs[0] += 1
                    for i in norms_at(l, s):
                        b = fill_begin(pe, ("hssq", l, i))
                        pe.wait_ge(S("hsq_ready"), first + i + 1)
                        ins = mm(b[:, 0:512], C("heads", P), HSQ[i % 2], True, True)
                        fill_end(ins, ("hssq", l, i))
                    for i in turns_at(s):
                        m = qk_pairs[l][i][0]
                        b = fill_begin(pe, ("rot", l, i))
                        pe.wait_ge(S("hn_ready"), first + i + 1)
                        fill_end(mm(b[:, 0:512], C("turn", P), QK[:, m : m + 2, :].rearrange("p a b -> p (a b)"), True, True),
                                 ("rot", l, i))
                if l == 1:
                    b = fill_begin(pe, ("forget", 1))
                    pe.wait_ge(S("wf_loaded"), 16)
                    for kk in range(KC):
                        ins = mm(b[0:8, 0:T], WF[:, kk, :], xh[:, kk, :].bitcast(F32), kk == 0, False)
                        if kk == 0:
                            release(ins)
                        ins = mm(b[0:8, 0:T], WF[:, kk, :], xl[:, kk, :].bitcast(F32), False, kk == KC - 1)
                    fill_end(ins, ("forget", 1))
                for m in (9, 10, 11):
                    emptied(pe, ("qk", l, m))
                for j in (5, 6, 7):
                    emptied(pe, ("v", l, j))
                if l == 0:
                    stick()
                else:
                    pe.wait_ge(S("hn_ready"), 12)
                    pe.wait_ge(S("forget_ready"), 32)
                pe.wait_ge(S("rope_ready"), 4 * (l + 1))
                h0 = 8 if l == 0 else 0
                soft(l, 8 if l == 0 else 16, 4 if l == 0 else 0,
                     lambda t: head(QK, 0, h0 + t), lambda t: head(QK, 8, h0 + t),
                     lambda t, kb: VT[:, kb, (h0 + t) * HD : (h0 + t + 1) * HD], False,
                     (lambda t: t < 8) if l == 1 else None)
                out_product(l, lambda kk: emptied(pe, ("o", l, kk)), MIX)

            def second_in():
                for s in range(10):
                    k = at["in2"] + s
                    have(k)
                    width = 32 if s == 9 else 256
                    w = slot(k, KC, width)
                    for half in range(1 if s == 9 else 2):
                        m = 2 * s + half
                        b = fill_begin(pe, ("u", m))
                        for kk in range(KC):
                            if m == 0:
                                pe.wait_ge(xn_ready, KC * 6 + kk + 1)
                            if s == 9:
                                ins = mm(b[64:96, 0:T], w[:, kk, :], xn[:, kk, :], kk == 0, kk == KC - 1)
                            else:
                                ins = mm(b[:, 0:T], w[:, kk, half * P : (half + 1) * P], xn[:, kk, :], kk == 0, kk == KC - 1)
                            if kk == 0:
                                release(ins)
                        fill_end(ins, ("u", m))
                    owed[0] += 1

            def gates(first, last):
                for m in range(first, last):
                    k = at["gates"] + m // 2
                    if m % 2 == 0:
                        have(k)
                    b = fill_begin(pe, ("gate", m))
                    for kk in range(KC):
                        ins = mm(b[:, 0:T], slot(k, KC, 256)[:, kk, (m % 2) * P : (m % 2 + 1) * P], xn[:, kk, :], kk == 0, kk == KC - 1)
                        if kk == 0:
                            release(ins)
                    fill_end(ins, ("gate", m))
                    owed[0] += m % 2

            def latent():
                pe.wait_ge(S("csq_ready"), 2)
                b = fill_begin(pe, ("mssq", 0))
                release(mm(b[:, 0:T], C("ones", P), TMPM[:, 0, :], True, False))
                fill_end(mm(b[:, 0:T], C("ones", P), TMPM[:, 1, :], False, True), ("mssq", 0))
                b = fill_begin(pe, ("mssq", 1))
                fill_end(mm(b[:, 0:T], C("ones", P), TMPM[:, 2, :], True, True), ("mssq", 1))
                kq = at["mla"]
                wq, wkv = slot(kq, 2, 768), slot(kq + 1, 1, 1024)
                have(kq)
                pe.wait_ge(S("cn_ready"), 3)
                for h in range(8):
                    b = fill_begin(pe, ("mq", h))
                    for kk in range(2):
                        ins = mm(b[0:96, 0:T], wq[:, kk, h * 96 : h * 96 + 96], CQN[:, kk, :], kk == 0, kk == 1)
                    fill_end(ins, ("mq", h))
                owed[0] += 1
                have(kq + 1)
                for h in range(8):
                    b = fill_begin(pe, ("mk", h))
                    fill_end(mm(b[0:64, 0:T], wkv[:, 0, h * P : h * P + 64], CKVN, True, True), ("mk", h))
                for j in range(2):
                    b = fill_begin(pe, ("mv", j))
                    fill_end(mm(b[:, 0:512].rearrange("p (a b) -> p a b", a=8), CKVN[:, j * P : (j + 1) * P],
                                wkv[:, 0, :].rearrange("p (a b) -> p a b", a=8)[:, :, 64:128], True, True), ("mv", j))
                owed[0] += 1
                gates(0, 2)
                for j in range(5):
                    b = fill_begin(pe, ("mrot", j))
                    if j < 4:
                        emptied(pe, ("mq", 2 * j))
                        emptied(pe, ("mq", 2 * j + 1))
                        src = QM[64:96, 2 * j : 2 * j + 2, :].rearrange("p a b -> p (a b)")
                    else:
                        emptied(pe, ("u", 18))
                        src = KR[64:96, :]
                    n = 512 if j < 4 else T
                    fill_end(mm(b[64:96, 0:n], C("turn_mla", 32)[64:96, :], src, True, True), ("mrot", j))
                gates(2, 6)
                pe.wait_ge(S("mrope_ready"), 2)
                for h in (5, 6, 7):
                    emptied(pe, ("mk", h))
                for j in range(2):
                    emptied(pe, ("mv", j))
                soft(2, 8, 0, lambda t: QM[0:96, t, :], lambda t: KM[0:96, t, :],
                     lambda t, kb: VM[:, kb, t * HD : (t + 1) * HD], True)

            def recurrence():
                pe.wait_ge(S("lora_loaded"), 48)
                pe.wait_ge(S("lora_in_ready"), 2)
                pe.wait_ge(S("shifted"), 15)
                for d in range(2):
                    for hp in range(4):
                        for j, name in enumerate(("lw", "la")):
                            b = fill_begin(pe, (name, d, hp))
                            ins = mm(b[:, 0:T], LORA[j][64 * d : 64 * d + 64, hp * P : (hp + 1) * P],
                                     US[64 * d : 64 * d + 64, 12 + j, :], True, True)
                            fill_end(ins, (name, d, hp))
                for hp in range(4):
                    b = fill_begin(pe, ("lg", hp))
                    fill_end(mm(b[:, 0:T], LORA[2][:, hp * P : (hp + 1) * P], US[:, 14, :], True, True), ("lg", hp))
                gates(6, 8)
                for j in range(2):
                    b = fill_begin(pe, ("kkss", j))
                    pe.wait_ge(S("kksq_ready"), 1)
                    fill_end(mm(b[:, 0:512], C("heads", P), sq[:, 2 * j : 2 * j + 2, :].rearrange("p a b -> p (a b)"), True, True),
                             ("kkss", j))
                for j in range(4):
                    c, half = j // 2, j % 2
                    b = fill_begin(pe, ("vtm", j))
                    for i in range(2):
                        ins = pe.transpose(b[:, i * P : (i + 1) * P], US[:, 8 + 2 * half + i, c * P : (c + 1) * P], ident)
                    fill_end(ins, ("vtm", j))
                gates(8, 16)
                pe.wait_ge(S("bkt_ready"), 2)
                for j in range(8):
                    d = j // 4
                    b = fill_begin(pe, ("bkt", j))
                    pe.transpose(b[:, 0:P], BT[:, j, d, :], ident)
                    fill_end(pe.transpose(b[:, P : 2 * P], KT[:, j, d, :], ident), ("bkt", j))
                pe.wait_ge(S("bonus_in_ready"), 4)
                for j in range(2):
                    b = fill_begin(pe, ("bonus", j))
                    fill_end(mm(b[:, 0:512], C("heads", P), US[:, 4 + 2 * j : 6 + 2 * j, :].rearrange("p a b -> p (a b)"), True, True),
                             ("bonus", j))
                for j in range(4):
                    emptied(pe, ("vtm", j))
                for j in range(4, 8):
                    emptied(pe, ("bkt", j))
                pe.wait_ge(S("ar_ready"), 2)
                for w, (d, c) in enumerate(WAVES):
                    for u in range(4):
                        j = 4 * d + u
                        for e in range(2):
                            ps = slice(64 * e, 64 * e + 64)
                            b = fill_begin(pe, ("gram", w, u, e))
                            ar = AR[ps, j, c, :, :].rearrange("p a b -> p (a b)")
                            mm(b[:, 0:T], BT[ps, j, c, :], ar, True, True)
                            fill_end(mm(b[:, T : 2 * T], KT[ps, j, c, :], ar, True, True), ("gram", w, u, e))
                    for l in range(7):
                        for u in range(4):
                            b = fill_begin(pe, ("W", w, l, u))
                            pe.wait_ge(S("level_ready"), 28 * w + 4 * l + u + 1)
                            if l:
                                emptied(pe, ("TT", w, l - 1, u) if l > 1 else ("W", w, 0, u))
                            for e in range(2):
                                if l:
                                    ins = mm(b[:, e * P : (e + 1) * P], LV[u][:, e, :], TNTT[u][:, 0, e, :], True, True)
                                else:
                                    ins = pe.transpose(b[:, e * P : (e + 1) * P], LV[u][:, e, :], ident)
                            fill_end(ins, ("W", w, l, u))
                        if l:
                            for u in range(4):
                                b = fill_begin(pe, ("TT", w, l, u))
                                emptied(pe, ("W", w, l, u))
                                for e in range(2):
                                    if l < 6:
                                        mm(b[:, e * P : (e + 1) * P], TNTT[u][:, 1, e, :], WW[u][:, e, :], True, True)
                                    ins = mm(b[:, (2 + e) * P : (3 + e) * P], WW[u][:, e, :], TNTT[u][:, 1, e, :], True, True)
                                fill_end(ins, ("TT", w, l, u))
                    for u in range(4):
                        j = 4 * d + u
                        b = fill_begin(pe, ("X", w, u))
                        if w >= 2:
                            emptied(pe, ("ST", w - 2, u))
                        if w >= 2:
                            mm(b[:, 0:P], AR[:, j, c, 0, :], ST[:, j, :], True, False, loose=True)
                        for e in range(2):
                            ins = mm(b[:, e * HD : (e + 1) * HD], M4[u][:, e, 2, :],
                                     VTM[:, c, u * P + e * HD : u * P + (e + 1) * HD], w < 2, True, loose=w >= 2)
                        fill_end(ins, ("X", w, u))
                    for u in range(4):
                        b = fill_begin(pe, ("U", w, u))
                        emptied(pe, ("X", w, u))
                        emptied(pe, ("TT", w, 6, u))
                        for e in range(2):
                            ins = mm(b[:, e * HD : (e + 1) * HD], TNTT[u][:, 1, e, :], XX[u][:, e * HD : (e + 1) * HD], True, True)
                        fill_end(ins, ("U", w, u))
                    for u in range(4):
                        j = 4 * d + u
                        b = fill_begin(pe, ("O", w, u))
                        emptied(pe, ("U", w, u))
                        if w >= 2:
                            mm(b[:, 0:P], ST[:, j, :], AR[:, j, c, 1, :], True, False, loose=True)
                        for e in range(2):
                            o = b[64 * e : 64 * e + 64, 0:P]
                            mm(o, VTM[:, c, u * P + e * HD : u * P + (e + 1) * HD], M4[u][:, e, 3, :], w < 2, False, loose=w >= 2)
                            ins = mm(o, UU[u][:, e * HD : (e + 1) * HD], M4[u][:, e, 1, :], False, True, loose=w >= 2)
                        fill_end(ins, ("O", w, u))
                    if w < 2:
                        for u in range(4):
                            b = fill_begin(pe, ("ST", w, u))
                            for e in range(2):
                                ps = slice(64 * e, 64 * e + 64)
                                cols = slice(u * P + e * HD, u * P + (e + 1) * HD)
                                mm(b[ps, 0:HD], BTM[:, d, cols], UU[u][:, e * HD : (e + 1) * HD], True, False)
                                ins = mm(b[ps, 0:HD], KTM[:, d, cols], VTM[:, c, cols], False, True)
                            fill_end(ins, ("ST", w, u))
                for name in ("gmean", "gvar"):
                    for j in range(2):
                        b = fill_begin(pe, (name, j))
                        if name == "gmean":
                            for u in range(4):
                                emptied(pe, ("O", 3, u))
                        else:
                            pe.wait_ge(S("ysq_ready"), 1)
                        src = YR if name == "gmean" else sq
                        fill_end(mm(b[:, 0:512], C("heads", P), src[:, 2 * j : 2 * j + 2, :].rearrange("p a b -> p (a b)"), True, True),
                                 (name, j))

            def branches_out():
                for pair in range(4):
                    emptied(pe, ("o", 2, pair))
                for branch, src in ((1, YM), (0, YR)):
                    if branch == 0:
                        pe.wait_ge(S("y_rw_ready"), 2)
                    for m in range(8):
                        k = at["br"] + 2 * (1 - branch) + m // 4
                        b = fill_begin(pe, ("br", branch, m))
                        if m % 4 == 0:
                            have(k)
                        for kk in range(4):
                            ins = mm(b[:, 0:T], slot(k, 4, 512)[:, kk, (m % 4) * P : (m % 4 + 1) * P], src[:, kk, :], kk == 0, kk == 3)
                            if kk == 0:
                                release(ins)
                        fill_end(ins, ("br", branch, m))
                        if m % 4 == 3:
                            owed[0] += 1
                out_product(2, lambda kk: pe.wait_ge(S("merged"), kk + 1), MG)

            def experts():
                def scores(h):
                    b = fill_begin(pe, ("sc", h))
                    emptied(pe, ("pq", 2 * h))
                    emptied(pe, ("pq", 2 * h + 1))
                    for tb in range(2):
                        for c in range(2):
                            at_ = (2 * tb + c) * P
                            ins = mm(b[:, at_ : at_ + P], QP[:, 2 * h + c, tb * P : (tb + 1) * P], KEYS[:, 2 * h + c, :], True, True)
                    fill_end(ins, ("sc", h))

                pe.wait_ge(S("keys_loaded"), 16)
                for h in range(8):
                    k = at["wq"] + h
                    have(k)
                    for c in range(2):
                        b = fill_begin(pe, ("pq", 2 * h + c))
                        for kk in range(KC):
                            if h + c == 0:
                                pe.wait_ge(xn_ready, KC * 7 + kk + 1)
                            ins = mm(b[:, 0:T], slot(k, KC, 256)[:, kk, c * P : (c + 1) * P], xn[:, kk, :], kk == 0, kk == KC - 1)
                            if kk == 0:
                                release(ins)
                        fill_end(ins, ("pq", 2 * h + c))
                    owed[0] += 1
                    if h:
                        scores(h - 1)
                scores(7)
                for j in range(4):
                    b = fill_begin(pe, ("htok", j))
                    for i in range(4):
                        ins = pe.transpose(b[:, i * P : (i + 1) * P], xn[:, 4 * (j % 2) + i, (j // 2) * P : (j // 2 + 1) * P], ident)
                        if j + i == 0:
                            release(ins)
                    fill_end(ins, ("htok", j))
                k = at["pp"]
                have(k)
                pe.wait_ge(S("p_loaded"), 16)
                for m in range(8):
                    b = fill_begin(pe, ("pp", m))
                    for kk in range(2):
                        ins = mm(b[:, 0:T], slot(k, 2, 1024)[:, kk, m * P : (m + 1) * P], PIN[:, kk, :], kk == 0, kk == 1)
                    fill_end(ins, ("pp", m))
                owed[0] += 1
                for j in range(4):
                    b = fill_begin(pe, ("back", j))
                    for i in range(4):
                        tb = i % 2
                        if j == 0:
                            pe.wait_ge(S("summed"), tb + 1)
                        m = 2 * j + i // 2
                        ins = pe.transpose(b[:, i * P : (i + 1) * P], ACC[:, tb, m * P : (m + 1) * P], ident)
                        if i == 0:
                            release(ins)
                    fill_end(ins, ("back", j))

            def ple():
                for m in range(8):
                    k = at["pg"] + m // 2
                    if m % 2 == 0:
                        have(k)
                    b = fill_begin(pe, ("pg", m))
                    for kk in range(KC):
                        if m == 0:
                            pe.wait_ge(xn_ready, KC * 8 + kk + 1)
                        ins = mm(b[:, 0:T], slot(k, KC, 256)[:, kk, (m % 2) * P : (m % 2 + 1) * P], xn[:, kk, :], kk == 0, kk == KC - 1)
                    fill_end(ins, ("pg", m))

            pe.wait_ge(loaded_c, 16)
            for l in range(2):
                norm(3 * l)
                ffn(2 * l, 3 * l)
                norm(3 * l + 1)
                layer(l)
                norm(3 * l + 2)
                ffn(2 * l + 1, 3 * l + 2)
            norm(6)
            second_in()
            latent()
            recurrence()
            branches_out()
            norm(7)
            experts()
            norm(8)
            ple()
            norm(9)

        @block.scalar
        def _(act):
            chain = Chain(act_done)
            act.dma_start(xT[:, :, :], rows(A["xT"])).then_inc(loaded_x, 16)
            act.dma_start(con[:, 0:NFIRST], A["con"][:, 0:NFIRST]).then_inc(loaded_c, 16)
            act.dma_start(vec[:, :], A["vec"]).then_inc(loaded_v, 16)
            act.wait_ge(loaded_x, 16)
            act.wait_ge(loaded_c, 16)
            act.wait_ge(loaded_v, 16)

            def high(f, kind, g, i=0):
                k = at["ffn", f] + place(kind, g)
                act.wait_ge(slot_loaded[k % RING], 16 * (k // RING + 1) + 16 * i)
                order = 3 * (g - (1 if kind == "down" else 2)) + {"gate": 1, "up": 2, "down": 3}[kind]
                if order > 0 or f == 2:
                    act.wait_ge(pair_used, SPLIT0["ffn", f] + order + 6 * i)
                act.activation(whi(kind, g), ring[:, k % RING, :], ACT.Copy).then_inc(hi_ready, 1)

            def high_qkv(l, s):
                k, base = at["qkv", l] + s, SPLIT0["qkv", l]
                act.wait_ge(slot_loaded[k % RING], 16 * (k // RING + 1))
                if s:
                    act.wait_ge(pair_used, base + s - (2 if s > 2 else 3))
                act.activation(qhi(s), ring[:, k % RING, :], ACT.Copy).then_inc(hi_ready, 1)

            def norm(n):
                f = {0: 0, 2: 1, 3: 2, 5: 3}.get(n)
                if n in (1, 4):
                    high_qkv(n // 3, 0)
                if f is not None and f > 0:
                    if n in (2, 5):
                        take(act, ("y", n // 3, 0))
                    high(f, "gate", 0)
                    high(f, "up", 0)
                act.preload_act_table(ACT.Sqrt)
                for m in range(4):
                    residual_done(act, n, [m])
                    act.activation(sq[:, 2 * m : 2 * m + 2, :], xT[:, 2 * m : 2 * m + 2, :], ACT.Square).then_inc(sq_ready, 1)
                if n == 0:
                    high(0, "gate", 0)
                src = take(act, ("ssq", n))
                give(act.activation(std[:, :], src[:, 0:T], ACT.Sqrt, bias=eps(0), scale=1.0 / D), ("ssq", n))
                if n <= 5:
                    for k in range(KC):
                        act.wait_ge(S("xraw_ready"), KC * n + k + 1)
                        act.activation(xh[:, k, :], sq[:, k, :], ACT.Copy).then_inc(xh_ready, 1)

            def ffn(f):
                base = CHUNKS * f
                if f == 0:
                    high(f, "up", 0)
                high(f, "gate", 1)
                high(f, "up", 1)
                if f == 0:
                    act.dma_start(con[:, NFIRST:NCON], A["con"][:, NFIRST:NCON]).then_inc(S("masks_loaded"), 16)
                    act.dma_start(WF, rows(A["w_in_cd"][0])[:, :, 3 * D : 3 * D + 8]).then_inc(S("wf_loaded"), 16)
                    act.dma_start(small[0:8, 40:41], A["b_f"].rearrange("a n -> n a")).then_inc(S("bf_loaded"), 16)
                act.preload_act_table(ACT.Silu)

                def chunk(c, i=0):
                    act.wait_ge(gu_ready, base + c + 1 + 4 * i)
                    act.activation(sgate[:, c % 2, :], bank[4 + c % 2][:, 0:T], ACT.Silu).then_inc(silu_ready, 1)
                    act.wait_ge(hraw_ready, base + c + 1 + 4 * i)
                    act.activation(HH[:, c % 2, :], hT[:, c % 2, :], ACT.Copy).then_inc(hh_ready, 1)
                    for kind, g in splits_after(c):
                        high(f, kind, g, i)

                for c in range(3):
                    chunk(c)
                with act.Fori(0, (GROUPS - 3) // 2) as i:
                    for c in range(3, 7):
                        chunk(c, i)
                for c in range(CHUNKS - 3, CHUNKS):
                    chunk(c)

            def soft(l, n, both):
                base = unit_base[l]
                sm, pr, ptb = (None, PR2, PT2) if both else (SM, PR, PT)
                for t in range(n + 2):
                    if t < n:
                        act.wait_ge(S("max_ready"), base + t + 1)
                        src = take(act, ("s", l, t)) if both else sm[t % 2]
                        for qb, (a, w) in enumerate(((0, T), (T, T)) if both else ((0, P), (P, T))):
                            c = 2 * (t % 3) + qb
                            ins = act.activation(pr[t % 3][:, a : a + w], src[:, a : a + w], ACT.Exp,
                                                 bias=NM[:, c : c + 1], scale=SCALE[l], accum_out=RS[:, c : c + 1])
                            if not both:
                                ins.then_inc(S("exp_ready"), 1)
                        if both:
                            give(ins, ("s", l, t))
                    if t >= 2:
                        u = t - 2
                        b = take(act, ("pt", l, u))
                        w = 512 if both else 384
                        give(act.activation(ptb[u % 2][:, 0:w], b[:, 0:w], ACT.Copy), ("pt", l, u))

            def layer(l):
                if l == 0:
                    act.wait_ge(S("masks_loaded"), 16)
                act.preload_act_table(ACT.Sqrt)
                high_qkv(l, 1)
                high_qkv(l, 2)
                first, n = 4 * l, len(qk_pairs[l])

                def roots(i):
                    b = take(act, ("hssq", l, i))
                    if i >= 2:
                        act.wait_ge(S("hn_ready"), first + i - 1)
                    give(act.activation(HSTD[i % 2], b[:, 0:512], ACT.Sqrt, bias=eps(0), scale=1.0 / HD), ("hssq", l, i))

                for s in range(QKV_SLOTS):
                    if s >= 4:
                        for _, _, m in chunks_of(l, s):
                            b = take(act, ("qk", l, m))
                            give(act.activation(QK[:, m, :], b[:, 0:T], ACT.Copy), ("qk", l, m))
                    if s + 3 < QKV_SLOTS:
                        high_qkv(l, s + 3)
                    if 0 <= s - 4 < n:
                        for label in chunks_of(l, s):
                            emptied(act, label)
                        i = s - 4
                        m = qk_pairs[l][i][0]
                        act.activation(HSQ[i % 2], QK[:, m : m + 2, :].rearrange("p a b -> p (a b)"),
                                       ACT.Square).then_inc(S("hsq_ready"), 1)
                    if 0 <= s - 5 < n:
                        roots(s - 5)
                if n == 8:
                    roots(7)
                act.preload_act_table_set("natural_log_exp_and_others")
                if l == 1:
                    b = take(act, ("forget", 1))
                    act.wait_ge(S("bf_loaded"), 16)
                    chain.link(act, act.activation(FG[0:8, 0, :], b[0:8, 0:T], ACT.Abs, bias=small[0:8, 40:41]))
                    chain.link(act, act.activation(FG[0:8, 0, :], FG[0:8, 0, :], ACT.Exp, scale=-1.0))
                    act.activation(FG[0:8, 0, :], FG[0:8, 0, :], ACT.Ln, bias=C("one", 1)[0:8, :]).then_inc(S("fln_ready"), 1)
                else:
                    for t in range(8 + 1):
                        if t < 8:
                            act.wait_ge(S("z_ready"), t + 1)
                            zl, z = ZL[t % 2][:, 0:384], bank[4 + t % 2][:, 0:384]
                            act.activation(zl, z, ACT.Abs).then_inc(S("abs_ready"), 1)
                            act.wait_ge(S("abs_ready"), t + 1)
                            chain.link(act, act.activation(zl, zl, ACT.Exp, scale=-0.125))
                            act.activation(zl, zl, ACT.Ln, bias=C("one", 1)).then_inc(S("ln_ready"), 1)
                        if t >= 1:
                            u = t - 1
                            b = take(act, ("z", 0, u))
                            give(act.activation(PT[u % 2][:, 0:384], b[:, 0:384], ACT.Exp, scale=0.125), ("z", 0, u))
                soft(l, 8 if l == 0 else 16, False)

            def second_in():
                act.preload_act_table(ACT.Sigmoid)
                residual_done(act, 6)
                act.dma_start(LORA[0], A["rw_w2_2"][0].rearrange("d l n -> (d l) n")).then_inc(S("lora_loaded"), 16)
                act.dma_start(LORA[1], A["rw_a2_2"][0].rearrange("d l n -> (d l) n")).then_inc(S("lora_loaded"), 16)
                act.dma_start(LORA[2], A["rw_g2_2"][0]).then_inc(S("lora_loaded"), 16)
                for m in range(19):
                    b = take(act, ("u", m))[:, 0:T]
                    if m < 15:
                        dst = U0[:, m, 1 : T + 1]
                    elif m < 17:
                        dst = CQ[:, m - 15, :]
                    elif m == 17:
                        dst = CKV
                    else:
                        dst, b = KR[64:96, :], b[64:96, :]
                    give(act.activation(dst, b, ACT.Copy), ("u", m))

            def gates(first, last):
                for m in range(first, last):
                    b = take(act, ("gate", m))
                    give(act.activation(GATES[:, m, :], b[:, 0:T], ACT.Copy), ("gate", m))

            def latent():
                for m in (15, 16, 17):
                    emptied(act, ("u", m))
                act.activation(TMPM[:, 0:2, :], CQ, ACT.Square).then_inc(S("csq_ready"), 1)
                act.activation(TMPM[:, 2, :], CKV, ACT.Square).then_inc(S("csq_ready"), 1)
                for j, width in ((0, 256), (1, 128)):
                    b = take(act, ("mssq", j))
                    give(act.activation(TMPM[:, 3 + j, :], b[:, 0:T], ACT.Sqrt, bias=eps(0), scale=1.0 / width), ("mssq", j))
                act.wait_ge(S("angle_ready"), 2)
                act.activation(SINM[64:96, :], ANG[64:96, :], ACT.Sin).then_inc(S("trig_ready"), 1)
                act.activation(COSM[64:96, :], ANG2[64:96, :], ACT.Sin).then_inc(S("trig_ready"), 1)
                for h in range(8):
                    b = take(act, ("mq", h))
                    give(act.activation(QM[0:96, h, :], b[0:96, 0:T], ACT.Copy), ("mq", h))
                for h in range(8):
                    b = take(act, ("mk", h))
                    give(act.activation(KM[0:64, h, :], b[0:64, 0:T], ACT.Copy), ("mk", h))
                act.preload_act_table(ACT.Exp)
                gates(0, 6)
                soft(2, 8, True)

            def recurrence():
                act.preload_act_table(ACT.Sigmoid)
                act.wait_ge(S("shifted"), 15)
                act.activation(US[:, 12, :], US[:, 12, :], ACT.Tanh).then_inc(S("lora_in_ready"), 1)
                act.activation(US[:, 14, :], US[:, 14, :], ACT.Sigmoid).then_inc(S("lora_in_ready"), 1)
                for d in range(2):
                    for hp in range(4):
                        j = 4 * d + hp
                        b = take(act, ("lw", d, hp))
                        give(act.activation(CF[:, j, :, :].rearrange("p a b -> p (a b)"), b[:, 0:T], ACT.Sigmoid,
                                            bias=V("rw_w0_2", j)), ("lw", d, hp))
                        b = take(act, ("la", d, hp))
                        give(act.activation(RATE[:, j, :], b[:, 0:T], ACT.Sigmoid, bias=V("rw_a0_2", j)), ("la", d, hp))
                for hp in range(4):
                    b = take(act, ("lg", hp))
                    give(act.activation(G2[hp // 2][:, hp % 2, :], b[:, 0:T], ACT.Copy), ("lg", hp))
                gates(6, 8)
                act.wait_ge(S("kk_ready"), 4)
                act.activation(sq[:, 0:4, :], KK, ACT.Square).then_inc(S("kksq_ready"), 1)
                for j in range(2):
                    emptied(act, ("kkss", j))
                act.activation(sq[:, 4:8, :], sq[:, 4:8, :], ACT.Sqrt).then_inc(S("kkstd_ready"), 1)
                act.preload_act_table(ACT.Exp)
                act.wait_ge(S("decay_ready"), 1)
                for d, (q, q_in, s) in enumerate(((CF, CE, 1.0), (CE, CF, -1.0))):
                    js = slice(4 * d, 4 * d + 4)
                    act.activation(BT[:, js, :, :], q[:, js, :, :], ACT.Exp, scale=-s).then_inc(S("expd_ready"), 1)
                    act.activation(AR[:, js, :, 0, :], q_in[:, js, :, :], ACT.Exp, scale=s).then_inc(S("expd_ready"), 1)
                    act.activation(AR[:, js, :, 1, :], q[:, js, :, :], ACT.Exp, scale=s).then_inc(S("expd_ready"), 1)
                act.activation(SSC, SSC, ACT.Exp).then_inc(S("carry_ready"), 1)
                gates(8, 16)
                for m in (14, 15):
                    emptied(act, ("gate", m))
                act.activation(GATES, GATES, ACT.Sigmoid).then_inc(S("gates_ready"), 1)
                for w in range(4):
                    for l in range(1, 7):
                        for u in range(4):
                            b = take(act, ("W", w, l, u))
                            give(act.activation(WW[u].rearrange("p a b -> p (a b)"), b[:, 0:T], ACT.Copy), ("W", w, l, u))
                    for u in range(4):
                        b = take(act, ("X", w, u))
                        give(act.activation(XX[u], b[:, 0:P], ACT.Copy), ("X", w, u))
                    for u in range(4):
                        b = take(act, ("U", w, u))
                        give(act.activation(UU[u], b[:, 0:P], ACT.Copy), ("U", w, u))
                for j in range(2):
                    emptied(act, ("gmean", j))
                act.activation(sq[:, 0:4, :], YR, ACT.Square).then_inc(S("ysq_ready"), 1)
                for j in range(2):
                    b = take(act, ("gvar", j))
                    give(act.activation(sq[:, 4 + 2 * j : 6 + 2 * j, :].rearrange("p a b -> p (a b)"), b[:, 0:512], ACT.Sqrt,
                                        bias=eps(1), scale=1.0 / HD), ("gvar", j))
                for m in range(8):
                    b = take(act, ("br", 1, m))
                    give(act.activation(MT[:, m, :], b[:, 0:T], ACT.Copy), ("br", 1, m))
                act.dma_start(PIN, rows(A["pT"])).then_inc(S("p_loaded"), 16)
                act.dma_start(KEYS, A["sub_keys_t"].rearrange("h d k -> d h k")).then_inc(S("keys_loaded"), 16)

            def experts():
                for h in range(8 + 1):
                    if h < 8:
                        for m in (2 * h, 2 * h + 1):
                            b = take(act, ("pq", m))
                            give(act.activation(QP[:, m, :], b[:, 0:T], ACT.Copy), ("pq", m))
                    if h:
                        b = take(act, ("sc", h - 1))
                        sc = b[:, 0:512].rearrange("p (t c k) -> p t c k", t=2, c=2)
                        act.activation(SC[0][:, 2 * h - 2 : 2 * h, :], sc[:, 0, :, :], ACT.Copy)
                        give(act.activation(SC[1][:, 2 * h - 2 : 2 * h, :], sc[:, 1, :, :], ACT.Copy), ("sc", h - 1))
                for j in range(4):
                    b = take(act, ("htok", j))
                    give(act.activation(HTOK[:, j // 2, (j % 2) * 512 : (j % 2 + 1) * 512], b[:, 0:512], ACT.Copy), ("htok", j))
                for m in range(8):
                    b = take(act, ("pp", m))
                    give(act.activation(PLE[:, m, :], b[:, 0:T], ACT.Copy), ("pp", m))
                for tb in range(2):
                    act.preload_act_table(ACT.Exp)
                    act.wait_ge(S("gate_in_ready"), tb + 1)
                    act.activation(PEX, PEX, ACT.Exp).then_inc(S("gate_exp_ready"), 1)
                    act.preload_act_table(ACT.Gelu)
                    act.wait_ge(S("dots_ready"), 16 * (tb + 1))
                    act.activation(WT[:, tb, :], DOTS[:, tb, :], ACT.Gelu).then_inc(S("gelu_ready"), 1)

            def ple():
                act.preload_act_table(ACT.Sigmoid)
                for m in range(8):
                    b = take(act, ("pg", m))
                    give(act.activation(view(4096 + T * m, T), b[:, 0:T], ACT.Sigmoid), ("pg", m))

            for l in range(2):
                norm(3 * l)
                ffn(2 * l)
                norm(3 * l + 1)
                layer(l)
                norm(3 * l + 2)
                ffn(2 * l + 1)
            norm(6)
            second_in()
            latent()
            recurrence()
            norm(7)
            experts()
            norm(8)
            ple()
            norm(9)

        @block.vector
        def _(dve):
            chain = Chain(dve_done)
            link = lambda ins: chain.link(dve, ins)
            dve.wait_ge(loaded_x, 16)
            dve.wait_ge(loaded_c, 16)
            dve.wait_ge(loaded_v, 16)

            def low(f, kind, g, i=0):
                k = at["ffn", f] + place(kind, g)
                dve.wait_ge(hi_ready, SPLIT0["ffn", f] + place(kind, g) + 1 + 6 * i)
                dve.tensor_tensor(wlo(kind, g), ring[:, k % RING, :], whi(kind, g), ALU.subtract).then_inc(split_ready, 1)

            def low_qkv(l, s):
                k = at["qkv", l] + s
                dve.wait_ge(hi_ready, SPLIT0["qkv", l] + s + 1)
                dve.tensor_tensor(qlo(s), ring[:, k % RING, :], qhi(s), ALU.subtract).then_inc(split_ready, 1)

            def norm(n):
                name, c0 = norm_g[n]
                f = {0: 0, 2: 1, 3: 2, 5: 3}.get(n)
                if n in (1, 4):
                    low_qkv(n // 3, 0)
                if f is not None:
                    low(f, "gate", 0)
                emptied(dve, ("ssq", n))
                link(dve.reciprocal(rstd[:, :], std[:, :]))
                split = n <= 5
                raw = sq if split else xn
                for k in range(KC + (2 if split else 0)):
                    if k < KC:
                        dve.scalar_tensor_tensor(out=raw[:, k, :], in0=xT[:, k, :], scalar=V(name, c0 + k), in1=rstd[:, :],
                                                 op0=ALU.mult, op1=ALU.mult).then_inc(S("xraw_ready") if split else xn_ready, 1)
                    if split and k >= 2:
                        dve.wait_ge(xh_ready, KC * n + k - 1)
                        dve.tensor_tensor(xl[:, k - 2, :], sq[:, k - 2, :], xh[:, k - 2, :], ALU.subtract).then_inc(xn_ready, 1)
                if f is not None:
                    low(f, "up", 0)

            def ffn(f):
                base = CHUNKS * f
                low(f, "gate", 1)
                low(f, "up", 1)

                def chunk(c, i=0):
                    dve.wait_ge(silu_ready, base + c + 1 + 4 * i)
                    if base + c >= 2:
                        dve.wait_ge(h_ready, base + c - 1 + 4 * i)
                    dve.tensor_tensor(hT[:, c % 2, :], sgate[:, c % 2, :], bank[4 + c % 2][:, T : 2 * T],
                                      ALU.mult).then_inc(hraw_ready, 1)
                    dve.wait_ge(hh_ready, base + c + 1 + 4 * i)
                    dve.tensor_tensor(HL[:, c % 2, :], hT[:, c % 2, :], HH[:, c % 2, :], ALU.subtract).then_inc(h_ready, 1)
                    for kind, g in splits_after(c):
                        low(f, kind, g, i)

                for c in range(3):
                    chunk(c)
                with dve.Fori(0, (GROUPS - 3) // 2) as i:
                    for c in range(3, 7):
                        chunk(c, i)
                for c in range(CHUNKS - 3, CHUNKS):
                    chunk(c)
                for m in range(4):
                    dve.wait_ge(y_ready, 4 * f + m + 1)
                    xs = xT[:, 2 * m : 2 * m + 2, :].rearrange("p a b -> p (a b)")
                    dve.scalar_tensor_tensor(out=xs, in0=bank[m][:, :], scalar=0.5, in1=xs, op0=ALU.mult,
                                             op1=ALU.add).then_inc(x_ready, 1)

            def residual(label):
                for m in range(4):
                    b = take(dve, (*label, m))
                    xs = xT[:, 2 * m : 2 * m + 2, :].rearrange("p a b -> p (a b)")
                    give(dve.tensor_tensor(xs, xs, b[:, :], ALU.add), (*label, m))

            def mix_out(l, pair, dst):
                b = take(dve, ("o", l, pair))
                give(dve.tensor_copy(dst[:, pair, :], b[:, 0:T]), ("o", l, pair))

            def soft(l, n, pair0, both, mask_of, dst):
                base = unit_base[l]
                sm, pr = (None, PR2) if both else (SM, PR)
                for t in range(n + 5):
                    if t < n:
                        b = take(dve, ("s", l, t))
                        mx = MX[:, 2 * (t % 3) : 2 * (t % 3) + 2]
                        if both:
                            link(dve.tensor_reduce(mx, b[:, 0:512].rearrange("p (a b) -> p a b", a=2), AX.X, ALU.max))
                        else:
                            mask = mask_of(t)
                            dve.tensor_tensor_reduce(sm[t % 2][:, 0:P], b[:, 0:P], mask[:, 0:P], 1.0, -3.0e38,
                                                     ALU.add, ALU.max, mx[:, 0:1])
                            give(dve.tensor_tensor_reduce(sm[t % 2][:, P : 3 * P], b[:, P : 3 * P], mask[:, P : 3 * P], 1.0,
                                                          -3.0e38, ALU.add, ALU.max, mx[:, 1:2]), ("s", l, t))
                            emptied(dve, ("s", l, t))
                        dve.tensor_scalar(NM[:, 2 * (t % 3) : 2 * (t % 3) + 2], mx, -SCALE[l], None, ALU.mult)\
                           .then_inc(S("max_ready"), 1)
                    if 1 <= t <= n:
                        u = t - 1
                        if both:
                            emptied(dve, ("s", l, u))
                        else:
                            dve.wait_ge(S("exp_ready"), 2 * (base + u + 1))
                        c = 2 * (u % 3)
                        link(dve.reciprocal(RI[:, c : c + 2], RS[:, c : c + 2]))
                        for qb, (a, w) in enumerate(((0, T), (T, T)) if both else ((0, P), (P, T))):
                            v = pr[u % 3][:, a : a + w]
                            ins = dve.tensor_scalar(v, v, RI[:, c + qb : c + qb + 1], None, ALU.mult)
                        ins.then_inc(S("weights_ready"), 1)
                    if t >= 4 and t % 2:
                        mix_out(l, pair0 + (t - 4) // 2, dst)

            def layer(l):
                if l == 0:
                    dve.wait_ge(S("masks_loaded"), 16)
                low_qkv(l, 1)
                low_qkv(l, 2)

                def normalise(i):
                    m, g, rope = qk_pairs[l][i]
                    emptied(dve, ("hssq", l, i))
                    link(dve.reciprocal(HSTD[i % 2], HSTD[i % 2]))
                    qk = QK[:, m : m + 2, :].rearrange("p a b -> p (a b)")
                    dve.scalar_tensor_tensor(out=qk, in0=qk, scalar=V(g), in1=HSTD[i % 2], op0=ALU.mult,
                                             op1=ALU.mult).then_inc(S("hn_ready"), 1)

                def turn(i):
                    m = qk_pairs[l][i][0]
                    b = take(dve, ("rot", l, i))
                    qk = QK[:, m : m + 2, :]
                    table = lambda name: C(name, T).unsqueeze(1).broadcast_to([P, 2, T])
                    rot = ROT.rearrange("p (a b) -> p a b", a=2)
                    if 4 * l + i:
                        dve.wait_ge(S("rope_ready"), 4 * l + i)
                    give(dve.tensor_tensor(rot, b[:, 0:512].rearrange("p (a b) -> p a b", a=2), table("sin"), ALU.mult),
                         ("rot", l, i))
                    link(dve.tensor_tensor(qk, qk, table("cos"), ALU.mult))
                    emptied(dve, ("rot", l, i))
                    dve.tensor_tensor(qk, qk, rot, ALU.add).then_inc(S("rope_ready"), 1)

                for s in range(QKV_SLOTS):
                    if s < 4:
                        for _, _, j in chunks_of(l, s):
                            b = take(dve, ("v", l, j))
                            give(dve.tensor_copy(VT[:, j % 2, (j // 2) * 256 : (j // 2 + 1) * 256], b[:, 0:T]), ("v", l, j))
                    if s + 3 < QKV_SLOTS:
                        low_qkv(l, s + 3)
                    for i in norms_at(l, s):
                        normalise(i)
                    for i in turns_at(s):
                        turn(i)
                if l == 1:
                    b = take(dve, ("forget", 1))
                    dve.wait_ge(S("bf_loaded"), 16)
                    dve.wait_ge(S("fln_ready"), 1)
                    give(dve.tensor_scalar(FG[0:8, 1, :], b[0:8, 0:T], small[0:8, 40:41], 0.0, ALU.add, ALU.min), ("forget", 1))
                    emptied(dve, ("forget", 1))
                    link(dve.tensor_tensor(FG[0:8, 2, :], FG[0:8, 1, :], FG[0:8, 0, :], ALU.subtract))
                    link(dve.memset(FG[0:8, 1, :], 1.0))
                    link(dve.tensor_tensor_scan(FG[0:8, 3, :], FG[0:8, 1, :], FG[0:8, 2, :], 0.0, ALU.mult, ALU.add))
                    dve.tensor_scalar(FG[0:8, 0, :], FG[0:8, 3, :], 8.0, None, ALU.mult).then_inc(S("sums_ready"), 1)
                    dve.tensor_scalar(FG[0:8, 1, :], FG[0:8, 3, :], -8.0, None, ALU.mult).then_inc(S("sums_ready"), 1)
                if l == 0:
                    for t in range(8 + 4):
                        if t < 8:
                            dve.wait_ge(S("abs_ready"), t + 1)
                            z, r, zl = bank[4 + t % 2][:, 0:384], ZR[t % 2][:, 0:384], ZL[t % 2][:, 0:384]
                            link(dve.tensor_scalar(r, z, 0.0, 0.125, ALU.max, ALU.mult))
                            dve.wait_ge(S("ln_ready"), t + 1)
                            dve.tensor_tensor(zl, zl, r, ALU.add).then_inc(S("softplus_ready"), 1)
                        if t >= 3 and (t - 3) % 2:
                            mix_out(0, (t - 3) // 2, MIX)
                causal = lambda t: C("causal", 384)
                soft(l, 8 if l == 0 else 16, 4 if l == 0 else 0, False,
                     causal if l == 0 else lambda t: C("causal" if t < 8 else "dilated", 384), MIX)
                residual(("y", l))

            def second_in():
                residual_done(dve, 6)
                link(dve.memset(U0[:, :, 0:1], 0.0))
                link(dve.memset(U0[:, :, T + 1 : T + 2], 0.0))
                for g in range(3):
                    ms = slice(5 * g, 5 * g + 5)
                    for m in range(5 * g + 1, 5 * g + 5):
                        emptied(dve, ("u", m))
                    link(dve.tensor_tensor(US[:, ms, :], U0[:, ms, 0:T], U0[:, ms, 2 : T + 2], ALU.add))
                    link(dve.scalar_tensor_tensor(out=US[:, ms, :], in0=US[:, ms, :], scalar=0.5, in1=U0[:, ms, 1 : T + 1],
                                                  op0=ALU.mult, op1=ALU.subtract))
                    for m in range(5 * g, 5 * g + 5):
                        dve.scalar_tensor_tensor(out=US[:, m, :], in0=US[:, m, :], scalar=V("rw_mu_2", m),
                                                 in1=U0[:, m, 1 : T + 1], op0=ALU.mult, op1=ALU.add).then_inc(S("shifted"), 1)

            def latent():
                r = slice(64, 96)
                dve.wait_ge(S("pos_loaded"), 16)
                link(dve.tensor_copy(POSF[r, :], POS[r, :]))
                link(dve.tensor_scalar(POSF[r, :], POSF[r, :], C("inv", 1)[r, :], None, ALU.mult))
                whole, hi, lo = 12582912.0, 6.28125, 0.0019353071795864769
                for dst, quarter in ((ANG, 0.0), (ANG2, 0.25)):
                    link(dve.tensor_scalar(dst[r, :], POSF[r, :], 1.0 / (2 * np.pi), quarter, ALU.mult, ALU.add))
                    link(dve.tensor_scalar(dst[r, :], dst[r, :], whole, None, ALU.add))
                    link(dve.tensor_scalar(dst[r, :], dst[r, :], -whole, None, ALU.add))
                    link(dve.scalar_tensor_tensor(out=COSM[r, :], in0=dst[r, :], scalar=-hi, in1=POSF[r, :],
                                                  op0=ALU.mult, op1=ALU.add))
                    link(dve.scalar_tensor_tensor(out=dst[r, :], in0=dst[r, :], scalar=-lo, in1=COSM[r, :],
                                                  op0=ALU.mult, op1=ALU.add))
                    link(dve.tensor_scalar(dst[r, :], dst[r, :], quarter * 2 * np.pi, 3.1415925, ALU.add, ALU.min))
                    dve.tensor_scalar(dst[r, :], dst[r, :], -3.1415925, None, ALU.max).then_inc(S("angle_ready"), 1)
                for j in range(2):
                    emptied(dve, ("mssq", j))
                link(dve.reciprocal(TMPM[:, 3:5, :], TMPM[:, 3:5, :]))
                for dst, src, g, j in ((CQN[:, 0, :], CQ[:, 0, :], V("mla_g_qa_2", 0), 3), (CQN[:, 1, :], CQ[:, 1, :], V("mla_g_qa_2", 1), 3),
                                       (CKVN, CKV, V("mla_g_kva_2"), 4)):
                    dve.scalar_tensor_tensor(out=dst, in0=src, scalar=g, in1=TMPM[:, j, :], op0=ALU.mult,
                                             op1=ALU.mult).then_inc(S("cn_ready"), 1)
                for j in range(2):
                    b = take(dve, ("mv", j))
                    give(dve.tensor_copy(VM[:, j, :], b[:, 0:512]), ("mv", j))
                dve.wait_ge(S("trig_ready"), 2)
                dve.wait_ge(S("cn_ready"), 3)
                sin2 = SINM[r, :].unsqueeze(1).broadcast_to([32, 2, T])
                for j in range(4):
                    b = take(dve, ("mrot", j))
                    give(dve.tensor_tensor(TMPM[r, 2 * j : 2 * j + 2, :], b[r, 0:512].rearrange("p (a b) -> p a b", a=2), sin2, ALU.mult),
                         ("mrot", j))
                link(dve.tensor_tensor(QM[r, :, :], QM[r, :, :], COSM[r, :].unsqueeze(1).broadcast_to([32, 8, T]), ALU.mult))
                for j in range(2, 4):
                    emptied(dve, ("mrot", j))
                dve.tensor_tensor(QM[r, :, :], QM[r, :, :], TMPM[r, :, :], ALU.add).then_inc(S("mrope_ready"), 1)
                b = take(dve, ("mrot", 4))
                give(dve.tensor_tensor(POSF[r, :], b[r, 0:T], SINM[r, :], ALU.mult), ("mrot", 4))
                emptied(dve, ("u", 18))
                link(dve.tensor_tensor(KR[r, :], KR[r, :], COSM[r, :], ALU.mult))
                emptied(dve, ("mrot", 4))
                dve.tensor_tensor(KM[r, :, :], KR[r, :].unsqueeze(1).broadcast_to([32, 8, T]),
                                  POSF[r, :].unsqueeze(1).broadcast_to([32, 8, T]), ALU.add).then_inc(S("mrope_ready"), 1)
                soft(2, 8, 0, True, None, YM)

            def recurrence():
                flat = lambda v: v.rearrange("p a b -> p (a b)")
                for hp in range(4):
                    emptied(dve, ("lw", 1, hp))
                    emptied(dve, ("lw", 0, hp))
                link(dve.tensor_scalar(CE, CF, -DECAY, None, ALU.mult))
                for j in range(8):
                    for c in range(2):
                        ins = dve.tensor_tensor_scan(CF[:, j, c, :], C("ones", P), CE[:, j, c, :], 0.0, ALU.mult, ALU.add)
                link(ins)
                link(dve.tensor_tensor(CE, CF, CE, ALU.subtract))
                dve.tensor_copy(REF[:, 0:4, :], CF[:, 0:4, :, 63])
                link(dve.tensor_copy(REF[:, 4:8, :], CE[:, 4:8, :, 64]))
                for buf in (CF, CE):
                    ins = dve.tensor_tensor(buf, buf, REF.unsqueeze(3).broadcast_to([P, 8, 2, P]), ALU.subtract)
                link(ins)
                dve.tensor_tensor(SSC, CF[:, :, 0, P - 1], REF[:, :, 1], ALU.add).then_inc(S("decay_ready"), 1)
                for hp in range(4):
                    dve.tensor_scalar(KK[:, hp, :], US[:, 4 + hp, :], V("rw_k_k_2", hp), None, ALU.mult).then_inc(S("kk_ready"), 1)
                for j in range(2):
                    b = take(dve, ("kkss", j))
                    give(dve.tensor_scalar(flat(sq[:, 4 + 2 * j : 6 + 2 * j, :]), b[:, 0:512], 1e-24, None, ALU.max), ("kkss", j))
                dve.wait_ge(S("kkstd_ready"), 1)
                link(dve.reciprocal(sq[:, 4:8, :], sq[:, 4:8, :]))
                link(dve.tensor_tensor(KK, KK, sq[:, 4:8, :], ALU.mult))
                for hp in range(4):
                    emptied(dve, ("la", 0, hp))
                    emptied(dve, ("la", 1, hp))
                dve.wait_ge(S("kd_ready"), 8)
                dve.wait_ge(S("expd_ready"), 6)
                link(dve.tensor_tensor(KT.rearrange("p j c t -> p j (c t)"), BT.rearrange("p j c t -> p j (c t)"), KD, ALU.mult))
                for d in range(2):
                    js = slice(4 * d, 4 * d + 4)
                    kk4 = KK.rearrange("p h (c t) -> p h c t", c=2)
                    r4 = US[:, 0:4, :].rearrange("p h (c t) -> p h c t", c=2)
                    ins = dve.tensor_tensor(RATE[:, js, :], RATE[:, js, :], KK, ALU.mult)
                    dve.tensor_tensor(AR[:, js, :, 0, :], AR[:, js, :, 0, :], kk4, ALU.mult)
                    dve.tensor_tensor(AR[:, js, :, 1, :], AR[:, js, :, 1, :], r4, ALU.mult).then_inc(S("ar_ready"), 1)
                dve.wait_ge(S("ar_ready"), 2)
                bt = BT.rearrange("p j c t -> p (j c t)")
                dve.scalar_tensor_tensor(out=bt, in0=bt, scalar=-1.0, in1=RATE.rearrange("p j t -> p (j t)"),
                                         op0=ALU.mult, op1=ALU.mult).then_inc(S("bkt_ready"), 2)
                for j in range(4):
                    b = take(dve, ("vtm", j))
                    give(dve.tensor_copy(VTM[:, j // 2, (j % 2) * T : (j % 2 + 1) * T], b[:, 0:T]), ("vtm", j))
                for j in range(8):
                    d, hp = j // 4, j % 4
                    b = take(dve, ("bkt", j))
                    dve.tensor_copy(BTM[:, d, hp * P : (hp + 1) * P], b[:, 0:P])
                    give(dve.tensor_copy(KTM[:, d, hp * P : (hp + 1) * P], b[:, P : 2 * P]), ("bkt", j))
                for j in range(2):
                    b = take(dve, ("bonus", j))
                    give(dve.tensor_tensor(flat(US[:, 2 * j : 2 * j + 2, :]), b[:, 0:512], flat(US[:, 8 + 2 * j : 10 + 2 * j, :]),
                                           ALU.mult), ("bonus", j))
                for j in range(2):
                    emptied(dve, ("bonus", j))
                link(dve.memset(ST, 0.0))
                dve.wait_ge(S("carry_ready"), 1)
                eye = ident.unsqueeze(1).broadcast_to([P, 2, P])
                for w, (d, c) in enumerate(WAVES):
                    seen = C("seen", 2 * P, 2 * P * d).rearrange("p (a b) -> p a b", a=2).unsqueeze(1).broadcast_to([P, 2, 2, P])
                    for u in range(4):
                        for e in range(2):
                            b = take(dve, ("gram", w, u, e))
                            give(dve.tensor_tensor(M4[u][:, e, :, :].rearrange("p (k a) t -> p k a t", k=2),
                                                   b[:, 0:512].rearrange("p (k a t) -> p k a t", k=2, a=2), seen, ALU.mult),
                                 ("gram", w, u, e))
                    for l in range(7):
                        for u in range(4):
                            if l == 0:
                                dve.wait_ge(S("level_ready"), 28 * w + u + 1)
                                dve.tensor_tensor(TNTT[u][:, 1, :, :], LV[u], eye, ALU.add)
                                b = take(dve, ("W", w, 0, u))
                                give(dve.tensor_tensor(TNTT[u][:, 0, :, :], b[:, 0:T].rearrange("p (a b) -> p a b", a=2), eye, ALU.add),
                                     ("W", w, 0, u))
                            else:
                                b = take(dve, ("TT", w, l, u))
                                half = TNTT[u].rearrange("p a e t -> p (a e t)")
                                lo = 0 if l < 6 else 2 * P
                                emptied(dve, ("TT", w, l - 1, u) if l > 1 else ("W", w, 0, u))
                                give(dve.tensor_tensor(half[:, lo:512], half[:, lo:512], b[:, lo:512], ALU.add), ("TT", w, l, u))
                    for u in range(4):
                        b = take(dve, ("O", w, u))
                        y = YR[:, u, c * P : (c + 1) * P]
                        if w < 2:
                            ins = dve.tensor_copy(y, b[:, 0:P])
                        else:
                            ins = dve.tensor_tensor(y, y, b[:, 0:P], ALU.add)
                        give(ins, ("O", w, u))
                    if w < 2:
                        for u in range(4):
                            j = 4 * d + u
                            b = take(dve, ("ST", w, u))
                            for e in range(2):
                                ps = slice(64 * e, 64 * e + 64)
                                ins = dve.tensor_scalar(ST[ps, j, ps], b[ps, 0:HD], SSC[ps, j : j + 1], None, ALU.mult)
                            give(ins, ("ST", w, u))
                for j in range(2):
                    b = take(dve, ("gmean", j))
                    ys = flat(YR[:, 2 * j : 2 * j + 2, :])
                    for u in range(4):
                        emptied(dve, ("O", 3, u))
                    give(dve.scalar_tensor_tensor(out=ys, in0=b[:, 0:512], scalar=-1.0 / HD, in1=ys, op0=ALU.mult, op1=ALU.add),
                         ("gmean", j))
                for j in range(2):
                    emptied(dve, ("gvar", j))
                link(dve.reciprocal(sq[:, 4:8, :], sq[:, 4:8, :]))
                link(dve.tensor_tensor(YR, YR, sq[:, 4:8, :], ALU.mult))
                for hp in range(4):
                    ins = dve.tensor_scalar(YR[:, hp, :], YR[:, hp, :], V("rw_gn_w_2", hp), V("rw_gn_b_2", hp), ALU.mult, ALU.add)
                link(ins)
                link(dve.tensor_tensor(YR, YR, US[:, 0:4, :], ALU.add))
                for hp in range(4):
                    emptied(dve, ("lg", hp))
                dve.tensor_tensor(YR[:, 0:2, :], YR[:, 0:2, :], G2[0][:, :, :], ALU.mult).then_inc(S("y_rw_ready"), 1)
                dve.tensor_tensor(YR[:, 2:4, :], YR[:, 2:4, :], G2[1][:, :, :], ALU.mult).then_inc(S("y_rw_ready"), 1)

            def branches_out():
                dve.wait_ge(S("gates_ready"), 1)
                for m in range(4, 8):
                    emptied(dve, ("br", 1, m))
                link(dve.tensor_tensor(MT, MT, GATES[:, 8:16, :], ALU.mult))
                for m in range(8):
                    b = take(dve, ("br", 0, m))
                    give(dve.tensor_tensor(MG[:, m, :], GATES[:, m, :], b[:, 0:T], ALU.mult), ("br", 0, m))
                    emptied(dve, ("br", 0, m))
                    dve.tensor_tensor(MG[:, m, :], MG[:, m, :], MT[:, m, :], ALU.add).then_inc(S("merged"), 1)
                residual(("y", 2))

            def top16(scores, scratch, vals, idx):
                n = len(scores)
                for r in range(2):
                    src = scratch if r else scores
                    lo = slice(8 * r, 8 * r + 8)
                    for j in range(n):
                        ins = dve.max(vals[j][:, lo], src[j])
                    link(ins)
                    for j in range(n):
                        ins = dve.max_index(idx[j][:, lo], vals[j][:, lo], src[j])
                        if r == 0:
                            ins = dve.match_replace(scratch[j], vals[j][:, lo], src[j], -3.0e38)
                    link(ins)

            def best_keys(tb, heads):
                lists = [2 * h + c for h in heads for c in range(2)]
                top16([SC[tb][:, m, :] for m in lists], [SCR[:, j, :] for j in range(len(lists))],
                      [TV[:, tb, m, :] for m in lists], [TI[:, tb, m, :] for m in lists])

            def best_sums(tb, heads):
                n, hs = len(heads), slice(heads[0], heads[-1] + 1)
                tv = TV[:, tb, :, :].rearrange("p (h c) k -> p h c k", c=2)
                link(dve.tensor_tensor(CAND[:, 0:n, :].rearrange("p h (a b) -> p h a b", a=16),
                                       tv[:, hs, 0, :].unsqueeze(3).broadcast_to([P, n, 16, 16]),
                                       tv[:, hs, 1, :].unsqueeze(2).broadcast_to([P, n, 16, 16]), ALU.add))
                top16([CAND[:, j, :] for j in range(n)], [CSCR[:, j, :] for j in range(n)],
                      [BV[:, h, :] for h in heads], [BP[:, h, :] for h in heads])
                dve.tensor_copy(TIF[:, tb, 2 * heads[0] : 2 * heads[-1] + 2, :], TI[:, tb, 2 * heads[0] : 2 * heads[-1] + 2, :])
                es = slice(16 * heads[0], 16 * heads[-1] + 16)
                bp = BP[:, hs, :].rearrange("p h e -> p (h e)")
                for half, (op, m) in enumerate(((ALU.logical_shift_right, 4), (ALU.bitwise_and, 15))):
                    ins = dve.tensor_scalar(BI[:, half, es], bp, m, None, op)
                link(ins)
                link(dve.tensor_copy(BF[:, :, es], BI[:, :, es]))
                ti = TIF[:, tb, :, :].rearrange("p (h c) k -> p h c k", c=2)
                count = C("count", 16).unsqueeze(1).broadcast_to([P, 16 * n, 16])
                for half in range(2):
                    eq = EQ[:, half, 0 : 16 * n, :]
                    ins = dve.tensor_tensor(eq, BF[:, half, es].unsqueeze(2).broadcast_to([P, 16 * n, 16]), count, ALU.is_equal)
                link(ins)
                for half in range(2):
                    eq4 = EQ[:, half, 0 : 16 * n, :].rearrange("p (h e) i -> p h e i", h=n)
                    ins = dve.tensor_tensor(eq4, eq4, ti[:, hs, half, :].unsqueeze(2).broadcast_to([P, n, 16, 16]), ALU.mult)
                link(ins)
                for half in range(2):
                    ins = dve.tensor_reduce((E0, E1)[half][:, es], EQ[:, half, 0 : 16 * n, :], AX.X, ALU.add)
                link(ins)

            def rows_of(tb):
                link(dve.scalar_tensor_tensor(out=E0, in0=E0, scalar=float(N_KEYS), in1=E1, op0=ALU.mult, op1=ALU.add))
                dve.tensor_scalar(EIDX[:, tb, :], E0, float(N_KEYS * N_KEYS - 1), None, ALU.min).then_inc(S("rows_known"), 1)
                dve.tensor_tensor(PEX, BV, BV[:, :, 0:1].broadcast_to([P, 8, 16]), ALU.subtract).then_inc(S("gate_in_ready"), 1)

            def gates(tb):
                dve.wait_ge(S("gate_exp_ready"), tb + 1)
                link(dve.tensor_reduce(SUM8[:, 0:8], PEX, AX.X, ALU.add))
                link(dve.reciprocal(SUM8[:, 8:16], SUM8[:, 0:8]))
                link(dve.tensor_tensor(GATE[:, tb, :].rearrange("p (h e) -> p h e", h=8), PEX,
                                       SUM8[:, 8:16].unsqueeze(2).broadcast_to([P, 8, 16]), ALU.mult))

            def experts():
                for h in range(8):
                    emptied(dve, ("sc", h))
                    best_keys(0, [h])
                    best_sums(0, [h])
                rows_of(0)
                gates(0)
                for j in range(4):
                    emptied(dve, ("htok", j))
                used = S("rows_used")

                def dots(tb, first, n):
                    q = 2 * tb
                    with dve.Fori(0, n) as i:
                        for j in range(8):
                            dve.wait_ge(S(f"row{j}_loaded"), 16 * (16 * q + first + 1) + 16 * i)
                            if j >= 2:
                                dve.wait_ge(used, 8 * (16 * q + first) + j - 1 + 8 * i)
                            dve.tensor_tensor_reduce(JUNK[j % 2], GR[:, j, :], HTOK[:, tb, :], 1.0, 0.0, ALU.mult, ALU.add,
                                                     DSTAGE[:, j : j + 1]).then_inc(used, 1)
                        dve.wait_ge(used, 8 * (16 * q + first + 1) + 8 * i)
                        dve.tensor_copy(DOTS[:, tb, bass.ds(i * 8 + 8 * first, 8)], DSTAGE).then_inc(S("dots_ready"), 1)
                        dve.wait_ge(S("dots_ready"), 16 * tb + first + 1 + i)

                def weights(tb):
                    dve.wait_ge(S("gelu_ready"), tb + 1)
                    link(dve.tensor_tensor(WT[:, tb, :], WT[:, tb, :], GATE[:, tb, :], ALU.mult))

                def sums(tb, first, n):
                    q = 2 * tb + 1
                    with dve.Fori(0, n) as i:
                        dve.wait_ge(used, 8 * (16 * q + first) + 8 * i)
                        dve.tensor_copy(WSTAGE, WT[:, tb, bass.ds(i * 8 + 8 * first, 8)]).then_inc(S("wstage"), 1)
                        dve.wait_ge(S("wstage"), 16 * tb + first + 1 + i)
                        for j in range(8):
                            dve.wait_ge(S(f"row{j}_loaded"), 16 * (16 * q + first + 1) + 16 * i)
                            if j >= 2:
                                dve.wait_ge(used, 8 * (16 * q + first) + j - 1 + 8 * i)
                            acc = ACC2 if j % 2 else ACC[:, tb, :]
                            dve.scalar_tensor_tensor(out=acc, in0=GR[:, j, :], scalar=WSTAGE[:, j : j + 1],
                                                     in1=acc, op0=ALU.mult, op1=ALU.add).then_inc(used, 1)

                def join(tb):
                    dve.wait_ge(used, 8 * 16 * (2 * tb + 2))
                    dve.tensor_tensor(ACC[:, tb, :], ACC[:, tb, :], ACC2, ALU.add).then_inc(S("summed"), 1)

                link(dve.memset(ACC, 0.0))
                link(dve.memset(ACC2, 0.0))
                for step, block_rows in ((0, dots), (1, sums)):
                    if step:
                        weights(0)
                    done = 0
                    for h in range(4 * step, 4 * step + 4):
                        for find, n in ((best_keys, 2 if done == 0 else 1), (best_sums, 2)):
                            block_rows(0, done, n)
                            find(1, [h])
                            done += n
                    if step:
                        rows_of(1)
                    block_rows(0, done, 16 - done)
                join(0)
                dve.wait_ge(S("summed"), 1)
                link(dve.memset(ACC2, 0.0))
                gates(1)
                dots(1, 0, 16)
                weights(1)
                sums(1, 0, 16)
                join(1)
                residual(("back",))

            def ple():
                for m in range(8):
                    emptied(dve, ("pg", m))
                    emptied(dve, ("pp", 4 + m % 4))
                    s = view(4096 + T * m, T)
                    link(dve.tensor_tensor(s, s, PLE[:, m, :], ALU.mult))
                    ins = dve.tensor_tensor(xT[:, m, :], xT[:, m, :], s, ALU.add)
                    if m % 2:
                        ins.then_inc(x_ready, 1)

            for l in range(2):
                norm(3 * l)
                ffn(2 * l)
                norm(3 * l + 1)
                layer(l)
                norm(3 * l + 2)
                ffn(2 * l + 1)
            norm(6)
            second_in()
            latent()
            recurrence()
            branches_out()
            norm(7)
            experts()
            norm(8)
            ple()
            norm(9)

        @block.gpsimd
        def _(pool):
            chain = Chain(pool_done)
            link = lambda ins: chain.link(pool, ins)

            def keep_before(buf, sem_):
                for a in (0, T):
                    v = buf[:, a : a + P]
                    pool.affine_select(out=v, in_=v, pattern=[[1, P]], compare_op=ALU.is_gt, fill=0.0, base=0,
                                       channel_multiplier=-1).then_inc(sem_, 1)

            for t in range(8 + 1):
                if t < 8:
                    pool.wait_ge(S("softplus_ready"), t + 1)
                    keep_before(ZL[t % 2], S("keep_ready"))
                if t >= 1:
                    emptied(pool, ("z", 0, t - 1))
                    keep_before(PT[(t - 1) % 2], S("stick_ready"))
            residual_done(pool, 4)
            link(pool.memset(FL[0:2, :, :], 1.0))
            link(pool.memset(FR[0:2, :, :], 1.0))
            pool.wait_ge(S("sums_ready"), 2)
            pool.dma_start(FL[0:1, :, :], FG[0:8, 0, :]).then_inc(S("forget_ready"), 16)
            pool.dma_start(FR[1:2, :, :], FG[0:8, 1, :]).then_inc(S("forget_ready"), 16)
            residual_done(pool, 6)
            pool.wait_ge(S("masks_loaded"), 16)
            pool.dma_start(POS[64:96, :], A["positions"].partition_broadcast(32)).then_inc(S("pos_loaded"), 16)
            pool.wait_ge(S("shifted"), 15)
            for j in range(8):
                emptied(pool, ("la", j // 4, j % 4))
                link(pool.tensor_scalar(KD[:, j, :], RATE[:, j, :], 1.0, V("rw_k_a_2", j % 4), ALU.subtract, ALU.mult))
                link(pool.tensor_scalar(KD[:, j, :], KD[:, j, :], 1.0, None, ALU.add))
                pool.tensor_tensor(KD[:, j, :], KD[:, j, :], US[:, 4 + j % 4, :], ALU.mult).then_inc(S("kd_ready"), 1)
            pool.wait_ge(S("kd_ready"), 8)
            pool.wait_ge(S("kk_ready"), 4)
            link(pool.tensor_tensor(US[:, 4:8, :], KD[:, 0:4, :], KD[:, 4:8, :], ALU.add))
            for hp in range(4):
                link(pool.tensor_scalar(US[:, 4 + hp, :], US[:, 4 + hp, :], V("rw_r_k_2", hp), None, ALU.mult))
                pool.tensor_tensor(US[:, 4 + hp, :], US[:, hp, :], US[:, 4 + hp, :], ALU.mult).then_inc(S("bonus_in_ready"), 1)
            for w, (d, c) in enumerate(WAVES):
                for l in range(7):
                    for u in range(4):
                        if l == 0:
                            emptied(pool, ("gram", w, u, 0))
                            emptied(pool, ("gram", w, u, 1))
                        else:
                            b, n = fill_of["W", w, l - 1, u]
                            pool.wait_ge(full[b], n)
                            if l == 1:
                                emptied(pool, ("W", w, 0, u))
                        mask = C("level", P, (7 * d + l) * P).unsqueeze(1).broadcast_to([P, 2, P])
                        pool.tensor_tensor(LV[u], M4[u][:, :, 0, :], mask, ALU.mult).then_inc(S("level_ready"), 1)
            used = S("rows_used")
            for h in range(8):
                emptied(pool, ("sc", h))
            def gather(q, table, i, half, fresh):
                tb = q // 2
                stage = STAGE[:, 8 * half : 8 * half + 8]
                if not fresh:
                    row_free = pool.snap(free_rows)
                pool.tensor_copy(stage, EIDX[:, tb, bass.ds(i * 16 + 8 * half, 8)]).then_inc(S("staged"), 1)
                pool.wait_ge(S("staged"), 16 * q + half + 1 + 2 * i)
                for j in range(8):
                    if not fresh:
                        if j:
                            row_free = pool.snap(free_rows)
                        pool.wait_ge(used, row_free)
                        pool.reg_add(free_rows, free_rows, 1)
                    pool.indirect_dma_start(out=GR[:, j, :], out_offset=None, in_=A[table][0],
                                            in_offset=bass.IndirectOffsetOnAxis(ap=stage[:, j : j + 1], axis=0))\
                        .then_inc(S(f"row{j}_loaded"), 16)

            pool.wait_ge(S("rows_known"), 1)
            free_rows = pool.alloc_register("free_rows")
            pool.reg_mov(free_rows, 1)
            gather(0, "peer_u_2", 0, 0, True)
            gather(0, "peer_u_2", 0, 1, False)
            with pool.Fori(1, 8) as i:
                for half in range(2):
                    gather(0, "peer_u_2", i, half, False)
            for q, table in ((1, "peer_v_2"), (2, "peer_u_2"), (3, "peer_v_2")):
                if q == 2:
                    pool.wait_ge(S("rows_known"), 2)
                with pool.Fori(0, 8) as i:
                    for half in range(2):
                        gather(q, table, i, half, False)


def kernel(**inputs):
    import concourse.bacc as bacc
    from concourse.bass_utils import run_bass_kernel_spmd

    arrays = {}
    take = lambda name: np.ascontiguousarray(np.asarray(inputs[name]))
    arrays["xT"] = np.ascontiguousarray(take("x")[0].T)
    arrays["pT"] = np.ascontiguousarray(take("p_2")[0, 0].T)
    arrays["positions"] = take("positions_2")[0]
    keys = take("peer_sub_keys_2")[0].reshape(16, N_KEYS, P)
    arrays["sub_keys_t"] = np.ascontiguousarray(keys.transpose(0, 2, 1))
    arrays["con"] = constants()
    arrays["vec"] = pack_vectors(inputs)
    for name in ("ffn1_w_gate", "ffn1_w_up", "ffn1_w_down", "ffn2_w_gate", "ffn2_w_up", "ffn2_w_down", "w_in_ab",
                 "w_in_cd", "b_f", "w_out", "w_in_2", "rw_w2_2", "rw_a2_2", "rw_g2_2", "mla_w_qup_2", "mla_w_kvup_2",
                 "w_br_rwkv_2", "w_br_mla_2", "w_out_2", "peer_w_q_2", "peer_u_2", "peer_v_2", "w_ple_gate_2",
                 "w_ple_proj_2"):
        arrays[name] = take(name)

    nc = bacc.Bacc("TRN2", target_bir_lowering=False, num_devices=1)
    aps = {
        name: nc.dram_tensor(name, a.shape, mybir.dt.from_np(a.dtype), kind="ExternalInput").ap()
        for name, a in arrays.items()
    }
    out = nc.dram_tensor("out", (D, T), F32, kind="ExternalOutput").ap()
    build(nc, aps, out)
    r = run_bass_kernel_spmd(nc, [arrays], core_ids=[0])
    return np.ascontiguousarray(r.results[0]["out"].T)[None]
```
